# Optimizing a Trainium2 kernel written in Bass

```python
import jax, jax.numpy as jnp
from jax import lax
import numpy as np

D_MODEL = 2048
BATCH = 1
SEQ = 256
DEPTH = 1

MLA_HEADS = D_MODEL // 128
Q_LORA = 512
KV_LORA = 512
NOPE_DIM = 128
ROPE_DIM = 64
V_DIM = 128
ROPE_THETA = 10000.0
Q_BLOCK = 128
MASK_VALUE = -1e30
HGRN_HEADS = D_MODEL // 128
HGRN_DK = 128
HGRN_DV = 128
HGRN_K = HGRN_HEADS * HGRN_DK
HGRN_V = HGRN_HEADS * HGRN_DV
CHUNK = 64
MIN_FORGET = 1e-30
D_FF = ((8 * D_MODEL // 3 + 255) // 256) * 256
CONV_WIDTH = 3
EPS = 1e-6
IN_SPLITS = (Q_LORA, KV_LORA, ROPE_DIM, HGRN_K, HGRN_K, HGRN_V, HGRN_V, D_MODEL, D_MODEL)
IN_WIDTH = sum(IN_SPLITS)

kernel_name = "hybrid_mla_hgrn2_convffn_trunk"

def rmsnorm(x, g):
    xf = x.astype(jnp.float32)
    y = xf * lax.rsqrt(jnp.mean(xf * xf, axis=-1, keepdims=True) + EPS)
    return (y * g.astype(jnp.float32)).astype(x.dtype)

def rope_tables(positions):
    inv_freq = ROPE_THETA ** (-jnp.arange(0, ROPE_DIM, 2, dtype=jnp.float32) / ROPE_DIM)
    ang = positions.astype(jnp.float32)[..., None] * inv_freq
    return jnp.cos(ang)[:, :, None, :], jnp.sin(ang)[:, :, None, :]

def apply_rope(x, cos, sin):
    xf = x.astype(jnp.float32)
    x1, x2 = jnp.split(xf, 2, axis=-1)
    return jnp.concatenate([x1 * cos - x2 * sin, x2 * cos + x1 * sin], axis=-1).astype(x.dtype)

def causal_block_attention(q, k, v):
    B, S, H, Dqk = q.shape
    nb = S // Q_BLOCK
    scale = Dqk ** -0.5
    qb = q.reshape(B, nb, Q_BLOCK, H, Dqk).transpose(1, 0, 2, 3, 4)
    key_pos = jnp.arange(S)

    def one_block(args):
        q_blk, blk = args
        s = jnp.einsum('bqhd,bkhd->bhqk', q_blk, k).astype(jnp.float32) * scale
        q_pos = blk * Q_BLOCK + jnp.arange(Q_BLOCK)
        s = jnp.where(key_pos[None, :] <= q_pos[:, None], s, MASK_VALUE)
        p = jax.nn.softmax(s, axis=-1).astype(v.dtype)
        return jnp.einsum('bhqk,bkhd->bqhd', p, v)

    out = lax.map(one_block, (qb, jnp.arange(nb)))
    return out.transpose(1, 0, 2, 3, 4).reshape(B, S, H, v.shape[-1])

def hgrn2_chunkwise(q, k, log_f, v):
    B, S, H, DK = q.shape
    DV = v.shape[-1]
    nc = S // CHUNK

    def to_chunks(t):
        return t.astype(jnp.float32).reshape(B, nc, CHUNK, H, t.shape[-1]).transpose(1, 0, 3, 2, 4)

    qc, kc, gc, vc = to_chunks(q), to_chunks(k), to_chunks(log_f), to_chunks(v)
    causal = jnp.tril(jnp.ones((CHUNK, CHUNK), dtype=bool))[:, :, None]

    def step(state, inp):
        q_, k_, g_, v_ = inp
        b = jnp.cumsum(g_, axis=-2)
        diff = b[..., :, None, :] - b[..., None, :, :]
        decay = jnp.where(causal, jnp.exp(jnp.where(causal, diff, 0.0)), 0.0)
        scores = jnp.einsum('bhtd,bhsd,bhtsd->bhts', q_, k_, decay)
        o_intra = jnp.einsum('bhts,bhsv->bhtv', scores, v_)
        o_inter = jnp.einsum('bhtd,bhdv->bhtv', q_ * jnp.exp(b), state)
        b_last = b[..., -1:, :]
        k_dec = k_ * jnp.exp(b_last - b)
        new_state = state * jnp.exp(b_last[..., 0, :])[..., None] + jnp.einsum('bhsd,bhsv->bhdv', k_dec, v_)
        return new_state, o_intra + o_inter

    state0 = jnp.zeros((B, H, DK, DV), jnp.float32)
    _, out = lax.scan(step, state0, (qc, kc, gc, vc))
    return out.transpose(1, 0, 3, 2, 4).reshape(B, S, H, DV)

def causal_dwconv(u, w, b):
    S = u.shape[1]
    up = jnp.pad(u, ((0, 0), (CONV_WIDTH - 1, 0), (0, 0)))
    y = b
    for j in range(CONV_WIDTH):
        y = y + w[j] * up[:, j:j + S, :]
    return y

def setup_inputs(seed: int = 0) -> dict:
    key = jax.random.key(seed)
    ks = jax.random.split(key, 24)
    f32 = jnp.float32

    def nrm(k, shape, scale):
        return jax.random.normal(k, shape, f32) * scale

    def gain(k, shape):
        return 1.0 + 0.02 * jax.random.normal(k, shape, f32)

    res_scale = (2.0 * DEPTH) ** -0.5
    x = jax.random.normal(ks[0], (BATCH, SEQ, D_MODEL), f32)
    offsets = jax.random.randint(ks[1], (BATCH, 1), 0, 4096, dtype=jnp.int32)
    positions = offsets + jnp.arange(SEQ, dtype=jnp.int32)[None, :]
    return {
        "x": x,
        "positions": positions,
        "attn_norm_g": gain(ks[2], (DEPTH, D_MODEL)),
        "w_in": nrm(ks[3], (DEPTH, D_MODEL, IN_WIDTH), D_MODEL ** -0.5),
        "q_norm_g": gain(ks[4], (DEPTH, Q_LORA)),
        "w_uq": nrm(ks[5], (DEPTH, Q_LORA, MLA_HEADS * (NOPE_DIM + ROPE_DIM)), Q_LORA ** -0.5),
        "kv_norm_g": gain(ks[6], (DEPTH, KV_LORA)),
        "w_ukv": nrm(ks[7], (DEPTH, KV_LORA, MLA_HEADS * (NOPE_DIM + V_DIM)), KV_LORA ** -0.5),
        "hgrn_lb_logits": nrm(ks[8], (DEPTH, HGRN_K), 0.5),
        "hgrn_out_norm_g": gain(ks[9], (DEPTH, HGRN_DV)),
        "w_branch_a": nrm(ks[10], (DEPTH, MLA_HEADS * V_DIM, D_MODEL), (MLA_HEADS * V_DIM) ** -0.5),
        "w_branch_b": nrm(ks[11], (DEPTH, HGRN_V, D_MODEL), HGRN_V ** -0.5),
        "w_out": nrm(ks[12], (DEPTH, D_MODEL, D_MODEL), D_MODEL ** -0.5 * res_scale),
        "ffn_norm_g": gain(ks[13], (DEPTH, D_MODEL)),
        "w_up": nrm(ks[14], (DEPTH, D_MODEL, 2 * D_FF), D_MODEL ** -0.5),
        "conv_w": nrm(ks[15], (DEPTH, CONV_WIDTH, 2 * D_FF), CONV_WIDTH ** -0.5),
        "conv_b": nrm(ks[16], (DEPTH, 2 * D_FF), 0.01),
        "w_down": nrm(ks[17], (DEPTH, D_FF, D_MODEL), D_FF ** -0.5 * res_scale),
        "final_norm_g": gain(ks[18], (D_MODEL,)),
    }

def reference(x, positions, attn_norm_g, w_in, q_norm_g, w_uq, kv_norm_g, w_ukv, hgrn_lb_logits,
              hgrn_out_norm_g, w_branch_a, w_branch_b, w_out, ffn_norm_g, w_up, conv_w, conv_b,
              w_down, final_norm_g):
    B, S, _ = x.shape
    cos, sin = rope_tables(positions)
    p = jax.nn.softmax(hgrn_lb_logits.astype(jnp.float32), axis=0)
    lower_bounds = jnp.cumsum(p, axis=0) - p[0]
    split_points = [int(s) for s in np.cumsum(IN_SPLITS)[:-1]]

    for l in range(DEPTH):
        h = rmsnorm(x, attn_norm_g[l])
        proj = h @ w_in[l]
        c_q, c_kv, k_rope, hq, hf, hi, hg, gate_a, gate_b = jnp.split(proj, split_points, axis=-1)

        q = (rmsnorm(c_q, q_norm_g[l]) @ w_uq[l]).reshape(B, S, MLA_HEADS, NOPE_DIM + ROPE_DIM)
        kv = (rmsnorm(c_kv, kv_norm_g[l]) @ w_ukv[l]).reshape(B, S, MLA_HEADS, NOPE_DIM + V_DIM)
        q_nope, q_pe = q[..., :NOPE_DIM], q[..., NOPE_DIM:]
        k_nope, v = kv[..., :NOPE_DIM], kv[..., NOPE_DIM:]
        q_pe = apply_rope(q_pe, cos, sin)
        k_pe = jnp.broadcast_to(apply_rope(k_rope[:, :, None, :], cos, sin), (B, S, MLA_HEADS, ROPE_DIM))
        attn = causal_block_attention(jnp.concatenate([q_nope, q_pe], axis=-1),
                                      jnp.concatenate([k_nope, k_pe], axis=-1), v)
        attn = attn.reshape(B, S, MLA_HEADS * V_DIM)

        lb = lower_bounds[l]
        z = hf.astype(jnp.float32)
        forget = lb + (1.0 - lb) * jax.nn.sigmoid(z)
        log_f = jnp.log(jnp.maximum(forget, MIN_FORGET))
        k_in = 1.0 - forget
        rec = hgrn2_chunkwise(jax.nn.silu(hq).reshape(B, S, HGRN_HEADS, HGRN_DK),
                              k_in.reshape(B, S, HGRN_HEADS, HGRN_DK),
                              log_f.reshape(B, S, HGRN_HEADS, HGRN_DK),
                              hi.reshape(B, S, HGRN_HEADS, HGRN_DV)).astype(x.dtype)
        rec = rmsnorm(rec, hgrn_out_norm_g[l]) * jax.nn.silu(hg.reshape(B, S, HGRN_HEADS, HGRN_DV))
        rec = rec.reshape(B, S, HGRN_V)

        merged = (jax.nn.sigmoid(gate_a) * (attn @ w_branch_a[l])
                  + jax.nn.sigmoid(gate_b) * (rec @ w_branch_b[l]))
        x = x + merged @ w_out[l]

        h = rmsnorm(x, ffn_norm_g[l])
        u = causal_dwconv(h @ w_up[l], conv_w[l], conv_b[l])
        g, up = jnp.split(u, 2, axis=-1)
        x = x + (jax.nn.silu(g) * up) @ w_down[l]

    return rmsnorm(x, final_norm_g)


_drawn_inputs = setup_inputs


def setup_inputs(seed=0):
    import zlib

    import numpy as np

    out = dict(_drawn_inputs(seed))
    spreads = {}
    factors = {'attn_norm_g': 7.205,
     'q_norm_g': 8.0,
     'kv_norm_g': 8.0,
     'hgrn_out_norm_g': 8.0,
     'ffn_norm_g': 18.154,
     'conv_b': 37.34,
     'final_norm_g': 8.095}
    for name, (base, spread) in spreads.items():
        noise = np.random.default_rng([zlib.crc32(name.encode()), seed]).standard_normal(out[name].shape)
        drawn = base * np.exp(spread * noise) if base else spread * noise
        out[name] = __import__('jax').numpy.asarray(drawn.astype(out[name].dtype))
    for name, factor in factors.items():
        out[name] = (out[name] * factor).astype(out[name].dtype)
    return out
```

```python
from contextlib import ExitStack

import numpy as np

import concourse.bass as bass
from concourse import mybir

F32 = mybir.dt.float32
F32R = mybir.dt.float32r

I32 = mybir.dt.int32
ALU = mybir.AluOpType
ACT = mybir.ActivationFunctionType
AX = mybir.AxisListType

P = 128
SEQ = 256
T = SEQ // P
D = 2048
KT = D // P
HEADS = D // 128
NOPE, ROPE = 128, 64
LORA = 512
D_FF = 5632
N = 512
EPS = 1e-6
MIN_FORGET = 1e-30
SCALE = float(NOPE + ROPE) ** -0.5
MASKED = -1e30
CHUNK = 64
LEVELS = (128, 64, 32, 16, 8, 4, 2, 1, 0)
SPAN = float(2.0 ** 60)

RING = 4
CH = 2 * N
QUADS = HEADS // 4
GROUP_CHUNKS = KT // 2
FF_GROUPS = D_FF // 256
FF_KT = D_FF // P
UP_PAIRS = FF_GROUPS // 2
DOWN_CHUNKS = FF_KT // 2
N_CHUNKS = (4 * QUADS * GROUP_CHUNKS + 4 * 4 * GROUP_CHUNKS + 2 * GROUP_CHUNKS + 1 + 7 * QUADS
            + 4 * GROUP_CHUNKS + FF_GROUPS * GROUP_CHUNKS + 4 * DOWN_CHUNKS)

GROUP_GB = 4 * QUADS
GROUP_CQ = GROUP_GB + 2
GROUP_Q0 = GROUP_CQ + 3 + 6
GROUP_GA = GROUP_Q0 + 4 * QUADS

G_ATTN, G_Q, G_KV, G_FFN, LOGITS, G_HGRN, CONV = 0, 16, 20, 24, 40, 56, 184
N_PARAMS = CONV + 4 * 4 * FF_GROUPS
C_IDENT, C_CAUSAL, C_SCAN, C_FREQ = 0, 128, 512, 1536
N_CONST = C_FREQ + 32


class Count:

    def __init__(self, k, per=0, i=None, first=0):
        self.k, self.per, self.i, self.first = k, per, i, first

    def plus(self, n):
        return Count(self.k + n, self.per, self.i, self.first)

    def over(self, m):
        assert self.per % m == 0
        return Count(self.k // m, self.per // m, self.i, self.first)

    def mod(self, m):
        assert self.per % m == 0
        return self.k % m

    def times(self, m):
        return Count(self.k * m, self.per * m, self.i, self.first)

    def least(self):
        return self.k + self.per * self.first

    def value(self):
        return self.i * self.per + self.k if self.per else self.k


def wait(eng, sem, count):
    if count.least() <= 0:
        assert count.per == 0 or count.i is None, "a wait that may be void inside a loop"
        return
    eng.wait_ge(sem, count.value())


FAMILIES = {
    "trans": ("operand", "hf_turn", "hq_turn", "kpe_turn", "q_turn", "k_turn", "qp_turn", "p_turn", "conv"),
    "misc": ("level", "mix", "scores", "pv"),
}


def names_of(step):
    name, args = step[0], step[1:]
    out = [name] + [f for f, members in FAMILIES.items() if name in members]
    if name == "chunk" and args[-1]:
        out.append("group")
    return out


def chunks(src, n, after=None, columns=N, nk=2, k0=0, lag=None):
    for k in range(n):
        first, last = k == 0, k == n - 1
        yield ("chunk", src, k0 + k * nk, nk, columns, lag if lag is not None else (0 if first else None),
               first, last)
        yield from (after or {}).get(k, ())
        yield ("split",)


def hgrn_new(i):
    return {
        7: [("hf_out",)],
        10: [("hf_turn", 0), ("hf_turn", 1)],
        15: [("hq_out",)],
        19: [("hq_turn", 0), ("hq_turn", 1), ("forget", i)],
        20: [("log_forget",)],
        22: [("cumsum",)],
        23: [("hi_out",)],
        31: [("hg_out",)],
    }


def hgrn_old(i):
    table = {}
    for n in range(len(LEVELS) - 1):
        table.setdefault(2 * n, []).append(("decay", n))
        table.setdefault(2 * n + 2, []).extend([("level", n, 0), ("level", n, 1)])
    table.setdefault(17, []).extend([("level", 8, 0), ("level", 8, 1)])
    table.setdefault(18, []).extend([("mix", 0), ("mix", 1)])
    table.setdefault(20, []).append(("mix_norm",))
    table.setdefault(24, []).extend([("operand", "rec", 0, i), ("operand", "rec", 1, i)])
    return table


def merged(*tables):
    out = {}
    for table in tables:
        for k, steps in table.items():
            out.setdefault(k, []).extend(steps)
    return out


def pick(table, start, n=GROUP_CHUNKS):
    return {k - start: s for k, s in table.items() if start <= k < start + n}


def hgrn_section(i, old):
    table = merged(hgrn_old(i - 1), hgrn_new(i)) if old else hgrn_new(i)
    if not old:
        yield from [("x_norm",), ("operand", "h", 0, 0), ("operand", "h", 1, 0)]
        yield from (("split",) for _ in range(RING))
        table = merged(table, {5: [("tables",)], 6: [("bounds",)]})
    for g in range(4):
        mine = pick(table, g * GROUP_CHUNKS)
        if not old and g == 0:
            yield from streamed("h", mine)
        else:
            yield from chunks("h", GROUP_CHUNKS, mine)


def streamed(kind, table=None):
    turns = {k: [("operand", kind, k + 2, 0)] for k in range(GROUP_CHUNKS - 2)}
    for k, (step) in enumerate(chunks("h", GROUP_CHUNKS)):
        yield step
        if step[0] == "chunk":
            c = step[2] // 2
            yield from turns.get(c, ())
            yield from (table or {}).get(c, ())


def with_lag(steps):
    for s in steps:
        if s[0] == "chunk":
            c = s[2] // 2
            s = (*s[:5], min(1, GROUP_CHUNKS - 1 - c), *s[6:])
        yield s


def branch_b_first():
    table = merged(hgrn_old(QUADS - 1), {
        7: [("gate_out", 0, "b")],
        15: [("gate_out", 1, "b")],
        23: [("latent", 0)],
        26: [("operand", "cq", 0, 0), ("operand", "cq", 1, 0)],
        31: [("latent", 1)],
    })
    for g in range(2):
        yield from chunks("h", GROUP_CHUNKS, pick(table, g * GROUP_CHUNKS))
    for g in range(2, 4):
        yield from chunks("h", GROUP_CHUNKS, pick(table, g * GROUP_CHUNKS))
    yield from chunks("h", 1, {0: [("key_rope",)]}, columns=ROPE, nk=KT)
    yield from chunks("rec", GROUP_CHUNKS, {
        1: [("kpe_turn",)],
        2: [("operand", "ckv", 0, 0), ("operand", "ckv", 1, 0)],
        7: [("branch_b", 0, 0, GROUP_GB)]})
    yield from chunks("rec", GROUP_CHUNKS, {7: [("branch_b", 1, 1, GROUP_GB + 1)]})


def branch_b_second():
    for g in range(2):
        yield from chunks("h", GROUP_CHUNKS, {7: [("gate_out", g, "b")]})
    for g in range(2):
        yield from chunks("rec", GROUP_CHUNKS, {7: [("branch_b", g, 2 + g, GROUP_GB + 7 + g)]})


FIRST_HEAD = 8


def heads_at(slot):
    for back, name in ((4, "pv"), (2, "p_turn"), (1, "probs"), (0, "scores")):
        h = slot - back - FIRST_HEAD
        if h >= 0 and h % 2 == 0 and h // 2 < HEADS:
            yield (name, h // 2)


def attention_section():
    for j in range(QUADS):
        s = 7 * j
        yield from chunks("cq", 2, {0: list(heads_at(s)), 1: [*heads_at(s + 1), ("q_out", j)]})
        yield from chunks("cq", 1, {0: [*heads_at(s + 2), ("q_rope", j)]}, columns=256, nk=4)
        yield from chunks("ckv", 2, {
            0: [*heads_at(s + 3), ("q_turn", j, 0), ("q_turn", j, 1)],
            1: [*heads_at(s + 4), ("k_out", j), ("qp_turn", j)]})
        yield from chunks("ckv", 2, {
            0: [*heads_at(s + 5)],
            1: [*heads_at(s + 6), ("v_out", j), ("k_turn", j, 0), ("k_turn", j, 1)]})


def branch_a(first):
    slot = 7 * QUADS
    for g in range(2):
        table = {k: list(heads_at(slot + g * GROUP_CHUNKS + k)) if first else [] for k in range(GROUP_CHUNKS)}
        table[7].append(("gate_out", g, "a"))
        yield from chunks("h", GROUP_CHUNKS, table)
        if not first and g == 0:
            yield ("reload_x",)
    for g in range(2):
        j = g if first else 2 + g
        yield from chunks("att", GROUP_CHUNKS, {7: [("branch_a", g, j, GROUP_GA + (0 if first else 4) + g)]})


def out_section():
    yield from [("operand", "merged", 0, 0), ("operand", "merged", 1, 0)]
    yield from with_lag(streamed("merged", {7: [("x2_out", 0)]}))
    for j in range(1, 4):
        yield from chunks("h", GROUP_CHUNKS, {7: [("x2_out", j)]})
    yield ("h2_norm",)


def up_first():
    yield from [("operand", "h2", 0, 0), ("operand", "h2", 1, 0)]
    yield from with_lag(streamed("h2", {7: [("up_out",)]}))
    yield from chunks("h", GROUP_CHUNKS, {
        1: [("conv", 0, 0, 0), ("conv", 0, 0, 1)], 3: [("ff_gate", 0, 0)], 7: [("up_out",)]})


def up_section(i):
    for g in range(2):
        yield from chunks("h", GROUP_CHUNKS, {
            1: [("conv", i, g - 1, 0), ("conv", i, g - 1, 1)], 3: [("ff_gate", i, g - 1)], 7: [("up_out",)]})


def down_section():
    last = FF_GROUPS - 1
    for j in range(4):
        table = {DOWN_CHUNKS - 1: [("y_out", j)]}
        if j == 0:
            table |= {1: [("conv", 0, last, 0), ("conv", 0, last, 1)], 3: [("ff_gate", 0, last)],
                      6: [("load_final_gain",)]}
        steps = list(chunks("act", DOWN_CHUNKS, table))
        if j == 0:
            steps = [(*s[:5], 0, *s[6:]) if s[0] == "chunk" and s[2] == FF_KT - 2 else s for s in steps]
        if j == 3:
            ends = [k for k, s in enumerate(steps) if s[0] == "split"][-RING:]
            steps = [s for k, s in enumerate(steps) if k not in ends]
        yield from steps
    yield ("final",)


SECTIONS = (
    (lambda i: with_lag_first(hgrn_section(0, False)), None, None),
    (lambda i: hgrn_section(i, True), 1, QUADS),
    (lambda i: branch_b_first(), None, None),
    (lambda i: branch_b_second(), None, None),
    (lambda i: attention_section(), None, None),
    (lambda i: branch_a(True), None, None),
    (lambda i: branch_a(False), None, None),
    (lambda i: out_section(), None, None),
    (lambda i: up_first(), None, None),
    (lambda i: up_section(i), 1, UP_PAIRS),
    (lambda i: down_section(), None, None),
)


def with_lag_first(steps):
    seen = 0
    for s in steps:
        if s[0] == "chunk":
            seen += 1
            if seen <= GROUP_CHUNKS:
                s = (*s[:5], min(1, GROUP_CHUNKS - 1 - s[2] // 2), *s[6:])
        yield s


class At:

    def __init__(self):
        self.done, self.rate, self.i, self.first = {}, {}, None, 0

    def __getitem__(self, name):
        per = self.rate.get(name, 0) if self.i is not None else 0
        return Count(self.done.get(name, 0) - per * self.first, per, self.i if per else None, self.first)

    def passed(self, step):
        for name in names_of(step):
            self.done[name] = self.done.get(name, 0) + 1


def walk(eng, at, do):
    for make, first, end in SECTIONS:
        if first is None:
            for step in make(None):
                if step[0] in do:
                    do[step[0]](*step[1:])
                at.passed(step)
            continue
        rate = {}
        for step in make(0):
            for name in names_of(step):
                rate[name] = rate.get(name, 0) + 1
        if not any(step[0] in do for step in make(0)):
            for name, n in rate.items():
                at.done[name] = at.done.get(name, 0) + n * (end - first)
            continue
        before = dict(at.done)
        with eng.Fori(first, end) as i:
            at.rate, at.i, at.first = rate, i, first
            for step in make(i):
                if step[0] in do:
                    do[step[0]](*step[1:])
                at.passed(step)
        at.rate, at.i, at.first = {}, None, 0
        at.done = {n: before.get(n, 0) + rate.get(n, 0) * (end - first) for n in {*before, *rate}}


def build(nc, weights, x, params, consts, level_masks, positions, final_gain, out):
    with ExitStack() as ctx:
        def sem(name):
            return ctx.enter_context(nc.semaphore(name))

        arena_bytes = 212480
        base = -(-nc.sbuf_base // 32) * 32
        ctx.enter_context(nc.sbuf_tensor("arena", [P, arena_bytes // 4], F32))
        assert nc.sbuf_base >= base + arena_bytes

        def place(name, offset, shape, dtype=F32):
            offset = -(-offset // 32) * 32
            size = int(np.prod(shape)) * 4
            assert offset + size <= arena_bytes, (name, offset + size)
            return nc.alloc_sbuf_tensor_at(name, [P, *shape], dtype, offset=base + offset), offset + size

        o = 0
        raw, o = place("raw", o, [RING, CH])
        w_hi, o = place("w_hi", o, [RING, CH], F32R)
        w_lo, o = place("w_lo", o, [RING, CH], F32R)
        hT_hi, o = place("hT_hi", o, [KT, SEQ], F32R)
        hT_lo, o = place("hT_lo", o, [KT, SEQ], F32R)
        tokens, o = place("tokens", o, [T, D])
        piece, o = place("piece", o, [2, N])
        par, o = place("par", o, [N_PARAMS])
        ident, o = place("ident", o, [P])
        causal, o = place("causal", o, [3 * P])
        cos2, o = place("cos2", o, [T, ROPE])
        sin2, o = place("sin2", o, [T, ROPE])
        kpeT, o = place("kpeT", o, [SEQ])
        sq_sum, o = place("sq_sum", o, [T, 4])
        stat, o = place("stat", o, [T, 4])
        root, o = place("root", o, [T, 4])
        rstd, o = place("rstd", o, [T, 4])
        bound, o = place("bound", o, [2, HEADS])
        pos_f, o = place("pos_f", o, [T])
        spare, o = place("spare", o, [2 * len(LEVELS)])
        shared = o

        recT_hi, o = place("recT_hi", shared, [KT, SEQ], F32R)
        recT_lo, o = place("recT_lo", o, [KT, SEQ], F32R)
        latents = o
        kk, o = place("kk", o, [4, SEQ])
        qq, o = place("qq", o, [4, SEQ])
        bb, o = place("bb", o, [4, SEQ])
        fac, o = place("fac", o, [2, 4, SEQ])
        rest = o
        forget, o = place("forget", o, [4, SEQ])
        tok, o = place("tok", o, [T, N])
        scores_T, o = place("scores_T", o, [4, 3, P])
        junk, _ = place("junk", o, [T, D])
        hv, o = place("hv", o, [T, N])
        hgate, o = place("hgate", o, [T, N])
        rec, o = place("rec", o, [T, N])
        square, o = place("square", o, [T, N])
        scan_mask, o = place("scan_mask", o, [4, SEQ])
        lmask, o = place("lmask", o, [len(LEVELS), P], I32)
        sums01, o = place("sums01", o, [4])
        gate_b_at = o
        gate_b, o = place("gate_b", o, [2, T, N])
        means4, o = place("means4", o, [T, 4])

        cqT_hi, o = place("cqT_hi", latents, [4, SEQ], F32R)
        cqT_lo, o = place("cqT_lo", o, [4, SEQ], F32R)
        ckvT_hi, o = place("ckvT_hi", o, [4, SEQ], F32R)
        ckvT_lo, o = place("ckvT_lo", o, [4, SEQ], F32R)
        assert o <= rest
        latent, _ = place("latent", rest, [T, N])
        gate_a, _ = place("gate_a", latents, [2, T, N])
        angle, o = place("angle", gate_b_at, [4, T, 32])
        freq, o = place("freq", o, [32])
        logit, o = place("logit", o, [4, HEADS])
        pos_i, _ = place("pos_i", o, [T], I32)
        _, o = place("kpe_skip", rest, [T, N])
        kpe_tok, o = place("kpe_tok", o, [T, P])
        kpe_t1, o = place("kpe_t1", o, [T, ROPE])
        kpe_t2, o = place("kpe_t2", o, [T, ROPE])

        attT_hi, o = place("attT_hi", shared, [KT, SEQ], F32R)
        attT_lo, o = place("attT_lo", o, [KT, SEQ], F32R)
        q_tok, o = place("q_tok", latents + 16384, [T, N])
        k_tok, o = place("k_tok", o, [T, N])
        qp_tok, o = place("qp_tok", o, [T, 256])
        rope1, o = place("rope1", o, [T, 256])
        rope2, o = place("rope2", o, [T, 256])
        qT, o = place("qT", o, [2, 4, SEQ])
        kT, o = place("kT", o, [2, 4, SEQ])
        s_sb, o = place("s_sb", o, [2, 3 * P])
        probs, o = place("probs", o, [2, 3 * P])
        probsT, o = place("probsT", o, [2, 3 * P])
        neg_max, o = place("neg_max", o, [2, T])
        row_sum, o = place("row_sum", o, [2, T])
        row_inv, o = place("row_inv", o, [2, T])
        qpT, o = place("qpT", o, [2, 2, SEQ])
        vv, o = place("vv", o, [2, T, N])

        actT_hi, o = place("actT_hi", shared, [FF_KT, SEQ], F32R)
        actT_lo, o = place("actT_lo", o, [FF_KT, SEQ], F32R)
        u_tok, o = place("u_tok", o, [T, N])
        yconv, o = place("yconv", o, [2, 2, SEQ])
        silu_g, o = place("silu_g", o, [2 * SEQ])
        prod, o = place("prod", o, [2 * SEQ])
        x_again, _ = place("x_again", shared + 2 * KT * SEQ * 4 + 16384, [T, D])
        gain_row, _ = place("gain_row", 3 * RING * CH * 4, [D])

        acc = ctx.enter_context(nc.psum_tensor("acc", [P, 2, T, N], F32))
        turn = ctx.enter_context(nc.psum_tensor("turn", [P, 2, N], F32))
        misc = ctx.enter_context(nc.psum_tensor("misc", [P, 2, N], F32))

        raw_in = [sem(f"raw_in{s}") for s in range(RING)]
        hi_made, lo_made, chunk_used = sem("hi_made"), sem("lo_made"), sem("chunk_used")
        acc_read = [sem("acc_read0"), sem("acc_read1")]
        turn_full, misc_full = sem("turn_full"), sem("misc_full")
        turn_read = [sem("turn_read0"), sem("turn_read1")]
        misc_read = [sem("misc_read0"), sem("misc_read1")]
        operand_hi, operand_lo = sem("operand_hi"), sem("operand_lo")
        x_in = [sem("x_in0"), sem("x_in1")]
        par_in, const_in, scan_in, lmask_in = sem("par_in"), sem("const_in"), sem("scan_in"), sem("lmask_in")
        causal_in, freq_in, pos_in = sem("causal_in"), sem("freq_in"), sem("pos_in")
        x_again_in, gain_in, stored = sem("x_again_in"), sem("gain_in"), sem("stored")
        squares, means, roots, normed0, normed1 = (
            sem("squares"), sem("means"), sem("roots"), sem("normed0"), sem("normed1"))
        inverses = sem("inverses")
        bounds_exp, bounds_done, sines, tables = sem("bounds_exp"), sem("bounds_done"), sem("sines"), sem("tables")
        forget_bounded, logs, cumsummed = sem("forget_bounded"), sem("logs"), sem("cumsummed")
        decay_diff, decay_exp, factors = sem("decay_diff"), sem("decay_exp"), sem("factors")
        gate_scaled, mix_squared, mix_mean, mix_root, rec_made = (
            sem("gate_scaled"), sem("mix_squared"), sem("mix_mean"), sem("mix_root"), sem("rec_made"))
        lat_squared, lat_mean, lat_root, lat_inverse = (
            sem("lat_squared"), sem("lat_mean"), sem("lat_root"), sem("lat_inverse"))
        rope_key, maxima, exps, inverted, probs_made, att_hi = (
            sem("rope_key"), sem("maxima"), sem("exps"), sem("inverted"), sem("probs_made"), sem("att_hi"))
        rope_query = sem("rope_query")
        x2_made, y_made, tap0, taps, silu_made, product, act_hi, act_lo = (
            sem("x2_made"), sem("y_made"), sem("tap0"), sem("taps"), sem("silu_made"), sem("product"),
            sem("act_hi"), sem("act_lo"))
        pool_own = sem("pool_own")
        sum_own, table_own, forget_own, cumsum_own, mix_own, mix_own2 = (
            sem("sum_own"), sem("table_own"), sem("forget_own"), sem("cumsum_own"), sem("mix_own"), sem("mix_own2"))
        merged_made = sem("merged_made")
        out_ready = sem("out_ready")

        operands = {"h": (hT_hi, hT_lo), "rec": (recT_hi, recT_lo), "cq": (cqT_hi, cqT_lo),
                    "ckv": (ckvT_hi, ckvT_lo), "att": (attT_hi, attT_lo), "act": (actT_hi, actT_lo)}
        targets = {"h": "h", "merged": "h", "h2": "h", "rec": "rec", "cq": "cq", "ckv": "ckv"}
        rows_of = {"h": tokens, "merged": tokens, "h2": x_again, "rec": rec, "cq": latent, "ckv": latent}
        gains = {"h": G_ATTN, "h2": G_FFN, "cq": G_Q, "ckv": G_KV}

        def f32(ap):
            return ap.bitcast(F32)

        def banks(at):
            u = at["trans"]
            return u.mod(2), u

        def halves(ap, h):
            v = ap.rearrange("p a s -> p (a s)").rearrange("p (m two h) -> p m two h", two=2, h=h)
            return v[:, :, 0, :], v[:, :, 1, :]

        block = ctx.enter_context(nc.Block())

        @block.sync
        def _(sp):
            for t in range(T):
                sp.dma_start(tokens[:, t, :], x[t * P:(t + 1) * P, :]).then_inc(x_in[t], 16)
                if t == 0:
                    sp.dma_start(ident[:], consts[:, C_IDENT:C_IDENT + P]).then_inc(const_in, 16)
            sp.dma_start(par[:], params).then_inc(par_in, 16)

            def load(slot, n):
                sp.dma_start(raw[:, slot, :], weights[bass.ds(n, 1), :, :].rearrange("a p c -> p (a c)")
                             ).then_inc(raw_in[slot], 16)

            for s in range(RING):
                load(s, s)
            with sp.Fori(1, N_CHUNKS // RING) as r:
                for s in range(RING):
                    sp.wait_ge(lo_made, r * RING + (s + 1 - RING))
                    load(s, r * RING + s)
            for n in range(N_CHUNKS // RING * RING, N_CHUNKS):
                sp.wait_ge(lo_made, n + 1 - RING)
                load(n % RING, n)
            for h in range(2 * T):
                sp.wait_ge(out_ready, h + 1)
                t, half = h // 2, (h % 2) * (D // 2)
                sp.dma_start(out[t * P:(t + 1) * P, half:half + D // 2],
                             tokens[:, t, half:half + D // 2]).then_inc(stored, 16)
            sp.wait_ge(stored, 16 * 2 * T)

        @block.tensor
        def _(pe):
            at = At()
            p_bank = {}

            def chunk(src, k0, nk, columns, lag, first, last):
                n, g = at["chunk"], at["group"]
                slot, b = n.mod(RING), g.mod(2)
                hi, lo = operands[src]
                wh = w_hi[:, slot, 0:nk * columns].rearrange("p (k c) -> p k c", c=columns)
                wl = w_lo[:, slot, 0:nk * columns].rearrange("p (k c) -> p k c", c=columns)
                wait(pe, lo_made, n.plus(1))
                if first:
                    wait(pe, acc_read[b], g.over(2))
                    if src == "att":
                        for m in range(2):
                            wait(pe, misc_read[m], at["misc"].plus(1 - m).over(2).plus(1))
                if lag is not None:
                    if src == "act":
                        wait(pe, act_lo, at["ff_gate"])
                    else:
                        wait(pe, operand_lo, at["operand"].plus(-lag))
                for k in range(nk):
                    for t in range(T):
                        x_h = hi[:, k0 + k, t * P:(t + 1) * P]
                        x_l = lo[:, k0 + k, t * P:(t + 1) * P]
                        to = acc[:, b, t, 0:columns]
                        begin, end = first and k == 0, last and k == nk - 1
                        pe.matmul(to, x_h, wh[:, k, :], start=begin, stop=False)
                        pe.matmul(to, x_h, wl[:, k, :], start=False, stop=False)
                        ins = pe.matmul(to, x_l, wh[:, k, :], start=False, stop=end)
                ins.then_inc(chunk_used, 1)

            def turn_bank():
                b, u = banks(at)
                wait(pe, turn_read[b], u.over(2))
                return b

            def turns(b, pieces):
                for q, (src, rows) in enumerate(pieces):
                    ins = pe.transpose(turn[0:rows, b, q * P:(q + 1) * P], src, ident[:])
                ins.then_inc(turn_full, 1)

            def operand(kind, p, i):
                b = turn_bank()
                if kind == "h":
                    if p == 0:
                        pe.wait_ge(normed0, 1)
                        pe.wait_ge(normed1, 1)
                        pe.wait_ge(const_in, 16)
                elif kind == "h2" and p == 0:
                    pe.wait_ge(normed0, 2)
                    pe.wait_ge(normed1, 2)
                elif kind == "rec":
                    wait(pe, rec_made, at["mix_norm"])
                elif kind in ("cq", "ckv"):
                    g = GROUP_CQ if kind == "cq" else GROUP_CQ + 1
                    pe.wait_ge(acc_read[g % 2], g // 2 + 1)
                elif kind == "merged" and p == 0:
                    wait(pe, merged_made, at["branch_a"])
                rows = rows_of[kind]
                turns(b, [(rows[:, t, (2 * p + k) * P:(2 * p + k + 1) * P], P) for k in range(2) for t in range(T)])

            def tok_turn(src, p):
                b = turn_bank()
                turns(b, [(src[:, t, (2 * p + k) * P:(2 * p + k + 1) * P], P) for k in range(2) for t in range(T)])

            def read_before(at_group):
                g = at_group.plus(-1)
                wait(pe, acc_read[g.mod(2)], g.over(2).plus(1))

            def hf_turn(p):
                read_before(at["group"])
                tok_turn(tok, p)

            def kpe_turn():
                b = turn_bank()
                pe.wait_ge(rope_key, 1)
                turns(b, [(kpe_tok[:, t, :], P) for t in range(T)])

            def level(n, p):
                m = at["misc"]
                b, h, f = m.mod(2), LEVELS[n], fac[:, n % 2]
                wait(pe, misc_read[b], m.over(2).plus(1))
                wait(pe, factors, at["decay"])
                for a in range(2):
                    head = 2 * p + a
                    if h == 2 * CHUNK:
                        ins = pe.matmul(misc[:, b, a * P:(a + 1) * P], f[:, head, 0:P], f[:, head, P:2 * P],
                                        start=True, stop=True)
                        continue
                    for t in range(T):
                        cols, q = slice(t * P, (t + 1) * P), 2 * a + t
                        keys, queries = (f, f) if h else (kk, qq)
                        ins = pe.matmul(misc[:, b, q * P:(q + 1) * P], keys[:, head, cols], queries[:, head, cols],
                                        start=True, stop=True)
                ins.then_inc(misc_full, 1)

            def mix(t):
                m = at["misc"]
                b = m.mod(2)
                wait(pe, misc_read[b], m.over(2).plus(1))
                if t == 0:
                    wait(pe, misc_read[1 - b], m.plus(1 - (1 - b)).over(2).plus(1))
                for h in range(4):
                    to = misc[:, b, h * P:(h + 1) * P]
                    cols = slice(h * P, (h + 1) * P)
                    if t == 0:
                        ins = pe.matmul(to, scores_T[:, h, 0, :], hv[:, 0, cols], start=True, stop=True)
                    else:
                        pe.matmul(to, scores_T[:, h, 2, :], hv[:, 0, cols], start=True, stop=False)
                        ins = pe.matmul(to, scores_T[:, h, 1, :], hv[:, 1, cols], start=False, stop=True)
                ins.then_inc(misc_full, 1)

            def q_turn(j, p):
                wait(pe, acc_read[q_group(j).mod(2)], q_group(j).over(2).plus(1))
                tok_turn(q_tok, p)

            def k_turn(j, p):
                g = q_group(j).plus(2)
                wait(pe, acc_read[g.mod(2)], g.over(2).plus(1))
                tok_turn(k_tok, p)

            def q_group(j):
                return Count(GROUP_Q0 + 4 * j)

            def qp_turn(j):
                b = turn_bank()
                pe.wait_ge(rope_query, j + 1)
                turns(b, [(qp_tok[:, t, a * P:(a + 1) * P], P) for a in range(2) for t in range(T)])

            def scores(h):
                m = at["misc"]
                b, j, a = m.mod(2), h // 4, h % 4
                wait(pe, misc_read[b], m.over(2).plus(1))
                if a == 0:
                    for r in range(2):
                        wait(pe, turn_read[r], at["trans"].plus(1 - r).over(2))
                    wait(pe, acc_read[q_group(j).plus(3).mod(2)], q_group(j).plus(3).over(2).plus(1))
                half = slice((a % 2) * ROPE, (a % 2 + 1) * ROPE)
                for t in range(T):
                    to = misc[:, b, 0:P] if t == 0 else misc[:, b, P:3 * P]
                    keys = (t + 1) * P
                    pe.matmul(to, qT[:, j % 2, a, t * P:(t + 1) * P], kT[:, j % 2, a, 0:keys], start=True, stop=False)
                    ins = pe.matmul(to, qpT[half, j % 2, a // 2, t * P:(t + 1) * P], kpeT[half, 0:keys],
                                    start=False, stop=True)
                ins.then_inc(misc_full, 1)

            def p_turn(h):
                b = turn_bank()
                pe.wait_ge(probs_made, h + 1)
                p_bank[h] = at["trans"].k
                turns(b, [(probs[:, h % 2, q * P:(q + 1) * P], P) for q in range(3)])

            def pv(h):
                m = at["misc"]
                b, j, a = m.mod(2), h // 4, h % 4
                wait(pe, misc_read[b], m.over(2).plus(1))
                u = p_bank[h]
                wait(pe, turn_read[u % 2], Count(u // 2 + 1))
                cols = slice(a * P, (a + 1) * P)
                pe.matmul(misc[:, b, 0:P], vv[:, j % 2, 0, cols], probsT[:, h % 2, 0:P], start=True, stop=True)
                pe.matmul(misc[:, b, P:2 * P], vv[:, j % 2, 0, cols], probsT[:, h % 2, P:2 * P], start=True, stop=False)
                pe.matmul(misc[:, b, P:2 * P], vv[:, j % 2, 1, cols], probsT[:, h % 2, 2 * P:3 * P],
                          start=False, stop=True).then_inc(misc_full, 1)

            def conv(i, g, p):
                read_before(at["group"])
                tok_turn(u_tok, p)

            walk(pe, at, dict(chunk=chunk, operand=operand, hf_turn=hf_turn, hq_turn=hf_turn, kpe_turn=kpe_turn,
                              level=level, mix=mix, q_turn=q_turn, k_turn=k_turn, qp_turn=qp_turn,
                              scores=scores, p_turn=p_turn, pv=pv, conv=conv))

        @block.scalar
        def _(act):
            at = At()

            def from_acc(out_ap, func, extra=()):
                g = at["group"].plus(-1)
                wait(act, chunk_used, at["chunk"])
                for s, count in extra:
                    wait(act, s, count)
                act.activation(out_ap, acc[:, g.mod(2)], func).then_inc(acc_read[g.mod(2)], 1)

            def from_turn(out_ap, func, columns=N):
                b, u = banks(at)
                wait(act, turn_full, u.plus(1))
                act.activation(out_ap, turn[:, b, 0:columns], func).then_inc(turn_read[b], 1)

            def split():
                n = at["split"]
                slot = n.mod(RING)
                wait(act, raw_in[slot], n.over(RING).plus(1).times(16))
                wait(act, chunk_used, n.plus(1 - RING))
                act.activation(w_hi[:, slot, :], raw[:, slot, :], ACT.Copy).then_inc(hi_made, 1)

            def x_norm():
                for t in range(T):
                    act.wait_ge(x_in[t], 16)
                    act.activation(junk[:, t, :], tokens[:, t, :], ACT.Square,
                                   accum_out=sq_sum[:, t, 0:1]).then_inc(squares, 1)
                normalise(0, tokens, 0)

            def normalise(which, to, col):
                act.wait_ge(means, which + 1)
                act.activation(root[:, :, 0], stat[:, :, 0], ACT.Sqrt).then_inc(roots, 1)
                act.wait_ge(inverses, which + 1)
                if to is not None:
                    act.activation(to[:, 0, :], tokens[:, 0, :], ACT.Copy, scale=rstd[:, 0, 0:1]).then_inc(normed0, 1)

            def operand(kind, p, i):
                b, u = banks(at)
                s = at["operand"]
                hi = operands[targets[kind]][0]
                kt = bass.ds(i * 4 + 2 * p, 2) if kind == "rec" else slice(2 * p, 2 * p + 2)
                wait(act, turn_read[b], u.over(2).plus(1))
                act.activation(hi[:, kt, :].rearrange("p k s -> p (k s)"), piece[:, s.mod(2), :],
                               ACT.Copy).then_inc(operand_hi, 1)

            def tables_step():
                act.wait_ge(bounds_exp, 2)
                act.activation(sin2[:, :, 0:32], angle[:, 2], ACT.Sin, scale=-1.0)
                act.activation(sin2[:, :, 32:64], angle[:, 2], ACT.Sin)
                act.activation(cos2[:, :, 0:32], angle[:, 3], ACT.Sin)
                act.activation(cos2[:, :, 32:64], angle[:, 3], ACT.Sin).then_inc(sines, 1)

            def bounds():
                act.wait_ge(bounds_exp, 3)
                act.activation(logit[:, 1, :], logit[:, 0, :], ACT.Exp).then_inc(bounds_done, 1)

            def row_copy():
                from_acc(tok[:], ACT.Copy, [(turn_full, at["trans"])])

            def hf_turn(p):
                from_turn(forget[:, 2 * p:2 * p + 2, :].rearrange("p h s -> p (h s)"), ACT.Sigmoid)

            def hq_turn(p):
                from_turn(qq[:, 2 * p:2 * p + 2, :].rearrange("p h s -> p (h s)"), ACT.Silu)

            def log_forget():
                wait(act, forget_bounded, at["forget"])
                act.activation(fac[:, 0], fac[:, 0], ACT.Ln)
                act.activation(fac[:, 1], fac[:, 1], ACT.Ln, scale=SPAN).then_inc(logs, 1)

            def hi_out():
                from_acc(hv[:], ACT.Copy)

            def hg_out():
                from_acc(hgate[:], ACT.Silu, [(rec_made, at["mix_norm"])])

            def decay(n):
                wait(act, decay_diff, at["decay"].plus(1))
                act.activation(fac[:, n % 2], fac[:, n % 2], ACT.Exp).then_inc(decay_exp, 1)

            def mix(t):
                m = at["misc"]
                wait(act, misc_full, m.plus(1))
                act.activation(square[:, t, :], misc[:, m.mod(2), :], ACT.Square).then_inc(mix_squared, 1)

            def mix_norm():
                wait(act, mix_mean, at["mix_norm"].plus(1))
                act.activation(root[:], means4[:], ACT.Sqrt).then_inc(mix_root, 1)

            def gate_out(g, which):
                if which == "a":
                    from_acc(gate_a[:, g], ACT.Sigmoid, [(merged_made, at["branch_a"])])
                else:
                    from_acc(gate_b[:, g], ACT.Sigmoid)

            def latent_step(w):
                g = at["group"].k - 1
                b = g % 2
                wait(act, chunk_used, at["chunk"])
                for t in range(T):
                    act.activation(square[:, t, :], acc[:, b, t, :], ACT.Square,
                                   accum_out=sq_sum[:, t, w:w + 1]).then_inc(lat_squared, 1)
                act.wait_ge(lat_mean, w + 1)
                act.activation(root[:, :, 1], stat[:, :, 1], ACT.Sqrt).then_inc(lat_root, 1)
                act.wait_ge(lat_inverse, w + 1)
                wait(act, turn_full, at["trans"])
                act.activation(latent[:, 0, :], acc[:, b, 0, :], ACT.Copy, scale=rstd[:, 0, 1:2])
                act.activation(latent[:, 1, :], acc[:, b, 1, :], ACT.Copy,
                               scale=rstd[:, 1, 1:2]).then_inc(acc_read[b], 1)

            def kpe_turn():
                from_turn(kpeT[:], ACT.Copy, SEQ)

            def q_out(j):
                from_acc(q_tok[:], ACT.Copy)

            def k_out(j):
                from_acc(k_tok[:], ACT.Copy)

            def v_out(j):
                from_acc(vv[:, j % 2], ACT.Copy)

            def q_turn(j, p):
                from_turn(qT[:, j % 2, 2 * p:2 * p + 2, :].rearrange("p h s -> p (h s)"), ACT.Copy)

            def qp_turn(j):
                from_turn(qpT[:, j % 2].rearrange("p h s -> p (h s)"), ACT.Copy)

            def scores(h):
                r = h % 2
                act.wait_ge(maxima, h + 1)
                act.activation(probs[:, r, 0:P], s_sb[:, r, 0:P], ACT.Exp, bias=neg_max[:, r, 0:1],
                               accum_out=row_sum[:, r, 0:1])
                act.activation(probs[:, r, P:3 * P], s_sb[:, r, P:3 * P], ACT.Exp, bias=neg_max[:, r, 1:2],
                               accum_out=row_sum[:, r, 1:2]).then_inc(exps, 1)

            def p_turn(h):
                from_turn(probsT[:, h % 2, :], ACT.Copy, 3 * P)

            def pv(h):
                m = at["misc"]
                wait(act, misc_full, m.plus(1))
                act.activation(attT_hi[:, h, :], misc[:, m.mod(2), 0:SEQ], ACT.Copy).then_inc(att_hi, 1)

            def reload_x():
                wait(act, chunk_used, at["chunk"])
                wait(act, merged_made, at["branch_a"])
                act.dma_start(x_again[:], x.rearrange("(t p) d -> p t d", p=P)).then_inc(x_again_in, 16)

            def squares_of(j):
                g = at["group"].k - 1
                act.wait_ge(acc_read[g % 2], g // 2 + 1)
                for t in range(T):
                    act.activation(u_tok[:, t, :], tokens[:, t, j * N:(j + 1) * N], ACT.Square,
                                   accum_out=sq_sum[:, t, j:j + 1]).then_inc(squares, 1)

            def h2_norm():
                normalise(1, x_again, 1)

            def up_out():
                from_acc(u_tok[:], ACT.Copy, [(turn_full, at["trans"])])

            def conv(i, g, p):
                b, u = banks(at)
                wait(act, turn_full, u.plus(1))
                wait(act, product, at["ff_gate"])
                for f in range(2):
                    taps_at = conv_taps(i, g, p, f)
                    ins = act.activation(yconv[:, p, f, :], turn[:, b, f * SEQ:(f + 1) * SEQ], ACT.Identity,
                                         scale=par[:, bass.ds(taps_at + 2, 1)], bias=par[:, bass.ds(taps_at + 3, 1)])
                ins.then_inc(tap0, 1)

            def ff_gate(i, g):
                both_turns_read(act)
                act.activation(silu_g[:], yconv[:, 0].rearrange("p f s -> p (f s)"), ACT.Silu).then_inc(silu_made, 1)
                wait(act, product, at["ff_gate"].plus(1))
                act.activation(actT_hi[:, bass.ds(i * 4 + 2 * g, 2), :].rearrange("p k s -> p (k s)"), prod[:],
                               ACT.Copy).then_inc(act_hi, 1)

            def both_turns_read(eng):
                for r in range(2):
                    wait(eng, turn_read[r], at["trans"].plus(1 - r).over(2))

            def load_final_gain():
                wait(act, chunk_used, at["chunk"])
                act.dma_start(gain_row[:], final_gain).then_inc(gain_in, 16)

            def final():
                normalise(2, None, 2)

            act.dma_start(freq[:], consts[:, C_FREQ:C_FREQ + 32]).then_inc(freq_in, 16)
            act.dma_start(pos_i[:], positions).then_inc(pos_in, 16)
            act.dma_start(scan_mask[:], consts[:, C_SCAN:C_SCAN + 4 * SEQ].rearrange("p (h s) -> p h s", h=4)
                          ).then_inc(scan_in, 16)
            act.dma_start(causal[:], consts[:, C_CAUSAL:C_CAUSAL + 3 * P]).then_inc(causal_in, 16)
            act.dma_start(lmask[:], level_masks).then_inc(lmask_in, 16)
            walk(act, at, dict(split=split, x_norm=x_norm, operand=operand, tables=tables_step, bounds=bounds,
                               hf_out=row_copy, hq_out=row_copy, hf_turn=hf_turn, hq_turn=hq_turn,
                               log_forget=log_forget, hi_out=hi_out, hg_out=hg_out, decay=decay, mix=mix,
                               mix_norm=mix_norm, gate_out=gate_out, latent=latent_step, kpe_turn=kpe_turn,
                               q_out=q_out, k_out=k_out, v_out=v_out, q_turn=q_turn, qp_turn=qp_turn,
                               scores=scores, p_turn=p_turn, pv=pv, reload_x=reload_x, x2_out=squares_of,
                               h2_norm=h2_norm, up_out=up_out, conv=conv, ff_gate=ff_gate, y_out=squares_of,
                               load_final_gain=load_final_gain, final=final))

        @block.vector
        def _(dve):
            at = At()

            def acc_here():
                g = at["group"].plus(-1)
                wait(dve, chunk_used, at["chunk"])
                return g.mod(2), g

            def split():
                n = at["split"]
                slot = n.mod(RING)
                wait(dve, hi_made, n.plus(1))
                dve.tensor_tensor(w_lo[:, slot, :], raw[:, slot, :], f32(w_hi[:, slot, :]),
                                  ALU.subtract).then_inc(lo_made, 1)

            def mean(columns, width, count_sem, to=0):
                dve.tensor_scalar(stat[:, :, to], columns, 1.0 / width, EPS, ALU.mult, ALU.add).then_inc(count_sem, 1)

            def normalise(which, to):
                dve.wait_ge(roots, which + 1)
                dve.reciprocal(rstd[:, :, 0], root[:, :, 0]).then_inc(inverses, 1)
                dve.wait_ge(inverses, which + 1)
                if to is not None:
                    dve.tensor_scalar(to[:, 1, :], tokens[:, 1, :], rstd[:, 1, 0:1], None, ALU.mult).then_inc(normed1, 1)

            def x_norm():
                dve.wait_ge(squares, 2)
                mean(sq_sum[:, :, 0], D, means)
                normalise(0, tokens)

            def summed_norm(which, to):
                dve.wait_ge(squares, 2 + 2 * 4 * which)
                dve.tensor_reduce(stat[:, :, 2], sq_sum[:], AX.X, ALU.add).then_inc(sum_own, 1)
                dve.wait_ge(sum_own, which)
                mean(stat[:, :, 2], D, means)
                normalise(which, to)

            def h2_norm():
                summed_norm(1, x_again)

            def operand(kind, p, i):
                b, u = banks(at)
                s = at["operand"]
                lo = operands[targets[kind]][1]
                hi = operands[targets[kind]][0]
                kt = bass.ds(i * 4 + 2 * p, 2) if kind == "rec" else slice(2 * p, 2 * p + 2)
                wait(dve, turn_full, u.plus(1))
                if kind in gains:
                    g0 = gains[kind] + 2 * p
                    dve.wait_ge(par_in, 16)
                    dve.tensor_tensor(piece[:, s.mod(2), :].rearrange("p (k s) -> p k s", k=2),
                                      turn[:, b, :].rearrange("p (k s) -> p k s", k=2),
                                      par[:, g0:g0 + 2].unsqueeze(2).to_broadcast([P, 2, SEQ]),
                                      ALU.mult).then_inc(turn_read[b], 1)
                else:
                    dve.tensor_copy(piece[:, s.mod(2), :], turn[:, b, :]).then_inc(turn_read[b], 1)
                wait(dve, operand_hi, s.plus(1))
                dve.tensor_tensor(lo[:, kt, :].rearrange("p k s -> p (k s)"), piece[:, s.mod(2), :],
                                  f32(hi[:, kt, :].rearrange("p k s -> p (k s)")), ALU.subtract).then_inc(operand_lo, 1)

            def tables_step():
                count = [0]

                def own(ins):
                    count[0] += 1
                    ins.then_inc(table_own, 1)
                    dve.wait_ge(table_own, count[0])

                two_pi = 2.0 * np.pi
                c1 = 6.28125
                c2 = float(np.float32(np.round((two_pi - c1) * 2.0 ** 20) / 2.0 ** 20))
                c3 = float(two_pi - c1 - c2)
                rounder = 1.5 * 2.0 ** 23
                top = 3.1415925
                dve.wait_ge(pos_in, 16)
                dve.wait_ge(freq_in, 16)
                own(dve.tensor_copy(pos_f[:], pos_i[:]))
                for t in range(T):
                    ins = dve.tensor_scalar(angle[:, 0, t, :], freq[:], pos_f[:, t:t + 1], None, ALU.mult)
                own(ins)
                own(dve.tensor_scalar(angle[:, 1], angle[:, 0], 1.0 / two_pi, rounder, ALU.mult, ALU.add))
                own(dve.tensor_scalar(angle[:, 1], angle[:, 1], -rounder, None, ALU.add))
                for c in (c1, c2, c3):
                    own(dve.scalar_tensor_tensor(out=angle[:, 0], in0=angle[:, 1], scalar=-c, in1=angle[:, 0],
                                                 op0=ALU.mult, op1=ALU.add))
                own(dve.tensor_scalar(angle[:, 2], angle[:, 0], top, -top, ALU.min, ALU.max))
                own(dve.scalar_tensor_tensor(out=angle[:, 1], in0=angle[:, 2], scalar=-1.0, in1=angle[:, 2],
                                             op0=ALU.mult, op1=ALU.max))
                dve.tensor_scalar(angle[:, 3], angle[:, 1], -1.0, float(np.pi / 2), ALU.mult,
                                  ALU.add).then_inc(bounds_exp, 2)

            def bounds():
                dve.wait_ge(par_in, 16)
                logits = par[:, LOGITS:LOGITS + HEADS]
                dve.tensor_tensor(logit[:, 0, :], logits, logits, ALU.subtract).then_inc(bounds_exp, 1)
                dve.wait_ge(bounds_done, 1)
                dve.reciprocal(logit[:, 2, :], logit[:, 1, :]).then_inc(bounds_done, 1)
                dve.wait_ge(bounds_done, 2)
                dve.tensor_tensor(logit[:, 3, :], logit[:, 1, :], logit[:, 2, :], ALU.mult).then_inc(bounds_done, 1)
                dve.wait_ge(bounds_done, 3)
                dve.tensor_tensor(bound[:, 0, :], logit[:, 3, :], logit[:, 3, :], ALU.subtract).then_inc(bounds_done, 1)
                dve.wait_ge(bounds_done, 4)
                dve.tensor_scalar(bound[:, 1, :], bound[:, 0, :], -1.0, 1.0, ALU.mult, ALU.add).then_inc(bounds_done, 1)

            def forget_step(i):
                for r in range(2):
                    wait(dve, turn_read[r], at["trans"].plus(1 - r).over(2))
                wait(dve, misc_full, at["misc"])
                dve.wait_ge(bounds_done, 5)
                for h in range(4):
                    head = bass.ds(i * 4 + h, 1)
                    ins = dve.tensor_scalar(forget[:, h, :], forget[:, h, :], bound[:, 1, head], bound[:, 0, head],
                                            ALU.mult, ALU.add)
                ins.then_inc(forget_own, 1)
                wait(dve, forget_own, at["forget"].plus(1))
                dve.tensor_scalar(fac[:, 0], forget[:], 1.0 / SPAN, None, ALU.max)
                dve.tensor_scalar(fac[:, 1], forget[:], MIN_FORGET, 1.0 / SPAN, ALU.max, ALU.min)
                dve.tensor_scalar(kk[:], forget[:], -1.0, 1.0, ALU.mult, ALU.add).then_inc(forget_bounded, 1)

            def cumsum():
                wait(dve, logs, at["log_forget"])
                dve.wait_ge(scan_in, 16)
                dve.tensor_tensor(fac[:, 0], fac[:, 0], fac[:, 1], ALU.add).then_inc(cumsum_own, 1)
                wait(dve, cumsum_own, at["cumsum"].plus(1))
                dve.tensor_tensor_scan(bb[:].rearrange("p h s -> p (h s)"), scan_mask[:].rearrange("p h s -> p (h s)"),
                                       fac[:, 0].rearrange("p h s -> p (h s)"), 0.0, ALU.mult,
                                       ALU.add).then_inc(cumsummed, 1)

            def decay(n):
                wait(dve, decay_exp, at["decay"].plus(1))
                f_lo, f_up = halves(fac[:, n % 2], LEVELS[n])
                k_lo, _ = halves(kk[:], LEVELS[n])
                _, q_up = halves(qq[:], LEVELS[n])
                dve.tensor_tensor(f_lo, f_lo, k_lo, ALU.mult)
                dve.tensor_tensor(f_up, f_up, q_up, ALU.mult).then_inc(factors, 1)

            def level(n, p):
                m = at["misc"]
                b = m.mod(2)
                wait(dve, misc_full, m.plus(1))
                heads = slice(2 * p, 2 * p + 2)
                if n == 0:
                    ins = dve.tensor_copy(scores_T[:, heads, 2, :], misc[:, b, 0:2 * P].rearrange("p (h s) -> p h s", h=2))
                else:
                    dve.memset(spare[:, 2 * n + p:2 * n + p + 1], 0.0)
                    dve.wait_ge(lmask_in, 16)
                    ins = dve.copy_predicated(
                        scores_T[:, heads, 0:2, :],
                        lmask[:, n, :].unsqueeze(1).unsqueeze(1).to_broadcast([P, 2, 2, P]),
                        misc[:, b, :].rearrange("p (h t s) -> p h t s", h=2, t=2))
                ins.then_inc(misc_read[b], 1)

            def mix(t):
                wait(dve, mix_squared, at["mix"].plus(1))
                dve.tensor_reduce(stat[:, t, :], square[:, t, :].rearrange("p (h v) -> p h v", h=4), AX.X,
                                  ALU.add).then_inc(mix_own, 1)

            def mix_norm():
                wait(dve, mix_own, at["mix"])
                dve.tensor_scalar(means4[:], stat[:], 1.0 / P, EPS, ALU.mult, ALU.add).then_inc(mix_mean, 1)
                wait(dve, mix_root, at["mix_norm"].plus(1))
                dve.reciprocal(rstd[:], root[:]).then_inc(mix_own2, 1)
                wait(dve, mix_own2, at["mix_norm"].plus(1))
                m0 = at["misc"].plus(-2)
                for t in range(T):
                    b = m0.plus(t).mod(2)
                    dve.tensor_tensor(rec[:, t, :].rearrange("p (h v) -> p h v", h=4),
                                      misc[:, b, :].rearrange("p (h v) -> p h v", h=4),
                                      rstd[:, t, :].unsqueeze(2).to_broadcast([P, 4, P]),
                                      ALU.mult).then_inc(misc_read[b], 1)
                for t in range(T):
                    c = m0.plus(t)
                    wait(dve, misc_read[c.mod(2)], c.over(2).plus(2))
                wait(dve, gate_scaled, at["hg_out"])
                dve.tensor_tensor(rec[:], rec[:], hgate[:], ALU.mult).then_inc(rec_made, 1)

            def latent_step(w):
                dve.wait_ge(lat_squared, 2 * (w + 1))
                mean(sq_sum[:, :, w], LORA, lat_mean, to=1)
                dve.wait_ge(lat_root, w + 1)
                dve.reciprocal(rstd[:, :, 1], root[:, :, 1]).then_inc(lat_inverse, 1)

            def rotate(out1, out2, src, t, heads):
                v = src.rearrange("p (h r) -> p h r", r=ROPE)
                o1 = out1.rearrange("p (h r) -> p h r", r=ROPE)
                o2 = out2.rearrange("p (h r) -> p h r", r=ROPE)
                half = ROPE // 2
                dve.tensor_tensor(o1, v, cos2[:, t, :].unsqueeze(1).to_broadcast([P, heads, ROPE]), ALU.mult)
                dve.tensor_tensor(o2[:, :, 0:half], v[:, :, half:ROPE],
                                  sin2[:, t, 0:half].unsqueeze(1).to_broadcast([P, heads, half]), ALU.mult)
                return dve.tensor_tensor(o2[:, :, half:ROPE], v[:, :, 0:half],
                                         sin2[:, t, half:ROPE].unsqueeze(1).to_broadcast([P, heads, half]), ALU.mult)

            def key_rope():
                b, g = acc_here()
                dve.wait_ge(sines, 1)
                for t in range(T):
                    ins = rotate(kpe_t1[:, t, :], kpe_t2[:, t, :], acc[:, b, t, 0:ROPE], t, 1)
                ins.then_inc(acc_read[b], 1)
                wait(dve, acc_read[b], g.over(2).plus(1))
                for c in range(2):
                    ins = dve.tensor_tensor(kpe_tok[:, :, c * ROPE:(c + 1) * ROPE], kpe_t1[:], kpe_t2[:], ALU.add)
                ins.then_inc(rope_key, 1)

            def q_rope(j):
                b, g = acc_here()
                for t in range(T):
                    ins = rotate(rope1[:, t, :], rope2[:, t, :], acc[:, b, t, 0:256], t, 4)
                ins.then_inc(acc_read[b], 1)
                wait(dve, acc_read[b], g.over(2).plus(1))
                dve.tensor_tensor(qp_tok[:], rope1[:], rope2[:], ALU.add).then_inc(rope_query, 1)

            def gate_ready(g):
                dve.wait_ge(acc_read[g % 2], g // 2 + 1)

            def branch_b(g, j, gate_group):
                b, _ = acc_here()
                gate_ready(gate_group)
                dve.tensor_tensor(tokens[:, :, j * N:(j + 1) * N], acc[:, b], gate_b[:, g], ALU.mult
                                  ).then_inc(acc_read[b], 1)

            def branch_a(g, j, gate_group):
                b, n = acc_here()
                gate_ready(gate_group)
                dve.tensor_tensor(gate_a[:, g], acc[:, b], gate_a[:, g], ALU.mult).then_inc(acc_read[b], 1)
                wait(dve, acc_read[b], n.over(2).plus(1))
                cols = tokens[:, :, j * N:(j + 1) * N]
                dve.tensor_tensor(cols, cols, gate_a[:, g], ALU.add).then_inc(merged_made, 1)

            def k_turn(j, p):
                b, u = banks(at)
                wait(dve, turn_full, u.plus(1))
                dve.tensor_copy(kT[:, j % 2, 2 * p:2 * p + 2, :].rearrange("p h s -> p (h s)"),
                                turn[:, b, :]).then_inc(turn_read[b], 1)

            def scores(h):
                m = at["misc"]
                b, r = m.mod(2), h % 2
                wait(dve, misc_full, m.plus(1))
                dve.wait_ge(causal_in, 16)
                dve.scalar_tensor_tensor(out=s_sb[:, r, :], in0=misc[:, b, 0:3 * P], scalar=SCALE, in1=causal[:],
                                         op0=ALU.mult, op1=ALU.add).then_inc(misc_read[b], 1)
                wait(dve, misc_read[b], m.over(2).plus(2))
                dve.tensor_reduce(neg_max[:, r, 0:1], s_sb[:, r, 0:P], AX.X, ALU.max, negate=True)
                dve.tensor_reduce(neg_max[:, r, 1:2], s_sb[:, r, P:3 * P], AX.X, ALU.max,
                                  negate=True).then_inc(maxima, 1)

            def probs_step(h):
                dve.wait_ge(exps, h + 1)
                dve.reciprocal(row_inv[:, h % 2, :], row_sum[:, h % 2, :]).then_inc(inverted, 1)

            def pv(h):
                m = at["misc"]
                b = m.mod(2)
                dve.wait_ge(att_hi, h + 1)
                dve.tensor_tensor(attT_lo[:, h, :], misc[:, b, 0:SEQ], f32(attT_hi[:, h, :]), ALU.subtract
                                  ).then_inc(misc_read[b], 1)

            def x2_out(j):
                b, _ = acc_here()
                dve.wait_ge(x_again_in, 16)
                cols = slice(j * N, (j + 1) * N)
                dve.tensor_tensor(tokens[:, :, cols], acc[:, b], x_again[:, :, cols], ALU.add).then_inc(acc_read[b], 1)

            def y_out(j):
                b, _ = acc_here()
                cols = slice(j * N, (j + 1) * N)
                dve.tensor_tensor(tokens[:, :, cols], acc[:, b], tokens[:, :, cols], ALU.add).then_inc(acc_read[b], 1)

            def conv(i, g, p):
                b, u = banks(at)
                wait(dve, tap0, at["conv"].plus(1))
                for back in (1, 2):
                    for f in range(2):
                        w = par[:, bass.ds(conv_taps(i, g, p, f) + 2 - back, 1)]
                        y = yconv[:, p, f, back:SEQ]
                        ins = dve.scalar_tensor_tensor(out=y, in0=turn[:, b, f * SEQ:(f + 1) * SEQ - back], scalar=w,
                                                       in1=y, op0=ALU.mult, op1=ALU.add)
                    if back == 1:
                        ins.then_inc(taps, 1)
                        wait(dve, taps, at["conv"].plus(1))
                ins.then_inc(turn_read[b], 1)

            def ff_gate(i, g):
                wait(dve, silu_made, at["ff_gate"].plus(1))
                dve.tensor_tensor(prod[:], silu_g[:], yconv[:, 1].rearrange("p f s -> p (f s)"),
                                  ALU.mult).then_inc(product, 1)
                wait(dve, act_hi, at["ff_gate"].plus(1))
                kt = bass.ds(i * 4 + 2 * g, 2)
                dve.tensor_tensor(actT_lo[:, kt, :].rearrange("p k s -> p (k s)"), prod[:],
                                  f32(actT_hi[:, kt, :].rearrange("p k s -> p (k s)")),
                                  ALU.subtract).then_inc(act_lo, 1)

            def final():
                summed_norm(2, None)
                dve.wait_ge(gain_in, 16)
                for h in range(2 * T):
                    t, cols = h // 2, slice((h % 2) * (D // 2), (h % 2 + 1) * (D // 2))
                    dve.scalar_tensor_tensor(out=tokens[:, t, cols], in0=tokens[:, t, cols], scalar=rstd[:, t, 0:1],
                                             in1=gain_row[:, cols], op0=ALU.mult, op1=ALU.mult
                                             ).then_inc(out_ready, 1)

            dve.memset(scores_T[:, 0:2], 0.0).then_inc(misc_read[0], 1)
            dve.memset(scores_T[:, 2:4], 0.0).then_inc(misc_read[1], 1)
            walk(dve, at, dict(split=split, x_norm=x_norm, operand=operand, tables=tables_step, bounds=bounds,
                               forget=forget_step, cumsum=cumsum, decay=decay, level=level, mix=mix,
                               mix_norm=mix_norm, latent=latent_step, key_rope=key_rope, q_rope=q_rope,
                               branch_b=branch_b, branch_a=branch_a, k_turn=k_turn, scores=scores, probs=probs_step,
                               pv=pv, x2_out=x2_out, h2_norm=h2_norm, conv=conv, ff_gate=ff_gate, y_out=y_out,
                               final=final))

        @block.gpsimd
        def _(pool):
            at = At()

            def hg_out():
                g = at["group"].plus(-1)
                wait(pool, acc_read[g.mod(2)], g.over(2).plus(1))
                v = hgate[:].rearrange("p t (h v) -> p (t h) v", h=4)
                pool.tensor_tensor(v, v, par[:, G_HGRN:G_HGRN + P].unsqueeze(1).to_broadcast([P, 4 * T, P]),
                                   ALU.mult).then_inc(gate_scaled, 1)

            def decay(n):
                h, f = LEVELS[n], fac[:, n % 2]
                wait(pool, cumsummed, at["cumsum"])
                if n >= 2:
                    wait(pool, misc_full, at["misc"].plus(-2))
                if h == 2 * CHUNK:
                    b4 = bb[:].rearrange("p h (c s) -> p h c s", s=CHUNK)
                    f4 = f.rearrange("p h (c s) -> p h c s", s=CHUNK)
                    end = b4[:, :, :, CHUNK - 1:CHUNK]
                    pool.tensor_tensor(sums01[:].unsqueeze(2), end[:, :, 0, :], end[:, :, 1, :],
                                       ALU.add).then_inc(pool_own, 1)
                    pool.tensor_tensor(f4[:, :, 1, :], end[:, :, 1, :].to_broadcast([P, 4, CHUNK]), b4[:, :, 1, :],
                                       ALU.subtract)
                    pool.tensor_copy(f4[:, :, 2, :], b4[:, :, 2, :])
                    pool.tensor_tensor(f4[:, :, 3, :], b4[:, :, 3, :], end[:, :, 2, :].to_broadcast([P, 4, CHUNK]),
                                       ALU.add)
                    wait(pool, pool_own, at["cumsum"])
                    pool.tensor_tensor(f4[:, :, 0, :], sums01[:].unsqueeze(2).to_broadcast([P, 4, CHUNK]),
                                       b4[:, :, 0, :], ALU.subtract).then_inc(decay_diff, 1)
                    return
                f_lo, f_up = halves(f, h)
                b_lo, b_up = halves(bb[:], h)
                blocks = 4 * SEQ // (2 * h)
                end = b_lo[:, :, h - 1:h].to_broadcast([P, blocks, h])
                pool.tensor_tensor(f_lo, end, b_lo, ALU.subtract)
                (pool.tensor_copy(f_up, b_up) if h == CHUNK else
                 pool.tensor_tensor(f_up, b_up, end, ALU.subtract)).then_inc(decay_diff, 1)

            def probs_step(h):
                r = h % 2
                pool.wait_ge(inverted, h + 1)
                pool.tensor_scalar(probs[:, r, 0:P], probs[:, r, 0:P], row_inv[:, r, 0:1], None, ALU.mult)
                pool.tensor_scalar(probs[:, r, P:3 * P], probs[:, r, P:3 * P], row_inv[:, r, 1:2], None,
                                   ALU.mult).then_inc(probs_made, 1)

            walk(pool, at, dict(hg_out=hg_out, decay=decay, probs=probs_step))


def conv_taps(i, g, p, f):
    return i * (2 * 16) + (CONV + 16 * g + 8 * p + 4 * f)


def shape_constants():
    c = np.zeros((P, N_CONST), np.float32)
    c[:, C_IDENT:C_IDENT + P] = np.eye(P)
    triangle = np.where(np.arange(P)[None, :] <= np.arange(P)[:, None], 0.0, MASKED)
    c[:, C_CAUSAL:C_CAUSAL + P] = triangle
    c[:, C_CAUSAL + 2 * P:C_CAUSAL + 3 * P] = triangle
    c[:, C_SCAN:C_SCAN + 4 * SEQ] = (np.arange(4 * SEQ) % CHUNK != 0)
    c[:, C_FREQ:] = np.float32(10000.0) ** (-np.arange(0, ROPE, 2, dtype=np.float32) / np.float32(ROPE))
    masks = np.zeros((P, len(LEVELS), P), np.int32)
    s, t = np.arange(P)[:, None], np.arange(P)[None, :]
    for n, h in enumerate(LEVELS):
        if h == 0:
            masks[:, n] = s == t
        elif h < P:
            masks[:, n] = (s // (2 * h) == t // (2 * h)) & (s // h % 2 == 0) & (t // h % 2 == 1)
    return c, masks


def kernel(**inputs):
    import concourse.bacc as bacc
    from concourse.bass_utils import run_bass_kernel_spmd

    a = {k: np.asarray(v) for k, v in inputs.items()}
    w_in, w_uq, w_ukv = a["w_in"][0], a["w_uq"][0], a["w_ukv"][0]
    w_a, w_b, w_out, w_up, w_down = (a[k][0] for k in ("w_branch_a", "w_branch_b", "w_out", "w_up", "w_down"))
    stream = np.empty((N_CHUNKS, P, CH), np.float32)
    n = 0

    def pack(w, k_tiles=2):
        nonlocal n
        count = w.shape[0] // (k_tiles * P)
        stream[n:n + count] = w.reshape(count, k_tiles, P, w.shape[1]).transpose(0, 2, 1, 3).reshape(count, P, CH)
        n += count

    o = np.concatenate([[0], np.cumsum([LORA, LORA, ROPE, D, D, D, D, D, D])])
    c_q, c_kv, k_rope, hq, hf, hi, hg, gate_a, gate_b = (w_in[:, o[k]:o[k + 1]] for k in range(9))

    def block(w, j):
        return w[:, j * N:(j + 1) * N]

    for j in range(QUADS):
        for w in (hf, hq, hi, hg):
            pack(block(w, j))
    pack(block(gate_b, 0))
    pack(block(gate_b, 1))
    pack(c_q)
    pack(c_kv)
    pack(k_rope, KT)
    pack(block(w_b, 0))
    pack(block(w_b, 1))
    for w in (gate_b, w_b):
        pack(block(w, 2))
        pack(block(w, 3))
    uq = w_uq.reshape(LORA, HEADS, NOPE + ROPE)
    ukv = w_ukv.reshape(LORA, HEADS, 2, 128)
    for j in range(QUADS):
        heads = slice(4 * j, 4 * j + 4)
        pack(uq[:, heads, :NOPE].reshape(LORA, N))
        pack(uq[:, heads, NOPE:].reshape(LORA, 256), 4)
        pack(ukv[:, heads, 0].reshape(LORA, N))
        pack(ukv[:, heads, 1].reshape(LORA, N))
    for first in (0, 2):
        for w in (gate_a, w_a):
            pack(block(w, first))
            pack(block(w, first + 1))
    for j in range(4):
        pack(block(w_out, j))
    up = w_up.reshape(D, 2, FF_GROUPS, 256)
    for g in range(FF_GROUPS):
        pack(up[:, :, g].reshape(D, N))
    for j in range(4):
        pack(block(w_down, j))
    assert n == N_CHUNKS

    def along_partitions(v):
        return v.reshape(-1, P).T

    taps = np.concatenate([a["conv_w"][0], a["conv_b"]], 0)
    taps = taps.reshape(4, 2, FF_GROUPS, 2, P).transpose(4, 2, 1, 3, 0).reshape(P, -1)
    params = np.concatenate([along_partitions(a[k][0]) for k in ("attn_norm_g", "q_norm_g", "kv_norm_g", "ffn_norm_g",
                                                                   "hgrn_lb_logits")]
                            + [np.broadcast_to(a["hgrn_out_norm_g"][0], (P, P)), taps], 1)
    constants, masks = shape_constants()
    arrays = {
        "weights": stream,
        "x": a["x"][0],
        "params": params,
        "consts": constants,
        "level_masks": masks,
        "positions": a["positions"][0].reshape(T, P).T,
        "final_gain": np.broadcast_to(a["final_norm_g"], (P, D)),
    }
    arrays = {k: np.ascontiguousarray(v) for k, v in arrays.items()}
    nc = bacc.Bacc("TRN2", target_bir_lowering=False, num_devices=1)
    aps = {k: nc.dram_tensor(k, v.shape, mybir.dt.from_np(v.dtype), kind="ExternalInput").ap()
           for k, v in arrays.items()}
    out = nc.dram_tensor("out", (SEQ, D), F32, kind="ExternalOutput").ap()
    build(nc, out=out, **aps)
    result = run_bass_kernel_spmd(nc, [arrays], core_ids=[0])
    return result.results[0]["out"].reshape(1, SEQ, D)
```

```python
from contextlib import ExitStack

import numpy as np

import concourse.bass as bass
from concourse import mybir

F32 = mybir.dt.float32
F32R = mybir.dt.float32r
I32 = mybir.dt.int32
ALU = mybir.AluOpType
ACT = mybir.ActivationFunctionType
AX = mybir.AxisListType

P = 128
SEQ = 256
T = SEQ // P
D = 2048
KT = D // P
HEADS = D // 128
NOPE, ROPE = 128, 64
LORA = 512
D_FF = 5632
N = 512
EPS = 1e-6
MIN_FORGET = 1e-30
SCALE = float(NOPE + ROPE) ** -0.5
MASKED = -1e30
CHUNK = 64
LEVELS = (128, 64, 32, 16, 8, 4, 2, 1, 0)
SPAN = float(2.0 ** 60)

RING = 4
CH = 2 * N
QUADS = HEADS // 4
GROUP_CHUNKS = KT // 2
FF_GROUPS = D_FF // 256
FF_KT = D_FF // P
UP_PAIRS = FF_GROUPS // 2
DOWN_CHUNKS = FF_KT // 2
N_CHUNKS = (4 * QUADS * GROUP_CHUNKS + 4 * 4 * GROUP_CHUNKS + 2 * GROUP_CHUNKS + 1 + 7 * QUADS
            + 4 * GROUP_CHUNKS + FF_GROUPS * GROUP_CHUNKS + 4 * DOWN_CHUNKS)

GROUP_GB = 4 * QUADS
GROUP_CQ = GROUP_GB + 2
GROUP_Q0 = GROUP_CQ + 3 + 6
GROUP_GA = GROUP_Q0 + 4 * QUADS
GROUP_OUT = GROUP_GA + 8

G_ATTN, G_Q, G_KV, G_FFN, LOGITS, G_HGRN, CONV = 0, 16, 20, 24, 40, 56, 184
N_PARAMS = CONV + 4 * 4 * FF_GROUPS
C_IDENT, C_CAUSAL, C_SCAN, C_FREQ = 0, 128, 512, 1536
N_CONST = C_FREQ + 32


class Count:

    def __init__(self, k, per=0, i=None, first=0):
        self.k, self.per, self.i, self.first = k, per, i, first

    def plus(self, n):
        return Count(self.k + n, self.per, self.i, self.first)

    def over(self, m):
        assert self.per % m == 0
        return Count(self.k // m, self.per // m, self.i, self.first)

    def mod(self, m):
        assert self.per % m == 0
        return self.k % m

    def times(self, m):
        return Count(self.k * m, self.per * m, self.i, self.first)

    def least(self):
        return self.k + self.per * self.first

    def value(self):
        return self.i * self.per + self.k if self.per else self.k


def wait(eng, sem, count):
    if count.least() <= 0:
        assert count.per == 0 or count.i is None, "a wait that may be void inside a loop"
        return
    eng.wait_ge(sem, count.value())


FAMILIES = {
    "trans": ("operand", "kr_turn", "kpe_turn", "qp_turn", "p_turn"),
    "misc": ("level", "mix", "scores", "pv", "row_scale"),
}


def names_of(step):
    name, args = step[0], step[1:]
    out = [name] + [f for f, members in FAMILIES.items() if name in members]
    if name == "chunk" and args[-1]:
        out.append("group")
    return out


def chunks(src, n, after=None, form="tokens", columns=N, nk=2):
    for k in range(n):
        first, last = k == 0, k == n - 1
        yield ("chunk", src, k * nk, nk, columns, 0 if first else None, form, first, last)
        yield from (after or {}).get(k, ())
        yield ("split",)


def hgrn_new(i):
    return {
        7: [("hf_out",)],
        17: [("hq_out", 2), ("forget", i)],
        19: [("log_forget",)],
        21: [("cumsum",)],
        23: [("hi_out",)],
        31: [("hg_out",)],
    }


def hgrn_old(i):
    table = {1: [("level", 8, 0), ("level", 8, 1)]}
    for n in range(len(LEVELS) - 1):
        table.setdefault(2 * n, []).append(("decay", n))
        table.setdefault(2 * n + 2, []).extend([("level", n, 0), ("level", n, 1)])
    table.setdefault(18, []).extend([("mix", 0), ("mix", 1)])
    table.setdefault(20, []).append(("mix_norm",))
    table.setdefault(24, []).extend([("operand", "rec", 0, i), ("operand", "rec", 1, i)])
    return table


def merged(*tables):
    out = {}
    for table in tables:
        for k, steps in table.items():
            out.setdefault(k, []).extend(steps)
    return out


def pick(table, start, n=GROUP_CHUNKS):
    return {k - start: s for k, s in table.items() if start <= k < start + n}


def hgrn_section(i, old):
    table = merged(hgrn_old(i - 1), hgrn_new(i)) if old else hgrn_new(i)
    if not old:
        yield from [("x_norm",), ("operand", "h", 0, 0), ("operand", "h", 1, 0)]
        yield from (("split",) for _ in range(RING))
        table = merged(table, {5: [("tables",)], 6: [("bounds",)]})
    for g in range(4):
        mine = pick(table, g * GROUP_CHUNKS)
        form = "features" if g < 2 else "tokens"
        if not old and g == 0:
            mine = merged({k: [("operand", "h", k + 2, 0)] for k in range(GROUP_CHUNKS - 2)}, mine)
            lags = {c: min(1, GROUP_CHUNKS - 1 - c) for c in range(GROUP_CHUNKS)}
            yield from with_lags(chunks("h", GROUP_CHUNKS, mine, form), lags)
        else:
            yield from chunks("h", GROUP_CHUNKS, mine, form)


def with_lags(steps, lags):
    for s in steps:
        if s[0] == "chunk":
            s = (*s[:5], lags.get(s[2] // 2), *s[6:])
        yield s


def branch_b_first():
    table = merged(hgrn_old(QUADS - 1), {
        7: [("gate_out", 0, "b")],
        15: [("gate_out", 1, "b")],
        23: [("latent", 0)],
        26: [("operand", "cq", 0, 0), ("operand", "cq", 1, 0)],
        31: [("latent", 1)],
    })
    for g in range(4):
        form = "features" if g < 2 else "tokens"
        yield from chunks("h", GROUP_CHUNKS, pick(table, g * GROUP_CHUNKS), form)
    yield from chunks("h", 1, {0: [("key_out",)]}, "features", columns=ROPE, nk=KT)
    yield from chunks("rec", GROUP_CHUNKS, {
        0: [("kr_turn",)],
        2: [("kpe_turn",)],
        3: [("operand", "ckv", 0, 0), ("operand", "ckv", 1, 0)],
        7: [("branch_b", 0, 0, GROUP_GB)]}, "features")
    yield from chunks("rec", GROUP_CHUNKS, {7: [("branch_b", 1, 1, GROUP_GB + 1)]}, "features")


def branch_b_second():
    for g in range(2):
        yield from chunks("h", GROUP_CHUNKS, {7: [("gate_out", g, "b")]}, "features")
    for g in range(2):
        yield from chunks("rec", GROUP_CHUNKS, {7: [("branch_b", g, 2 + g, GROUP_GB + 7 + g)]}, "features")


FIRST_HEAD = 8


def heads_at(slot):
    for back, name in ((4, "pv"), (2, "p_turn"), (1, "probs"), (0, "scores")):
        h = slot - back - FIRST_HEAD
        if h >= 0 and h % 2 == 0 and h // 2 < HEADS:
            yield (name, h // 2)


def attention_section():
    for j in range(QUADS):
        s = 7 * j
        yield from chunks("cq", 2, {0: list(heads_at(s)), 1: [*heads_at(s + 1), ("q_out", j)]}, "features")
        yield from chunks("cq", 1, {0: [*heads_at(s + 2), ("q_rope", j)]}, columns=256, nk=4)
        yield from chunks("ckv", 2, {
            0: [*heads_at(s + 3)],
            1: [*heads_at(s + 4), ("k_out", j), ("qp_turn", j)]}, "features")
        yield from chunks("ckv", 2, {
            0: [*heads_at(s + 5)],
            1: [*heads_at(s + 6), ("v_out", j)]})


def branch_a(first):
    slot = 7 * QUADS
    for g in range(2):
        table = {k: list(heads_at(slot + g * GROUP_CHUNKS + k)) if first else [] for k in range(GROUP_CHUNKS)}
        table[7].append(("gate_out", g, "a"))
        if not first:
            table[3].append(("merge", g))
        yield from chunks("h", GROUP_CHUNKS, table, "features")
        if not first and g == 0:
            yield ("reload_x",)
    for g in range(2):
        j = g if first else 2 + g
        table = {7: [("branch_a", g, j, GROUP_GA + (0 if first else 4) + g)]}
        if not first and g == 1:
            table[2] = [("merge", 2)]
        yield from chunks("att", GROUP_CHUNKS, table, "features")


def out_section():
    yield ("merge", 3)
    for j in range(4):
        table = {7: [("x2_out", j)]}
        if j > 0:
            table |= {k: [("operand", "h2", 2 * j - 2 + k // 2, 0)] for k in (1, 3)}
        lags = {0: 3, 2: 2, 4: 1, 6: 0} if j == 0 else {}
        yield from with_lags(chunks("merged", GROUP_CHUNKS, table), lags)


def up_first():
    table = {0: [("h2_norm",)], 1: [("operand", "h2", 6, 0)], 2: [("operand", "h2", 7, 0)],
             4: [("row_scale",)], 7: [("up_out",)]}
    yield from with_lags(chunks("h", GROUP_CHUNKS, table, "features"), {0: 0, 6: 0})
    yield from chunks("h", GROUP_CHUNKS, {
        1: [("conv", 0, 0)], 3: [("ff_gate", 0, 0)], 7: [("up_out",)]}, "features")


def up_section(i):
    for g in range(2):
        yield from chunks("h", GROUP_CHUNKS, {
            1: [("conv", i, g - 1)], 3: [("ff_gate", i, g - 1)], 7: [("up_out",)]}, "features")


def down_section():
    last = FF_GROUPS - 1
    for j in range(4):
        table = {DOWN_CHUNKS - 1: [("y_out", j)]}
        if j == 0:
            table |= {1: [("conv", 0, last)], 3: [("ff_gate", 0, last)],
                      6: [("load_final_gain",)]}
        steps = list(chunks("act", DOWN_CHUNKS, table))
        if j == 0:
            steps = [(*s[:5], 0, *s[6:]) if s[0] == "chunk" and s[2] == FF_KT - 2 else s for s in steps]
        if j == 3:
            ends = [k for k, s in enumerate(steps) if s[0] == "split"][-RING:]
            steps = [s for k, s in enumerate(steps) if k not in ends]
        yield from steps
    yield ("final",)


SECTIONS = (
    (lambda i: hgrn_section(0, False), None, None),
    (lambda i: hgrn_section(i, True), 1, QUADS),
    (lambda i: branch_b_first(), None, None),
    (lambda i: branch_b_second(), None, None),
    (lambda i: attention_section(), None, None),
    (lambda i: branch_a(True), None, None),
    (lambda i: branch_a(False), None, None),
    (lambda i: out_section(), None, None),
    (lambda i: up_first(), None, None),
    (lambda i: up_section(i), 1, UP_PAIRS),
    (lambda i: down_section(), None, None),
)


class At:

    def __init__(self):
        self.done, self.rate, self.i, self.first = {}, {}, None, 0

    def __getitem__(self, name):
        per = self.rate.get(name, 0) if self.i is not None else 0
        return Count(self.done.get(name, 0) - per * self.first, per, self.i if per else None, self.first)

    def passed(self, step):
        for name in names_of(step):
            self.done[name] = self.done.get(name, 0) + 1


def walk(eng, at, do):
    for make, first, end in SECTIONS:
        if first is None:
            for step in make(None):
                if step[0] in do:
                    do[step[0]](*step[1:])
                at.passed(step)
            continue
        rate = {}
        for step in make(0):
            for name in names_of(step):
                rate[name] = rate.get(name, 0) + 1
        if not any(step[0] in do for step in make(0)):
            for name, n in rate.items():
                at.done[name] = at.done.get(name, 0) + n * (end - first)
            continue
        before = dict(at.done)
        with eng.Fori(first, end) as i:
            at.rate, at.i, at.first = rate, i, first
            for step in make(i):
                if step[0] in do:
                    do[step[0]](*step[1:])
                at.passed(step)
        at.rate, at.i, at.first = {}, None, 0
        at.done = {n: before.get(n, 0) + rate.get(n, 0) * (end - first) for n in {*before, *rate}}


def build(nc, weights, x, params, consts, level_masks, positions, final_gain, out):
    with ExitStack() as ctx:
        def sem(name):
            return ctx.enter_context(nc.semaphore(name))

        arena_bytes = 212480
        base = -(-nc.sbuf_base // 32) * 32
        ctx.enter_context(nc.sbuf_tensor("arena", [P, arena_bytes // 4], F32))
        assert nc.sbuf_base >= base + arena_bytes

        def place(name, offset, shape, dtype=F32):
            offset = -(-offset // 32) * 32
            size = int(np.prod(shape)) * 4
            assert offset + size <= arena_bytes, (name, offset + size)
            return nc.alloc_sbuf_tensor_at(name, [P, *shape], dtype, offset=base + offset), offset + size

        o = 0
        raw, o = place("raw", o, [RING, CH])
        w_hi, o = place("w_hi", o, [RING, CH], F32R)
        w_lo, o = place("w_lo", o, [RING, CH], F32R)
        hT_hi, o = place("hT_hi", o, [KT, SEQ], F32R)
        hT_lo, o = place("hT_lo", o, [KT, SEQ], F32R)
        merged, _ = place("merged", o, [4, T, N])
        tokens, o = place("tokens", o, [T, D])
        piece, o = place("piece", o, [2, N])
        par, o = place("par", o, [N_PARAMS])
        ident, o = place("ident", o, [P])
        factor_diag, _ = place("factor_diag", o, [T, P])
        causal, o = place("causal", o, [3 * P])
        factor_row, _ = place("factor_row", o, [SEQ])
        cos2, o = place("cos2", o, [T, ROPE])
        sin2, o = place("sin2", o, [T, ROPE])
        ones, _ = place("ones", o, [P])
        kpeT, o = place("kpeT", o, [SEQ])
        sq_sum, o = place("sq_sum", o, [T, 4])
        stat, o = place("stat", o, [T, 4])
        root, o = place("root", o, [T, 4])
        rstd, o = place("rstd", o, [T, 4])
        bound, o = place("bound", o, [2, HEADS])
        pos_f, o = place("pos_f", o, [T])
        spare, o = place("spare", o, [2 * len(LEVELS)])
        shared = o

        recT_hi, o = place("recT_hi", shared, [KT, SEQ], F32R)
        recT_lo, o = place("recT_lo", o, [KT, SEQ], F32R)
        latents = o
        kk, o = place("kk", o, [4, SEQ])
        qq, o = place("qq", o, [4, SEQ])
        bb, o = place("bb", o, [4, SEQ])
        fac, o = place("fac", o, [2, 4, SEQ])
        rest = o
        forget, o = place("forget", o, [4, SEQ])
        krT, o = place("krT", o, [SEQ])
        kpe_tok, o = place("kpe_tok", o, [T, P])
        kpe_t1, o = place("kpe_t1", o, [T, ROPE])
        kpe_t2, o = place("kpe_t2", o, [T, ROPE])
        scores_T, o = place("scores_T", o, [4, 3, P])
        junk, _ = place("junk", o, [T, D])
        hv, o = place("hv", o, [T, N])
        hgate, o = place("hgate", o, [T, N])
        rec, o = place("rec", o, [T, N])
        square, o = place("square", o, [T, N])
        scan_mask, o = place("scan_mask", o, [4, SEQ])
        lmask, o = place("lmask", o, [len(LEVELS), P], I32)
        sums01, o = place("sums01", o, [4])
        gate_b_at = o
        gate_b, o = place("gate_b", o, [2, T, N])
        means4, o = place("means4", o, [T, 4])

        cqT_hi, o = place("cqT_hi", latents, [4, SEQ], F32R)
        cqT_lo, o = place("cqT_lo", o, [4, SEQ], F32R)
        ckvT_hi, o = place("ckvT_hi", o, [4, SEQ], F32R)
        ckvT_lo, o = place("ckvT_lo", o, [4, SEQ], F32R)
        assert o <= rest
        latent, _ = place("latent", rest, [T, N])
        gate_a, _ = place("gate_a", latents, [2, T, N])
        angle, o = place("angle", gate_b_at, [4, T, 32])
        freq, o = place("freq", o, [32])
        logit, o = place("logit", o, [4, HEADS])
        pos_i, _ = place("pos_i", o, [T], I32)

        attT_hi, o = place("attT_hi", shared, [KT, SEQ], F32R)
        attT_lo, o = place("attT_lo", o, [KT, SEQ], F32R)
        qp_tok, o = place("qp_tok", latents + 16384, [T, 256])
        rope1, o = place("rope1", o, [T, 256])
        rope2, o = place("rope2", o, [T, 256])
        qT, o = place("qT", o, [2, 4, SEQ])
        kT, o = place("kT", o, [2, 4, SEQ])
        s_sb, o = place("s_sb", o, [2, 3 * P])
        probs, o = place("probs", o, [2, 3 * P])
        probsT, o = place("probsT", o, [2, 3 * P])
        neg_max, o = place("neg_max", o, [2, T])
        row_sum, o = place("row_sum", o, [2, T])
        row_inv, o = place("row_inv", o, [2, T])
        qpT, o = place("qpT", o, [2, 2, SEQ])
        vv, o = place("vv", o, [2, T, N])

        x_again, o = place("x_again", latents + 16384, [T, D])
        merged_hi, o = place("merged_hi", o, [KT, SEQ], F32R)
        merged_lo, o = place("merged_lo", o, [KT, SEQ], F32R)
        x2_squares, _ = place("x2_squares", shared, [T, N])

        actT_hi, o = place("actT_hi", shared, [FF_KT, SEQ], F32R)
        actT_lo, o = place("actT_lo", o, [FF_KT, SEQ], F32R)
        uT, o = place("uT", o, [4, SEQ])
        yconv, o = place("yconv", o, [2, 2, SEQ])
        silu_g, o = place("silu_g", o, [2 * SEQ])
        prod, o = place("prod", o, [2 * SEQ])
        gain_row, o = place("gain_row", 3 * RING * CH * 4, [D])
        result, _ = place("result", o, [T, D])

        acc = ctx.enter_context(nc.psum_tensor("acc", [P, 2, T, N], F32))
        turn = ctx.enter_context(nc.psum_tensor("turn", [P, 2, N], F32))
        misc = ctx.enter_context(nc.psum_tensor("misc", [P, 2, N], F32))

        raw_in = [sem(f"raw_in{s}") for s in range(RING)]
        hi_made, lo_made, chunk_used = sem("hi_made"), sem("lo_made"), sem("chunk_used")
        acc_read = [sem("acc_read0"), sem("acc_read1")]
        turn_full, misc_full = sem("turn_full"), sem("misc_full")
        turn_read = [sem("turn_read0"), sem("turn_read1")]
        misc_read = [sem("misc_read0"), sem("misc_read1")]
        operand_hi, operand_lo = sem("operand_hi"), sem("operand_lo")
        x_in = [sem("x_in0"), sem("x_in1")]
        par_in, const_in, scan_in, lmask_in = sem("par_in"), sem("const_in"), sem("scan_in"), sem("lmask_in")
        causal_in, freq_in, pos_in = sem("causal_in"), sem("freq_in"), sem("pos_in")
        x_again_in, gain_in, stored = sem("x_again_in"), sem("gain_in"), sem("stored")
        squares, means, roots, normed0, normed1 = (
            sem("squares"), sem("means"), sem("roots"), sem("normed0"), sem("normed1"))
        inverses = sem("inverses")
        bounds_exp, bounds_done, sines = sem("bounds_exp"), sem("bounds_done"), sem("sines")
        forget_bounded, logs, cumsummed = sem("forget_bounded"), sem("logs"), sem("cumsummed")
        decay_diff, decay_exp, factors = sem("decay_diff"), sem("decay_exp"), sem("factors")
        gate_scaled, mix_squared, mix_mean, mix_root, rec_made = (
            sem("gate_scaled"), sem("mix_squared"), sem("mix_mean"), sem("mix_root"), sem("rec_made"))
        lat_squared, lat_mean, lat_root, lat_inverse = (
            sem("lat_squared"), sem("lat_mean"), sem("lat_root"), sem("lat_inverse"))
        rope_key, maxima, exps, inverted, probs_made, att_hi = (
            sem("rope_key"), sem("maxima"), sem("exps"), sem("inverted"), sem("probs_made"), sem("att_hi"))
        rope_query = sem("rope_query")
        diag_made, factors_out = sem("diag_made"), sem("factors_out")
        tap0, taps, silu_made, product, act_hi, act_lo = (
            sem("tap0"), sem("taps"), sem("silu_made"), sem("product"), sem("act_hi"), sem("act_lo"))
        pool_own = sem("pool_own")
        sum_own, table_own, forget_own, cumsum_own, mix_own, mix_own2 = (
            sem("sum_own"), sem("table_own"), sem("forget_own"), sem("cumsum_own"), sem("mix_own"), sem("mix_own2"))
        merged_made, merged_his, merged_los = sem("merged_made"), sem("merged_his"), sem("merged_los")
        gained = sem("gained")
        result_ready = [sem("result_ready0"), sem("result_ready1")]

        operands = {"h": (hT_hi, hT_lo), "rec": (recT_hi, recT_lo), "cq": (cqT_hi, cqT_lo),
                    "ckv": (ckvT_hi, ckvT_lo), "att": (attT_hi, attT_lo), "merged": (merged_hi, merged_lo),
                    "act": (actT_hi, actT_lo)}
        targets = {"h": "h", "h2": "h", "rec": "rec", "cq": "cq", "ckv": "ckv"}
        rows_of = {"h": tokens, "h2": tokens, "rec": rec, "cq": latent, "ckv": latent}
        gains = {"h": G_ATTN, "h2": G_FFN, "cq": G_Q, "ckv": G_KV}

        def f32(ap):
            return ap.bitcast(F32)

        def banks(at):
            u = at["trans"]
            return u.mod(2), u

        def halves(ap, h):
            v = ap.rearrange("p a s -> p (a s)").rearrange("p (m two h) -> p m two h", two=2, h=h)
            return v[:, :, 0, :], v[:, :, 1, :]

        block = ctx.enter_context(nc.Block())

        @block.sync
        def _(sp):
            for t in range(T):
                sp.dma_start(tokens[:, t, :], x[t * P:(t + 1) * P, :]).then_inc(x_in[t], 16)
                if t == 0:
                    sp.dma_start(ident[:], consts[:, C_IDENT:C_IDENT + P]).then_inc(const_in, 16)
            sp.dma_start(par[:], params).then_inc(par_in, 16)

            def load(slot, n):
                sp.dma_start(raw[:, slot, :], weights[bass.ds(n, 1), :, :].rearrange("a p c -> p (a c)")
                             ).then_inc(raw_in[slot], 16)

            for s in range(RING):
                load(s, s)
            with sp.Fori(1, N_CHUNKS // RING) as r:
                for s in range(RING):
                    sp.wait_ge(lo_made, r * RING + (s + 1 - RING))
                    load(s, r * RING + s)
            for n in range(N_CHUNKS // RING * RING, N_CHUNKS):
                sp.wait_ge(lo_made, n + 1 - RING)
                load(n % RING, n)
            for part in range(2):
                for t in range(T):
                    sp.wait_ge(result_ready[t], part + 1)
                    cols = slice(part * (D // 2), (part + 1) * (D // 2))
                    sp.dma_start(out[t * P:(t + 1) * P, cols], result[:, t, cols]).then_inc(stored, 16)
            sp.wait_ge(stored, 16 * 2 * T)

        @block.tensor
        def _(pe):
            at = At()
            p_bank = {}

            def chunk(src, k0, nk, columns, lag, form, first, last):
                n, g = at["chunk"], at["group"]
                slot, b = n.mod(RING), g.mod(2)
                hi, lo = operands[src]
                wh = w_hi[:, slot, 0:nk * columns].rearrange("p (k c) -> p k c", c=columns)
                wl = w_lo[:, slot, 0:nk * columns].rearrange("p (k c) -> p k c", c=columns)
                wait(pe, lo_made, n.plus(1))
                if first:
                    wait(pe, acc_read[b], g.over(2))
                    if src == "att":
                        for m in range(2):
                            wait(pe, misc_read[m], at["misc"].plus(1 - m).over(2).plus(1))
                if lag is not None:
                    if src == "act":
                        wait(pe, act_lo, at["ff_gate"])
                    elif src == "merged":
                        wait(pe, merged_los, at["merge"].plus(-lag))
                    else:
                        wait(pe, operand_lo, at["operand"].plus(-lag))
                for k in range(nk if form == "features" else 0):
                    for c in range(0, columns, P):
                        width = min(P, columns - c)
                        half, at_col = c // (2 * P), c % (2 * P) // P * SEQ
                        to = acc[0:width, b, half, at_col:at_col + SEQ]
                        begin = first and k == 0 and at_col == 0
                        end = last and k == nk - 1 and (at_col > 0 or columns <= P)
                        w_h, w_l = wh[:, k, c:c + width], wl[:, k, c:c + width]
                        pe.matmul(to, w_h, hi[:, k0 + k, :], start=begin, stop=False)
                        pe.matmul(to, w_h, lo[:, k0 + k, :], start=False, stop=False)
                        ins = pe.matmul(to, w_l, hi[:, k0 + k, :], start=False, stop=end)
                for k in range(nk if form == "tokens" else 0):
                    for t in range(T):
                        x_h = hi[:, k0 + k, t * P:(t + 1) * P]
                        x_l = lo[:, k0 + k, t * P:(t + 1) * P]
                        to = acc[:, b, t, 0:columns]
                        begin, end = first and k == 0, last and k == nk - 1
                        pe.matmul(to, x_h, wh[:, k, :], start=begin, stop=False)
                        pe.matmul(to, x_h, wl[:, k, :], start=False, stop=False)
                        ins = pe.matmul(to, x_l, wh[:, k, :], start=False, stop=end)
                ins.then_inc(chunk_used, 1)

            def turn_bank():
                b, u = banks(at)
                wait(pe, turn_read[b], u.over(2))
                return b

            def turns(b, pieces):
                for q, (src, rows) in enumerate(pieces):
                    ins = pe.transpose(turn[0:rows, b, q * P:(q + 1) * P], src, ident[:])
                ins.then_inc(turn_full, 1)

            def operand(kind, p, i):
                b = turn_bank()
                if kind == "h":
                    if p == 0:
                        pe.wait_ge(normed0, 1)
                        pe.wait_ge(normed1, 1)
                        pe.wait_ge(const_in, 16)
                elif kind == "h2":
                    g = GROUP_OUT + p // 2
                    pe.wait_ge(acc_read[g % 2], g // 2 + 1)
                elif kind == "rec":
                    wait(pe, rec_made, at["mix_norm"])
                elif kind in ("cq", "ckv"):
                    g = GROUP_CQ if kind == "cq" else GROUP_CQ + 1
                    pe.wait_ge(acc_read[g % 2], g // 2 + 1)
                rows = rows_of[kind]
                turns(b, [(rows[:, t, (2 * p + k) * P:(2 * p + k + 1) * P], P) for k in range(2) for t in range(T)])

            def kr_turn():
                b = turn_bank()
                g = at["group"].plus(-1)
                wait(pe, acc_read[g.mod(2)], g.over(2).plus(1))
                for t in range(T):
                    ins = pe.transpose(turn[:, b, t * ROPE:(t + 1) * ROPE], krT[0:ROPE, t * P:(t + 1) * P],
                                       ident[0:ROPE, 0:ROPE])
                ins.then_inc(turn_full, 1)

            def kpe_turn():
                b = turn_bank()
                pe.wait_ge(rope_key, 1)
                turns(b, [(kpe_tok[:, t, :], P) for t in range(T)])

            def level(n, p):
                m = at["misc"]
                b, h, f = m.mod(2), LEVELS[n], fac[:, n % 2]
                wait(pe, misc_read[b], m.over(2).plus(1))
                if h:
                    wait(pe, factors, at["decay"])
                else:
                    wait(pe, forget_bounded, at["forget"])
                    g = at["group"].plus(-3)
                    wait(pe, acc_read[g.mod(2)], g.over(2).plus(1))
                for a in range(2):
                    head = 2 * p + a
                    if h == 2 * CHUNK:
                        ins = pe.matmul(misc[:, b, a * P:(a + 1) * P], f[:, head, 0:P], f[:, head, P:2 * P],
                                        start=True, stop=True)
                        continue
                    for t in range(T):
                        cols, q = slice(t * P, (t + 1) * P), 2 * a + t
                        keys, queries = (f, f) if h else (kk, qq)
                        if h == CHUNK:
                            ins = pe.matmul(misc[0:h, b, q * P + h:(q + 1) * P], keys[:, head, t * P:t * P + h],
                                            queries[:, head, t * P + h:(t + 1) * P], start=True, stop=True)
                            continue
                        ins = pe.matmul(misc[:, b, q * P:(q + 1) * P], keys[:, head, cols], queries[:, head, cols],
                                        start=True, stop=True)
                ins.then_inc(misc_full, 1)

            def mix(t):
                m = at["misc"]
                b = m.mod(2)
                wait(pe, misc_read[b], m.over(2).plus(1))
                if t == 0:
                    wait(pe, misc_read[1 - b], m.plus(1 - (1 - b)).over(2).plus(1))
                for h in range(4):
                    to = misc[:, b, h * P:(h + 1) * P]
                    cols = slice(h * P, (h + 1) * P)
                    if t == 0:
                        ins = pe.matmul(to, scores_T[:, h, 0, :], hv[:, 0, cols], start=True, stop=True)
                    else:
                        pe.matmul(to, scores_T[:, h, 2, :], hv[:, 0, cols], start=True, stop=False)
                        ins = pe.matmul(to, scores_T[:, h, 1, :], hv[:, 1, cols], start=False, stop=True)
                ins.then_inc(misc_full, 1)

            def q_group(j):
                return Count(GROUP_Q0 + 4 * j)

            def qp_turn(j):
                b = turn_bank()
                pe.wait_ge(rope_query, j + 1)
                turns(b, [(qp_tok[:, t, a * P:(a + 1) * P], P) for a in range(2) for t in range(T)])

            def scores(h):
                m = at["misc"]
                b, j, a = m.mod(2), h // 4, h % 4
                wait(pe, misc_read[b], m.over(2).plus(1))
                if a == 0:
                    for r in range(2):
                        wait(pe, turn_read[r], at["trans"].plus(1 - r).over(2))
                    for g in (q_group(j).plus(2), q_group(j).plus(3)):
                        wait(pe, acc_read[g.mod(2)], g.over(2).plus(1))
                half = slice((a % 2) * ROPE, (a % 2 + 1) * ROPE)
                for t in range(T):
                    to = misc[:, b, 0:P] if t == 0 else misc[:, b, P:3 * P]
                    keys = (t + 1) * P
                    pe.matmul(to, qT[:, j % 2, a, t * P:(t + 1) * P], kT[:, j % 2, a, 0:keys], start=True, stop=False)
                    ins = pe.matmul(to, qpT[half, j % 2, a // 2, t * P:(t + 1) * P], kpeT[half, 0:keys],
                                    start=False, stop=True)
                ins.then_inc(misc_full, 1)

            def p_turn(h):
                b = turn_bank()
                pe.wait_ge(probs_made, h + 1)
                p_bank[h] = at["trans"].k
                turns(b, [(probs[:, h % 2, q * P:(q + 1) * P], P) for q in range(3)])

            def pv(h):
                m = at["misc"]
                b, j, a = m.mod(2), h // 4, h % 4
                wait(pe, misc_read[b], m.over(2).plus(1))
                u = p_bank[h]
                wait(pe, turn_read[u % 2], Count(u // 2 + 1))
                cols = slice(a * P, (a + 1) * P)
                pe.matmul(misc[:, b, 0:P], vv[:, j % 2, 0, cols], probsT[:, h % 2, 0:P], start=True, stop=True)
                pe.matmul(misc[:, b, P:2 * P], vv[:, j % 2, 0, cols], probsT[:, h % 2, P:2 * P], start=True, stop=False)
                pe.matmul(misc[:, b, P:2 * P], vv[:, j % 2, 1, cols], probsT[:, h % 2, 2 * P:3 * P],
                          start=False, stop=True).then_inc(misc_full, 1)

            def row_scale():
                b = at["misc"].mod(2)
                wait(pe, misc_read[b], at["misc"].over(2).plus(1))
                pe.wait_ge(diag_made, 1)
                for t in range(T):
                    ins = pe.matmul(misc[:, b, t * P:(t + 1) * P], ones[:], factor_diag[:, t, :], start=True, stop=True)
                ins.then_inc(misc_full, 1)

            walk(pe, at, dict(chunk=chunk, operand=operand, kr_turn=kr_turn, kpe_turn=kpe_turn,
                              level=level, mix=mix, qp_turn=qp_turn, scores=scores, p_turn=p_turn, pv=pv,
                              row_scale=row_scale))

        @block.scalar
        def _(act):
            at = At()

            def from_acc(out_ap, func, extra=(), since=0):
                g = at["group"].plus(-1)
                wait(act, chunk_used, at["chunk"].plus(-since))
                for s, count in extra:
                    wait(act, s, count)
                act.activation(out_ap, acc[:, g.mod(2)], func).then_inc(acc_read[g.mod(2)], 1)

            def heads_rows(ap):
                return ap.rearrange("p (t h) s -> p t (h s)", t=T)

            def from_turn(out_ap, func, columns=N):
                b, u = banks(at)
                wait(act, turn_full, u.plus(1))
                act.activation(out_ap, turn[:, b, 0:columns], func).then_inc(turn_read[b], 1)

            def split():
                n = at["split"]
                slot = n.mod(RING)
                wait(act, raw_in[slot], n.over(RING).plus(1).times(16))
                wait(act, chunk_used, n.plus(1 - RING))
                act.activation(w_hi[:, slot, :], raw[:, slot, :], ACT.Copy).then_inc(hi_made, 1)

            def x_norm():
                for t in range(T):
                    act.wait_ge(x_in[t], 16)
                    act.activation(junk[:, t, :], tokens[:, t, :], ACT.Square,
                                   accum_out=sq_sum[:, t, 0:1]).then_inc(squares, 1)
                normalise(0, tokens)

            def normalise(which, to):
                act.wait_ge(means, which + 1)
                act.activation(root[:, :, 0], stat[:, :, 0], ACT.Sqrt).then_inc(roots, 1)
                act.wait_ge(inverses, which + 1)
                if to is not None:
                    act.activation(to[:, 0, :], tokens[:, 0, :], ACT.Copy, scale=rstd[:, 0, 0:1]).then_inc(normed0, 1)

            def operand(kind, p, i):
                b, u = banks(at)
                s = at["operand"]
                hi = operands[targets[kind]][0]
                kt = bass.ds(i * 4 + 2 * p, 2) if kind == "rec" else slice(2 * p, 2 * p + 2)
                wait(act, turn_read[b], u.over(2).plus(1))
                act.activation(hi[:, kt, :].rearrange("p k s -> p (k s)"), piece[:, s.mod(2), :],
                               ACT.Copy).then_inc(operand_hi, 1)

            def tables_step():
                act.wait_ge(bounds_exp, 2)
                act.activation(sin2[:, :, 0:32], angle[:, 2], ACT.Sin, scale=-1.0)
                act.activation(sin2[:, :, 32:64], angle[:, 2], ACT.Sin)
                act.activation(cos2[:, :, 0:32], angle[:, 3], ACT.Sin)
                act.activation(cos2[:, :, 32:64], angle[:, 3], ACT.Sin).then_inc(sines, 1)

            def bounds():
                act.wait_ge(bounds_exp, 3)
                act.activation(logit[:, 1, :], logit[:, 0, :], ACT.Exp).then_inc(bounds_done, 1)

            def hf_out():
                from_acc(heads_rows(forget[:]), ACT.Sigmoid)

            def hq_out(since):
                from_acc(heads_rows(qq[:]), ACT.Silu, [(misc_full, at["misc"])], since)

            def log_forget():
                wait(act, forget_bounded, at["forget"])
                act.activation(fac[:, 0], fac[:, 0], ACT.Ln)
                act.activation(fac[:, 1], fac[:, 1], ACT.Ln, scale=SPAN).then_inc(logs, 1)

            def hi_out():
                from_acc(hv[:], ACT.Copy)

            def hg_out():
                from_acc(hgate[:], ACT.Silu, [(rec_made, at["mix_norm"])])

            def decay(n):
                wait(act, decay_diff, at["decay"].plus(1))
                act.activation(fac[:, n % 2], fac[:, n % 2], ACT.Exp).then_inc(decay_exp, 1)

            def mix(t):
                m = at["misc"]
                wait(act, misc_full, m.plus(1))
                act.activation(square[:, t, :], misc[:, m.mod(2), :], ACT.Square).then_inc(mix_squared, 1)

            def mix_norm():
                wait(act, mix_mean, at["mix_norm"].plus(1))
                act.activation(root[:], means4[:], ACT.Sqrt).then_inc(mix_root, 1)

            def gate_out(g, which):
                if which == "a":
                    from_acc(gate_a[:, g], ACT.Sigmoid, [(merged_made, at["branch_a"])])
                else:
                    from_acc(gate_b[:, g], ACT.Sigmoid)

            def latent_step(w):
                g = at["group"].k - 1
                b = g % 2
                wait(act, chunk_used, at["chunk"])
                for t in range(T):
                    act.activation(square[:, t, :], acc[:, b, t, :], ACT.Square,
                                   accum_out=sq_sum[:, t, w:w + 1]).then_inc(lat_squared, 1)
                act.wait_ge(lat_mean, w + 1)
                act.activation(root[:, :, 1], stat[:, :, 1], ACT.Sqrt).then_inc(lat_root, 1)
                act.wait_ge(lat_inverse, w + 1)
                wait(act, turn_full, at["trans"])
                act.activation(latent[:, 0, :], acc[:, b, 0, :], ACT.Copy, scale=rstd[:, 0, 1:2])
                act.activation(latent[:, 1, :], acc[:, b, 1, :], ACT.Copy,
                               scale=rstd[:, 1, 1:2]).then_inc(acc_read[b], 1)

            def key_out():
                g = at["group"].plus(-1)
                wait(act, chunk_used, at["chunk"])
                act.activation(krT[0:ROPE, :], acc[0:ROPE, g.mod(2), 0, 0:SEQ], ACT.Copy).then_inc(acc_read[g.mod(2)], 1)

            def kpe_turn():
                from_turn(kpeT[:], ACT.Copy, SEQ)

            def q_out(j):
                from_acc(heads_rows(qT[:, j % 2]), ACT.Copy, [(misc_full, at["misc"])])

            def k_out(j):
                from_acc(heads_rows(kT[:, j % 2]), ACT.Copy, [(misc_full, at["misc"])])

            def v_out(j):
                from_acc(vv[:, j % 2], ACT.Copy, [(misc_full, at["misc"])])

            def qp_turn(j):
                from_turn(qpT[:, j % 2].rearrange("p h s -> p (h s)"), ACT.Copy)

            def scores(h):
                r = h % 2
                act.wait_ge(maxima, h + 1)
                act.activation(probs[:, r, 0:P], s_sb[:, r, 0:P], ACT.Exp, bias=neg_max[:, r, 0:1],
                               accum_out=row_sum[:, r, 0:1])
                act.activation(probs[:, r, P:3 * P], s_sb[:, r, P:3 * P], ACT.Exp, bias=neg_max[:, r, 1:2],
                               accum_out=row_sum[:, r, 1:2]).then_inc(exps, 1)

            def p_turn(h):
                from_turn(probsT[:, h % 2, :], ACT.Copy, 3 * P)

            def pv(h):
                m = at["misc"]
                wait(act, misc_full, m.plus(1))
                act.activation(attT_hi[:, h, :], misc[:, m.mod(2), 0:SEQ], ACT.Copy).then_inc(att_hi, 1)

            def reload_x():
                wait(act, chunk_used, at["chunk"])
                wait(act, merged_made, at["branch_a"])
                act.dma_start(x_again[:], x.rearrange("(t p) d -> p t d", p=P)).then_inc(x_again_in, 16)

            def merge(j):
                wait(act, chunk_used, at["chunk"].plus(-2))
                wait(act, merged_made, Count(j + 1))
                act.activation(merged_hi[:, 4 * j:4 * j + 4, :], merged[:, j].rearrange("p t (h s) -> p (t h) s", s=SEQ),
                               ACT.Copy).then_inc(merged_his, 1)

            def squares_of(junk_rows, j):
                g = at["group"].k - 1
                act.wait_ge(acc_read[g % 2], g // 2 + 1)
                for t in range(T):
                    act.activation(junk_rows[:, t, :], tokens[:, t, j * N:(j + 1) * N], ACT.Square,
                                   accum_out=sq_sum[:, t, j:j + 1]).then_inc(squares, 1)

            def x2_squares_of(j):
                squares_of(x2_squares, j)

            def y_squares_of(j):
                squares_of(uT[:].rearrange("p (t h) s -> p t (h s)", t=T), j)

            def h2_norm():
                normalise(1, None)

            def conv(i, g):
                n = at["group"].plus(-1)
                wait(act, acc_read[n.mod(2)], n.over(2).plus(1))
                wait(act, product, at["ff_gate"])
                for p in range(2):
                    for f in range(2):
                        taps_at = conv_taps(i, g, p, f)
                        ins = act.activation(yconv[:, p, f, :], uT[:, 2 * p + f, :], ACT.Identity,
                                             scale=par[:, bass.ds(taps_at + 2, 1)],
                                             bias=par[:, bass.ds(taps_at + 3, 1)])
                ins.then_inc(tap0, 1)

            def ff_gate(i, g):
                wait(act, taps, at["ff_gate"].plus(1).times(2))
                act.activation(silu_g[:], yconv[:, 0].rearrange("p f s -> p (f s)"), ACT.Silu).then_inc(silu_made, 1)
                wait(act, product, at["ff_gate"].plus(1))
                act.activation(actT_hi[:, bass.ds(i * 4 + 2 * g, 2), :].rearrange("p k s -> p (k s)"), prod[:],
                               ACT.Copy).then_inc(act_hi, 1)

            def load_final_gain():
                wait(act, chunk_used, at["chunk"])
                act.dma_start(gain_row[:], final_gain).then_inc(gain_in, 16)

            def final():
                normalise(2, None)
                act.wait_ge(gained, 4)
                for part in range(2):
                    cols = slice(part * (D // 2), (part + 1) * (D // 2))
                    act.activation(result[:, 0, cols], result[:, 0, cols], ACT.Copy,
                                   scale=rstd[:, 0, 0:1]).then_inc(result_ready[0], 1)

            act.dma_start(freq[:], consts[:, C_FREQ:C_FREQ + 32]).then_inc(freq_in, 16)
            act.dma_start(pos_i[:], positions).then_inc(pos_in, 16)
            act.dma_start(scan_mask[:], consts[:, C_SCAN:C_SCAN + 4 * SEQ].rearrange("p (h s) -> p h s", h=4)
                          ).then_inc(scan_in, 16)
            act.dma_start(causal[:], consts[:, C_CAUSAL:C_CAUSAL + 3 * P]).then_inc(causal_in, 16)
            act.dma_start(lmask[:], level_masks).then_inc(lmask_in, 16)
            walk(act, at, dict(split=split, x_norm=x_norm, operand=operand, tables=tables_step, bounds=bounds,
                               hf_out=hf_out, hq_out=hq_out,
                               log_forget=log_forget, hi_out=hi_out, hg_out=hg_out, decay=decay, mix=mix,
                               mix_norm=mix_norm, gate_out=gate_out, latent=latent_step, key_out=key_out, kpe_turn=kpe_turn,
                               q_out=q_out, k_out=k_out, v_out=v_out, qp_turn=qp_turn, merge=merge,
                               scores=scores, p_turn=p_turn, pv=pv, reload_x=reload_x, x2_out=x2_squares_of,
                               h2_norm=h2_norm, conv=conv, ff_gate=ff_gate, y_out=y_squares_of,
                               load_final_gain=load_final_gain, final=final))

        @block.vector
        def _(dve):
            at = At()

            def acc_here():
                g = at["group"].plus(-1)
                wait(dve, chunk_used, at["chunk"])
                return g.mod(2), g

            def split():
                n = at["split"]
                slot = n.mod(RING)
                wait(dve, hi_made, n.plus(1))
                dve.tensor_tensor(w_lo[:, slot, :], raw[:, slot, :], f32(w_hi[:, slot, :]),
                                  ALU.subtract).then_inc(lo_made, 1)

            def mean(columns, width, count_sem, to=0):
                dve.tensor_scalar(stat[:, :, to], columns, 1.0 / width, EPS, ALU.mult, ALU.add).then_inc(count_sem, 1)

            def normalise(which, to):
                dve.wait_ge(roots, which + 1)
                dve.reciprocal(rstd[:, :, 0], root[:, :, 0]).then_inc(inverses, 1)
                dve.wait_ge(inverses, which + 1)
                if to is not None:
                    dve.tensor_scalar(to[:, 1, :], tokens[:, 1, :], rstd[:, 1, 0:1], None, ALU.mult).then_inc(normed1, 1)

            def x_norm():
                dve.wait_ge(squares, 2)
                mean(sq_sum[:, :, 0], D, means)
                normalise(0, tokens)

            def summed_norm(which, to):
                dve.wait_ge(squares, 2 + 2 * 4 * which)
                dve.tensor_reduce(stat[:, :, 2], sq_sum[:], AX.X, ALU.add).then_inc(sum_own, 1)
                dve.wait_ge(sum_own, which)
                mean(stat[:, :, 2], D, means)
                normalise(which, to)

            def h2_norm():
                dve.memset(ones[:], 1.0)
                summed_norm(1, None)
                for t in range(T):
                    ins = dve.tensor_scalar(factor_diag[:, t, :], ident[:], rstd[:, t, 0:1], None, ALU.mult)
                ins.then_inc(diag_made, 1)

            def row_scale():
                m = at["misc"]
                wait(dve, misc_full, m.plus(1))
                dve.tensor_copy(factor_row[:], misc[:, m.mod(2), 0:SEQ]).then_inc(factors_out, 1)

            def up_out():
                b, _ = acc_here()
                dve.wait_ge(factors_out, 1)
                dve.tensor_tensor(uT[:], acc[:, b].rearrange("p t (h s) -> p (t h) s", s=SEQ),
                                  factor_row[:].unsqueeze(1).to_broadcast([P, 4, SEQ]), ALU.mult
                                  ).then_inc(acc_read[b], 1)

            def merge(j):
                wait(dve, merged_his, Count(j + 1))
                dve.tensor_tensor(merged_lo[:, 4 * j:4 * j + 4, :],
                                  merged[:, j].rearrange("p t (h s) -> p (t h) s", s=SEQ),
                                  f32(merged_hi[:, 4 * j:4 * j + 4, :]), ALU.subtract).then_inc(merged_los, 1)

            def operand(kind, p, i):
                b, u = banks(at)
                s = at["operand"]
                lo = operands[targets[kind]][1]
                hi = operands[targets[kind]][0]
                kt = bass.ds(i * 4 + 2 * p, 2) if kind == "rec" else slice(2 * p, 2 * p + 2)
                wait(dve, turn_full, u.plus(1))
                if kind in gains:
                    g0 = gains[kind] + 2 * p
                    dve.wait_ge(par_in, 16)
                    dve.tensor_tensor(piece[:, s.mod(2), :].rearrange("p (k s) -> p k s", k=2),
                                      turn[:, b, :].rearrange("p (k s) -> p k s", k=2),
                                      par[:, g0:g0 + 2].unsqueeze(2).to_broadcast([P, 2, SEQ]),
                                      ALU.mult).then_inc(turn_read[b], 1)
                else:
                    dve.tensor_copy(piece[:, s.mod(2), :], turn[:, b, :]).then_inc(turn_read[b], 1)
                wait(dve, operand_hi, s.plus(1))
                dve.tensor_tensor(lo[:, kt, :].rearrange("p k s -> p (k s)"), piece[:, s.mod(2), :],
                                  f32(hi[:, kt, :].rearrange("p k s -> p (k s)")), ALU.subtract).then_inc(operand_lo, 1)

            def tables_step():
                count = [0]

                def own(ins):
                    count[0] += 1
                    ins.then_inc(table_own, 1)
                    dve.wait_ge(table_own, count[0])

                two_pi = 2.0 * np.pi
                c1 = 6.28125
                c2 = float(np.float32(np.round((two_pi - c1) * 2.0 ** 20) / 2.0 ** 20))
                c3 = float(two_pi - c1 - c2)
                rounder = 1.5 * 2.0 ** 23
                top = 3.1415925
                dve.wait_ge(pos_in, 16)
                dve.wait_ge(freq_in, 16)
                own(dve.tensor_copy(pos_f[:], pos_i[:]))
                for t in range(T):
                    ins = dve.tensor_scalar(angle[:, 0, t, :], freq[:], pos_f[:, t:t + 1], None, ALU.mult)
                own(ins)
                own(dve.tensor_scalar(angle[:, 1], angle[:, 0], 1.0 / two_pi, rounder, ALU.mult, ALU.add))
                own(dve.tensor_scalar(angle[:, 1], angle[:, 1], -rounder, None, ALU.add))
                for c in (c1, c2, c3):
                    own(dve.scalar_tensor_tensor(out=angle[:, 0], in0=angle[:, 1], scalar=-c, in1=angle[:, 0],
                                                 op0=ALU.mult, op1=ALU.add))
                own(dve.tensor_scalar(angle[:, 2], angle[:, 0], top, -top, ALU.min, ALU.max))
                own(dve.scalar_tensor_tensor(out=angle[:, 1], in0=angle[:, 2], scalar=-1.0, in1=angle[:, 2],
                                             op0=ALU.mult, op1=ALU.max))
                dve.tensor_scalar(angle[:, 3], angle[:, 1], -1.0, float(np.pi / 2), ALU.mult,
                                  ALU.add).then_inc(bounds_exp, 2)

            def bounds():
                dve.wait_ge(par_in, 16)
                logits = par[:, LOGITS:LOGITS + HEADS]
                dve.tensor_tensor(logit[:, 0, :], logits, logits, ALU.subtract).then_inc(bounds_exp, 1)
                dve.wait_ge(bounds_done, 1)
                dve.reciprocal(logit[:, 2, :], logit[:, 1, :]).then_inc(bounds_done, 1)
                dve.wait_ge(bounds_done, 2)
                dve.tensor_tensor(logit[:, 3, :], logit[:, 1, :], logit[:, 2, :], ALU.mult).then_inc(bounds_done, 1)
                dve.wait_ge(bounds_done, 3)
                dve.tensor_tensor(bound[:, 0, :], logit[:, 3, :], logit[:, 3, :], ALU.subtract).then_inc(bounds_done, 1)
                dve.wait_ge(bounds_done, 4)
                dve.tensor_scalar(bound[:, 1, :], bound[:, 0, :], -1.0, 1.0, ALU.mult, ALU.add).then_inc(bounds_done, 1)

            def forget_step(i):
                g = at["group"].plus(-2)
                wait(dve, acc_read[g.mod(2)], g.over(2).plus(1))
                wait(dve, misc_full, at["misc"])
                dve.wait_ge(bounds_done, 5)
                for h in range(4):
                    head = bass.ds(i * 4 + h, 1)
                    ins = dve.tensor_scalar(forget[:, h, :], forget[:, h, :], bound[:, 1, head], bound[:, 0, head],
                                            ALU.mult, ALU.add)
                ins.then_inc(forget_own, 1)
                wait(dve, forget_own, at["forget"].plus(1))
                dve.tensor_scalar(fac[:, 0], forget[:], 1.0 / SPAN, None, ALU.max)
                dve.tensor_scalar(fac[:, 1], forget[:], MIN_FORGET, 1.0 / SPAN, ALU.max, ALU.min)
                dve.tensor_scalar(kk[:], forget[:], -1.0, 1.0, ALU.mult, ALU.add).then_inc(forget_bounded, 1)

            def cumsum():
                wait(dve, logs, at["log_forget"])
                dve.wait_ge(scan_in, 16)
                dve.tensor_tensor(fac[:, 0], fac[:, 0], fac[:, 1], ALU.add).then_inc(cumsum_own, 1)
                wait(dve, cumsum_own, at["cumsum"].plus(1))
                dve.tensor_tensor_scan(bb[:].rearrange("p h s -> p (h s)"), scan_mask[:].rearrange("p h s -> p (h s)"),
                                       fac[:, 0].rearrange("p h s -> p (h s)"), 0.0, ALU.mult,
                                       ALU.add).then_inc(cumsummed, 1)

            def decay(n):
                wait(dve, decay_exp, at["decay"].plus(1))
                f_lo, f_up = halves(fac[:, n % 2], LEVELS[n])
                k_lo, _ = halves(kk[:], LEVELS[n])
                _, q_up = halves(qq[:], LEVELS[n])
                dve.tensor_tensor(f_lo, f_lo, k_lo, ALU.mult)
                dve.tensor_tensor(f_up, f_up, q_up, ALU.mult).then_inc(factors, 1)

            def level(n, p):
                m = at["misc"]
                b = m.mod(2)
                wait(dve, misc_full, m.plus(1))
                heads = slice(2 * p, 2 * p + 2)
                if LEVELS[n] == CHUNK:
                    ins = dve.tensor_copy(scores_T[0:CHUNK, heads, 0:2, CHUNK:P],
                                          misc[0:CHUNK, b, :].rearrange("p (h t s) -> p h t s", h=2, t=2)[:, :, :, CHUNK:P])
                elif n == 0:
                    ins = dve.tensor_copy(scores_T[:, heads, 2, :], misc[:, b, 0:2 * P].rearrange("p (h s) -> p h s", h=2))
                else:
                    dve.memset(spare[:, 2 * n + p:2 * n + p + 1], 0.0)
                    dve.wait_ge(lmask_in, 16)
                    ins = dve.copy_predicated(
                        scores_T[:, heads, 0:2, :],
                        lmask[:, n, :].unsqueeze(1).unsqueeze(1).to_broadcast([P, 2, 2, P]),
                        misc[:, b, :].rearrange("p (h t s) -> p h t s", h=2, t=2))
                ins.then_inc(misc_read[b], 1)

            def mix(t):
                wait(dve, mix_squared, at["mix"].plus(1))
                dve.tensor_reduce(stat[:, t, :], square[:, t, :].rearrange("p (h v) -> p h v", h=4), AX.X,
                                  ALU.add).then_inc(mix_own, 1)

            def mix_norm():
                wait(dve, mix_own, at["mix"])
                dve.tensor_scalar(means4[:], stat[:], 1.0 / P, EPS, ALU.mult, ALU.add).then_inc(mix_mean, 1)
                wait(dve, mix_root, at["mix_norm"].plus(1))
                dve.reciprocal(rstd[:], root[:]).then_inc(mix_own2, 1)
                wait(dve, mix_own2, at["mix_norm"].plus(1))
                m0 = at["misc"].plus(-2)
                for t in range(T):
                    b = m0.plus(t).mod(2)
                    dve.tensor_tensor(rec[:, t, :].rearrange("p (h v) -> p h v", h=4),
                                      misc[:, b, :].rearrange("p (h v) -> p h v", h=4),
                                      rstd[:, t, :].unsqueeze(2).to_broadcast([P, 4, P]),
                                      ALU.mult).then_inc(misc_read[b], 1)
                for t in range(T):
                    c = m0.plus(t)
                    wait(dve, misc_read[c.mod(2)], c.over(2).plus(2))
                wait(dve, gate_scaled, at["hg_out"])
                dve.tensor_tensor(rec[:], rec[:], hgate[:], ALU.mult).then_inc(rec_made, 1)

            def latent_step(w):
                dve.wait_ge(lat_squared, 2 * (w + 1))
                mean(sq_sum[:, :, w], LORA, lat_mean, to=1)
                dve.wait_ge(lat_root, w + 1)
                dve.reciprocal(rstd[:, :, 1], root[:, :, 1]).then_inc(lat_inverse, 1)

            def rotate(out1, out2, src, t, heads):
                v = src.rearrange("p (h r) -> p h r", r=ROPE)
                o1 = out1.rearrange("p (h r) -> p h r", r=ROPE)
                o2 = out2.rearrange("p (h r) -> p h r", r=ROPE)
                half = ROPE // 2
                dve.tensor_tensor(o1, v, cos2[:, t, :].unsqueeze(1).to_broadcast([P, heads, ROPE]), ALU.mult)
                dve.tensor_tensor(o2[:, :, 0:half], v[:, :, half:ROPE],
                                  sin2[:, t, 0:half].unsqueeze(1).to_broadcast([P, heads, half]), ALU.mult)
                return dve.tensor_tensor(o2[:, :, half:ROPE], v[:, :, 0:half],
                                         sin2[:, t, half:ROPE].unsqueeze(1).to_broadcast([P, heads, half]), ALU.mult)

            def kr_turn():
                b, u = banks(at)
                wait(dve, turn_full, u.plus(1))
                dve.wait_ge(sines, 1)
                for t in range(T):
                    ins = rotate(kpe_t1[:, t, :], kpe_t2[:, t, :], turn[:, b, t * ROPE:(t + 1) * ROPE], t, 1)
                ins.then_inc(turn_read[b], 1)
                wait(dve, turn_read[b], u.over(2).plus(1))
                for c in range(2):
                    ins = dve.tensor_tensor(kpe_tok[:, :, c * ROPE:(c + 1) * ROPE], kpe_t1[:], kpe_t2[:], ALU.add)
                ins.then_inc(rope_key, 1)

            def q_rope(j):
                b, g = acc_here()
                for t in range(T):
                    ins = rotate(rope1[:, t, :], rope2[:, t, :], acc[:, b, t, 0:256], t, 4)
                ins.then_inc(acc_read[b], 1)
                wait(dve, acc_read[b], g.over(2).plus(1))
                dve.tensor_tensor(qp_tok[:], rope1[:], rope2[:], ALU.add).then_inc(rope_query, 1)

            def gate_ready(g):
                dve.wait_ge(acc_read[g % 2], g // 2 + 1)

            def branch_b(g, j, gate_group):
                b, _ = acc_here()
                gate_ready(gate_group)
                dve.tensor_tensor(merged[:, j], acc[:, b], gate_b[:, g], ALU.mult
                                  ).then_inc(acc_read[b], 1)

            def branch_a(g, j, gate_group):
                b, n = acc_here()
                gate_ready(gate_group)
                dve.tensor_tensor(gate_a[:, g], acc[:, b], gate_a[:, g], ALU.mult).then_inc(acc_read[b], 1)
                wait(dve, acc_read[b], n.over(2).plus(1))
                dve.tensor_tensor(merged[:, j], merged[:, j], gate_a[:, g], ALU.add).then_inc(merged_made, 1)

            def scores(h):
                m = at["misc"]
                b, r = m.mod(2), h % 2
                wait(dve, misc_full, m.plus(1))
                dve.wait_ge(causal_in, 16)
                dve.scalar_tensor_tensor(out=s_sb[:, r, :], in0=misc[:, b, 0:3 * P], scalar=SCALE, in1=causal[:],
                                         op0=ALU.mult, op1=ALU.add).then_inc(misc_read[b], 1)
                wait(dve, misc_read[b], m.over(2).plus(2))
                dve.tensor_reduce(neg_max[:, r, 0:1], s_sb[:, r, 0:P], AX.X, ALU.max, negate=True)
                dve.tensor_reduce(neg_max[:, r, 1:2], s_sb[:, r, P:3 * P], AX.X, ALU.max,
                                  negate=True).then_inc(maxima, 1)

            def probs_step(h):
                dve.wait_ge(exps, h + 1)
                dve.reciprocal(row_inv[:, h % 2, :], row_sum[:, h % 2, :]).then_inc(inverted, 1)

            def pv(h):
                m = at["misc"]
                b = m.mod(2)
                dve.wait_ge(att_hi, h + 1)
                dve.tensor_tensor(attT_lo[:, h, :], misc[:, b, 0:SEQ], f32(attT_hi[:, h, :]), ALU.subtract
                                  ).then_inc(misc_read[b], 1)

            def x2_out(j):
                b, _ = acc_here()
                dve.wait_ge(x_again_in, 16)
                cols = slice(j * N, (j + 1) * N)
                dve.tensor_tensor(tokens[:, :, cols], acc[:, b], x_again[:, :, cols], ALU.add).then_inc(acc_read[b], 1)

            def y_out(j):
                b, _ = acc_here()
                cols = slice(j * N, (j + 1) * N)
                dve.tensor_tensor(tokens[:, :, cols], acc[:, b], tokens[:, :, cols], ALU.add).then_inc(acc_read[b], 1)
                if j == 3:
                    g = at["group"].k - 1
                    dve.wait_ge(acc_read[b], g // 2 + 1)
                    dve.wait_ge(gain_in, 16)
                    dve.tensor_tensor(result[:, :, cols], tokens[:, :, cols],
                                      gain_row[:, cols].unsqueeze(1).to_broadcast([P, T, N]), ALU.mult
                                      ).then_inc(gained, 1)

            def conv(i, g):
                wait(dve, tap0, at["conv"].plus(1))
                for back in (1, 2):
                    for p in range(2):
                        for f in range(2):
                            w = par[:, bass.ds(conv_taps(i, g, p, f) + 2 - back, 1)]
                            y = yconv[:, p, f, back:SEQ]
                            ins = dve.scalar_tensor_tensor(out=y, in0=uT[:, 2 * p + f, 0:SEQ - back], scalar=w,
                                                           in1=y, op0=ALU.mult, op1=ALU.add)
                    ins.then_inc(taps, 1)
                    if back == 1:
                        wait(dve, taps, at["conv"].times(2).plus(1))

            def ff_gate(i, g):
                wait(dve, silu_made, at["ff_gate"].plus(1))
                dve.tensor_tensor(prod[:], silu_g[:], yconv[:, 1].rearrange("p f s -> p (f s)"),
                                  ALU.mult).then_inc(product, 1)
                wait(dve, act_hi, at["ff_gate"].plus(1))
                kt = bass.ds(i * 4 + 2 * g, 2)
                dve.tensor_tensor(actT_lo[:, kt, :].rearrange("p k s -> p (k s)"), prod[:],
                                  f32(actT_hi[:, kt, :].rearrange("p k s -> p (k s)")),
                                  ALU.subtract).then_inc(act_lo, 1)

            def final():
                summed_norm(2, None)
                dve.wait_ge(gained, 4)
                for part in range(2):
                    cols = slice(part * (D // 2), (part + 1) * (D // 2))
                    dve.tensor_scalar(result[:, 1, cols], result[:, 1, cols], rstd[:, 1, 0:1], None,
                                      ALU.mult).then_inc(result_ready[1], 1)

            dve.memset(scores_T[:, 0:2], 0.0).then_inc(misc_read[0], 1)
            dve.memset(scores_T[:, 2:4], 0.0).then_inc(misc_read[1], 1)
            walk(dve, at, dict(split=split, x_norm=x_norm, operand=operand, tables=tables_step, bounds=bounds,
                               forget=forget_step, cumsum=cumsum, decay=decay, level=level, mix=mix,
                               mix_norm=mix_norm, latent=latent_step, kr_turn=kr_turn, q_rope=q_rope,
                               branch_b=branch_b, branch_a=branch_a, scores=scores, probs=probs_step, pv=pv,
                               merge=merge, x2_out=x2_out, h2_norm=h2_norm, row_scale=row_scale, up_out=up_out, conv=conv, ff_gate=ff_gate, y_out=y_out,
                               final=final))

        @block.gpsimd
        def _(pool):
            at = At()

            def hg_out():
                g = at["group"].plus(-1)
                wait(pool, acc_read[g.mod(2)], g.over(2).plus(1))
                v = hgate[:].rearrange("p t (h v) -> p (t h) v", h=4)
                pool.tensor_tensor(v, v, par[:, G_HGRN:G_HGRN + P].unsqueeze(1).to_broadcast([P, 4 * T, P]),
                                   ALU.mult).then_inc(gate_scaled, 1)

            def decay(n):
                h, f = LEVELS[n], fac[:, n % 2]
                wait(pool, cumsummed, at["cumsum"])
                if n >= 2:
                    wait(pool, misc_full, at["misc"].plus(-2))
                if h == 2 * CHUNK:
                    b4 = bb[:].rearrange("p h (c s) -> p h c s", s=CHUNK)
                    f4 = f.rearrange("p h (c s) -> p h c s", s=CHUNK)
                    end = b4[:, :, :, CHUNK - 1:CHUNK]
                    pool.tensor_tensor(sums01[:].unsqueeze(2), end[:, :, 0, :], end[:, :, 1, :],
                                       ALU.add).then_inc(pool_own, 1)
                    pool.tensor_tensor(f4[:, :, 1, :], end[:, :, 1, :].to_broadcast([P, 4, CHUNK]), b4[:, :, 1, :],
                                       ALU.subtract)
                    pool.tensor_copy(f4[:, :, 2, :], b4[:, :, 2, :])
                    pool.tensor_tensor(f4[:, :, 3, :], b4[:, :, 3, :], end[:, :, 2, :].to_broadcast([P, 4, CHUNK]),
                                       ALU.add)
                    wait(pool, pool_own, at["cumsum"])
                    pool.tensor_tensor(f4[:, :, 0, :], sums01[:].unsqueeze(2).to_broadcast([P, 4, CHUNK]),
                                       b4[:, :, 0, :], ALU.subtract).then_inc(decay_diff, 1)
                    return
                f_lo, f_up = halves(f, h)
                b_lo, b_up = halves(bb[:], h)
                blocks = 4 * SEQ // (2 * h)
                end = b_lo[:, :, h - 1:h].to_broadcast([P, blocks, h])
                pool.tensor_tensor(f_lo, end, b_lo, ALU.subtract)
                (pool.tensor_copy(f_up, b_up) if h == CHUNK else
                 pool.tensor_tensor(f_up, b_up, end, ALU.subtract)).then_inc(decay_diff, 1)

            def probs_step(h):
                r = h % 2
                pool.wait_ge(inverted, h + 1)
                pool.tensor_scalar(probs[:, r, 0:P], probs[:, r, 0:P], row_inv[:, r, 0:1], None, ALU.mult)
                pool.tensor_scalar(probs[:, r, P:3 * P], probs[:, r, P:3 * P], row_inv[:, r, 1:2], None,
                                   ALU.mult).then_inc(probs_made, 1)

            def y_out(j):
                if j < 3:
                    g = at["group"].k - 1
                    cols = slice(j * N, (j + 1) * N)
                    pool.wait_ge(acc_read[g % 2], g // 2 + 1)
                    pool.wait_ge(gain_in, 16)
                    pool.tensor_tensor(result[:, :, cols], tokens[:, :, cols],
                                       gain_row[:, cols].unsqueeze(1).to_broadcast([P, T, N]), ALU.mult
                                       ).then_inc(gained, 1)

            walk(pool, at, dict(hg_out=hg_out, decay=decay, probs=probs_step, y_out=y_out))


def conv_taps(i, g, p, f):
    return i * (2 * 16) + (CONV + 16 * g + 8 * p + 4 * f)


def shape_constants():
    c = np.zeros((P, N_CONST), np.float32)
    c[:, C_IDENT:C_IDENT + P] = np.eye(P)
    triangle = np.where(np.arange(P)[None, :] <= np.arange(P)[:, None], 0.0, MASKED)
    c[:, C_CAUSAL:C_CAUSAL + P] = triangle
    c[:, C_CAUSAL + 2 * P:C_CAUSAL + 3 * P] = triangle
    c[:, C_SCAN:C_SCAN + 4 * SEQ] = (np.arange(4 * SEQ) % CHUNK != 0)
    c[:, C_FREQ:] = np.float32(10000.0) ** (-np.arange(0, ROPE, 2, dtype=np.float32) / np.float32(ROPE))
    masks = np.zeros((P, len(LEVELS), P), np.int32)
    s, t = np.arange(P)[:, None], np.arange(P)[None, :]
    for n, h in enumerate(LEVELS):
        if h == 0:
            masks[:, n] = s == t
        elif h < P:
            masks[:, n] = (s // (2 * h) == t // (2 * h)) & (s // h % 2 == 0) & (t // h % 2 == 1)
    return c, masks


def kernel(**inputs):
    import concourse.bacc as bacc
    from concourse.bass_utils import run_bass_kernel_spmd

    a = {k: np.asarray(v) for k, v in inputs.items()}
    w_in, w_uq, w_ukv = a["w_in"][0], a["w_uq"][0], a["w_ukv"][0]
    w_a, w_b, w_out, w_up, w_down = (a[k][0] for k in ("w_branch_a", "w_branch_b", "w_out", "w_up", "w_down"))
    stream = np.empty((N_CHUNKS, P, CH), np.float32)
    n = 0

    def pack(w, k_tiles=2):
        nonlocal n
        count = w.shape[0] // (k_tiles * P)
        stream[n:n + count] = w.reshape(count, k_tiles, P, w.shape[1]).transpose(0, 2, 1, 3).reshape(count, P, CH)
        n += count

    o = np.concatenate([[0], np.cumsum([LORA, LORA, ROPE, D, D, D, D, D, D])])
    c_q, c_kv, k_rope, hq, hf, hi, hg, gate_a, gate_b = (w_in[:, o[k]:o[k + 1]] for k in range(9))

    def block(w, j):
        return w[:, j * N:(j + 1) * N]

    for j in range(QUADS):
        for w in (hf, hq, hi, hg):
            pack(block(w, j))
    pack(block(gate_b, 0))
    pack(block(gate_b, 1))
    pack(c_q)
    pack(c_kv)
    pack(k_rope, KT)
    pack(block(w_b, 0))
    pack(block(w_b, 1))
    for w in (gate_b, w_b):
        pack(block(w, 2))
        pack(block(w, 3))
    uq = w_uq.reshape(LORA, HEADS, NOPE + ROPE)
    ukv = w_ukv.reshape(LORA, HEADS, 2, 128)
    for j in range(QUADS):
        heads = slice(4 * j, 4 * j + 4)
        pack(uq[:, heads, :NOPE].reshape(LORA, N))
        pack(uq[:, heads, NOPE:].reshape(LORA, 256), 4)
        pack(ukv[:, heads, 0].reshape(LORA, N))
        pack(ukv[:, heads, 1].reshape(LORA, N))
    for first in (0, 2):
        for w in (gate_a, w_a):
            pack(block(w, first))
            pack(block(w, first + 1))
    for j in range(4):
        pack(block(w_out, j))
    up = w_up.reshape(D, 2, FF_GROUPS, 256)
    for g in range(FF_GROUPS):
        pack(up[:, :, g].reshape(D, N))
    for j in range(4):
        pack(block(w_down, j))
    assert n == N_CHUNKS

    def along_partitions(v):
        return v.reshape(-1, P).T

    taps = np.concatenate([a["conv_w"][0], a["conv_b"]], 0)
    taps = taps.reshape(4, 2, FF_GROUPS, 2, P).transpose(4, 2, 1, 3, 0).reshape(P, -1)
    params = np.concatenate([along_partitions(a[k][0]) for k in ("attn_norm_g", "q_norm_g", "kv_norm_g", "ffn_norm_g",
                                                                   "hgrn_lb_logits")]
                            + [np.broadcast_to(a["hgrn_out_norm_g"][0], (P, P)), taps], 1)
    constants, masks = shape_constants()
    arrays = {
        "weights": stream,
        "x": a["x"][0],
        "params": params,
        "consts": constants,
        "level_masks": masks,
        "positions": a["positions"][0].reshape(T, P).T,
        "final_gain": np.broadcast_to(a["final_norm_g"], (P, D)),
    }
    arrays = {k: np.ascontiguousarray(v) for k, v in arrays.items()}
    nc = bacc.Bacc("TRN2", target_bir_lowering=False, num_devices=1)
    aps = {k: nc.dram_tensor(k, v.shape, mybir.dt.from_np(v.dtype), kind="ExternalInput").ap()
           for k, v in arrays.items()}
    out = nc.dram_tensor("out", (SEQ, D), F32, kind="ExternalOutput").ap()
    build(nc, out=out, **aps)
    result = run_bass_kernel_spmd(nc, [arrays], core_ids=[0])
    return result.results[0]["out"].reshape(1, SEQ, D)
```

```python
from contextlib import ExitStack

import numpy as np

import concourse.bass as bass
from concourse import mybir

F32 = mybir.dt.float32
F32R = mybir.dt.float32r
I32 = mybir.dt.int32
ALU = mybir.AluOpType
ACT = mybir.ActivationFunctionType
AX = mybir.AxisListType

P = 128
SEQ = 256
T = SEQ // P
D = 2048
KT = D // P
HEADS = D // 128
NOPE, ROPE = 128, 64
LORA = 512
D_FF = 5632
N = 512
EPS = 1e-6
MIN_FORGET = 1e-30
SCALE = float(NOPE + ROPE) ** -0.5
MASKED = -1e30
CHUNK = 64
LEVELS = (128, 64, 32, 16, 8, 4, 2, 1)
SPAN = float(2.0 ** 60)

X_SHARE = D * 5 // 8
H_FIRST = 2
WARM_UP = 8
RING = 4
CH = 2 * N
QUADS = HEADS // 4
GROUP_CHUNKS = KT // 2
FF_GROUPS = D_FF // 256
FF_KT = D_FF // P
UP_PAIRS = FF_GROUPS // 2
DOWN_CHUNKS = FF_KT // 2
N_CHUNKS = (4 * QUADS * GROUP_CHUNKS + 4 * 4 * GROUP_CHUNKS + 2 * GROUP_CHUNKS + 1 + 7 * QUADS
            + 4 * GROUP_CHUNKS + FF_GROUPS * GROUP_CHUNKS + 4 * DOWN_CHUNKS)

GROUP_GB = 4 * QUADS
GROUP_CQ = GROUP_GB + 2
GROUP_Q0 = GROUP_CQ + 3 + 6
GROUP_GA = GROUP_Q0 + 4 * QUADS
GROUP_OUT = GROUP_GA + 8

G_ATTN, G_Q, G_KV, G_FFN, LOGITS, G_HGRN, CONV = 0, 16, 20, 24, 40, 56, 184
N_PARAMS = CONV + 4 * 4 * FF_GROUPS
C_IDENT, C_CAUSAL, C_SCAN, C_FREQ = 0, 128, 512, 1536
N_CONST = C_FREQ + 32


class Count:

    def __init__(self, k, per=0, i=None, first=0):
        self.k, self.per, self.i, self.first = k, per, i, first

    def plus(self, n):
        return Count(self.k + n, self.per, self.i, self.first)

    def over(self, m):
        assert self.per % m == 0
        return Count(self.k // m, self.per // m, self.i, self.first)

    def mod(self, m):
        assert self.per % m == 0
        return self.k % m

    def times(self, m):
        return Count(self.k * m, self.per * m, self.i, self.first)

    def least(self):
        return self.k + self.per * self.first

    def value(self):
        return self.i * self.per + self.k if self.per else self.k


def wait(eng, sem, count):
    if count.least() <= 0:
        assert count.per == 0 or count.i is None, "a wait that may be void inside a loop"
        return
    eng.wait_ge(sem, count.value())


FAMILIES = {
    "trans": ("row_scale", "operand", "kr_turn", "kpe_turn", "qp_turn", "p_turn"),
    "misc": ("level", "mix", "scores", "pv"),
}


def names_of(step):
    name, args = step[0], step[1:]
    out = [name] + [f for f, members in FAMILIES.items() if name in members]
    if name == "chunk" and args[-1]:
        out.append("group")
    return out


def chunks(src, n, after=None, form="tokens", columns=N, nk=2):
    for k in range(n):
        first, last = k == 0, k == n - 1
        yield ("chunk", src, k * nk, nk, columns, 0 if first else None, form, first, last)
        yield from (after or {}).get(k, ())
        yield ("split",)


def hgrn_new(i):
    return {
        7: [("hf_out",)],
        17: [("hq_out", 2), ("forget", i)],
        19: [("log_forget",)],
        21: [("cumsum",)],
        23: [("hi_out",)],
        31: [("hg_out",)],
    }


def hgrn_old(i):
    table = {0: [("diff", 0)], 4: [("gate_scale",)]}
    for n in range(len(LEVELS)):
        if n:
            table.setdefault(2 * n - 1, []).append(("diff", n))
        table.setdefault(2 * n, []).append(("decay", n))
        table.setdefault(2 * n + 1, []).append(("factors", n))
        table.setdefault(2 * n + 2, []).extend([("level", n, 0), ("level", n, 1)])
    table.setdefault(18, []).extend([("mix", 0), ("mix", 1)])
    table.setdefault(20, []).append(("mix_norm",))
    table.setdefault(24, []).extend([("operand", "rec", 0, i), ("operand", "rec", 1, i)])
    return table


def together(*tables):
    out = {}
    for table in tables:
        for k, steps in table.items():
            out.setdefault(k, []).extend(steps)
    return out


def pick(table, start, n=GROUP_CHUNKS):
    return {k - start: s for k, s in table.items() if start <= k < start + n}


def hgrn_section(i, old):
    table = together(hgrn_old(i - 1), hgrn_new(i)) if old else hgrn_new(i)
    if not old:
        yield from [("x_norm",), ("split",), ("row_scale", 0), ("row_scale", 1), ("h_make", 0), ("h_make", 1),
                    ("h_lo", 0), ("split",), ("h_gain", 2), ("h_lo", 1), ("h_gain", 3), ("split",), ("h_make", 2),
                    ("split",), ("h_gain", 4)]
        table = together(table, {6: [("bounds",)], 26: [("tables",)]})
    for g in range(4):
        mine = pick(table, g * GROUP_CHUNKS)
        form = "features" if g < 2 else "tokens"
        if not old and g == 0:
            ahead = {k: [(name, k + more) for name, more in (("h_make", 3), ("h_gain", 5), ("h_lo", 2))
                         if k + more < GROUP_CHUNKS] for k in range(GROUP_CHUNKS)}
            lags = {c: min(1, GROUP_CHUNKS - 1 - c) for c in range(GROUP_CHUNKS)}
            yield from with_lags(chunks("first h", GROUP_CHUNKS, together(ahead, mine), form), lags)
        else:
            yield from chunks("h", GROUP_CHUNKS, mine, form)


def with_lags(steps, lags):
    for s in steps:
        if s[0] == "chunk":
            s = (*s[:5], lags.get(s[2] // 2), *s[6:])
        yield s


def branch_b_first():
    table = together(hgrn_old(QUADS - 1), {
        7: [("gate_out", 0, "b")],
        15: [("gate_out", 1, "b")],
        23: [("latent", 0)],
        26: [("operand", "cq", 0, 0), ("operand", "cq", 1, 0)],
        31: [("latent", 1)],
    })
    for g in range(4):
        form = "features" if g < 2 else "tokens"
        yield from chunks("h", GROUP_CHUNKS, pick(table, g * GROUP_CHUNKS), form)
    yield from chunks("h", 1, {0: [("key_out",)]}, "features", columns=ROPE, nk=KT)
    yield from chunks("rec", GROUP_CHUNKS, {
        0: [("kr_turn",)],
        2: [("kpe_turn",)],
        3: [("operand", "ckv", 0, 0), ("operand", "ckv", 1, 0)],
        7: [("branch_b", 0, 0, GROUP_GB)]}, "features")
    yield from chunks("rec", GROUP_CHUNKS, {7: [("branch_b", 1, 1, GROUP_GB + 1)]}, "features")


def branch_b_second():
    for g in range(2):
        yield from chunks("h", GROUP_CHUNKS, {7: [("gate_out", g, "b")]}, "features")
    for g in range(2):
        yield from chunks("rec", GROUP_CHUNKS, {7: [("branch_b", g, 2 + g, GROUP_GB + 7 + g)]}, "features")


FIRST_HEAD = 7


def heads_at(slot):
    for back, name in ((5, "pv"), (3, "p_turn"), (1, "probs"), (0, "scores")):
        h = slot - back - FIRST_HEAD
        if h >= 0 and h % 2 == 0 and h // 2 < HEADS:
            yield (name, h // 2)


def attention_section():
    for j in range(QUADS):
        s = 7 * j
        yield from chunks("cq", 2, {0: list(heads_at(s)), 1: [*heads_at(s + 1), ("q_out", j)]}, "features")
        yield from chunks("cq", 1, {0: [*heads_at(s + 2), ("q_rope", j)]}, columns=256, nk=4)
        yield from chunks("ckv", 2, {
            0: [*heads_at(s + 3)],
            1: [*heads_at(s + 4), ("k_out", j), ("qp_turn", j)]}, "features")
        yield from chunks("ckv", 2, {
            0: [*heads_at(s + 5)],
            1: [*heads_at(s + 6), ("v_out", j)]})


def branch_a(first):
    slot = 7 * QUADS
    for g in range(2):
        table = {k: list(heads_at(slot + g * GROUP_CHUNKS + k)) if first else [] for k in range(GROUP_CHUNKS)}
        table[7].append(("gate_out", g, "a"))
        if not first:
            table[3].append(("merge", g))
        yield from chunks("h", GROUP_CHUNKS, table, "features")
        if not first and g == 0:
            yield ("reload_x",)
    for g in range(2):
        j = g if first else 2 + g
        table = {7: [("branch_a", g, j, GROUP_GA + (0 if first else 4) + g)]}
        if not first and g == 1:
            table[2] = [("merge", 2)]
        yield from chunks("att", GROUP_CHUNKS, table, "features")


def out_section():
    yield ("merge", 3)
    for j in range(4):
        table = {7: [("x2_out", j)]}
        if j > 0:
            table |= {k: [("operand", "h2", 2 * j - 2 + k // 2, 0)] for k in (1, 3)}
        lags = {0: 3, 2: 2, 4: 1, 6: 0} if j == 0 else {}
        yield from with_lags(chunks("merged", GROUP_CHUNKS, table), lags)


def up_first():
    table = {0: [("h2_norm",)], 1: [("operand", "h2", 6, 0)], 2: [("operand", "h2", 7, 0)],
             4: [("row_scale", 0), ("row_scale", 1)], 7: [("up_out",)]}
    yield from with_lags(chunks("h2", GROUP_CHUNKS, table, "features"), {0: 0, 6: 0})
    yield from chunks("h2", GROUP_CHUNKS, {
        1: [("conv", 0, 0)], 3: [("ff_gate", 0, 0)], 7: [("up_out",)]}, "features")


def up_section(i):
    for g in range(2):
        yield from chunks("h2", GROUP_CHUNKS, {
            1: [("conv", i, g - 1)], 3: [("ff_gate", i, g - 1)], 7: [("up_out",)]}, "features")


def down_section():
    last = FF_GROUPS - 1
    for j in range(4):
        table = {DOWN_CHUNKS - 1: [("y_out", j)]}
        if j == 0:
            table |= {1: [("conv", 0, last)], 3: [("ff_gate", 0, last)],
                      6: [("load_final_gain",)]}
        steps = list(chunks("act", DOWN_CHUNKS, table))
        if j == 0:
            steps = [(*s[:5], 0, *s[6:]) if s[0] == "chunk" and s[2] == FF_KT - 2 else s for s in steps]
        if j == 3:
            ends = [k for k, s in enumerate(steps) if s[0] == "split"][-RING:]
            steps = [s for k, s in enumerate(steps) if k not in ends]
        yield from steps
    yield ("final",)


SECTIONS = (
    (lambda i: hgrn_section(0, False), None, None),
    (lambda i: hgrn_section(i, True), 1, QUADS),
    (lambda i: branch_b_first(), None, None),
    (lambda i: branch_b_second(), None, None),
    (lambda i: attention_section(), None, None),
    (lambda i: branch_a(True), None, None),
    (lambda i: branch_a(False), None, None),
    (lambda i: out_section(), None, None),
    (lambda i: up_first(), None, None),
    (lambda i: up_section(i), 1, UP_PAIRS),
    (lambda i: down_section(), None, None),
)


class At:

    def __init__(self):
        self.done, self.rate, self.i, self.first = {}, {}, None, 0

    def __getitem__(self, name):
        per = self.rate.get(name, 0) if self.i is not None else 0
        return Count(self.done.get(name, 0) - per * self.first, per, self.i if per else None, self.first)

    def passed(self, step):
        for name in names_of(step):
            self.done[name] = self.done.get(name, 0) + 1


def walk(eng, at, do):
    for make, first, end in SECTIONS:
        if first is None:
            for step in make(None):
                if step[0] in do:
                    do[step[0]](*step[1:])
                at.passed(step)
            continue
        rate = {}
        for step in make(0):
            for name in names_of(step):
                rate[name] = rate.get(name, 0) + 1
        if not any(step[0] in do for step in make(0)):
            for name, n in rate.items():
                at.done[name] = at.done.get(name, 0) + n * (end - first)
            continue
        before = dict(at.done)
        with eng.Fori(first, end) as i:
            at.rate, at.i, at.first = rate, i, first
            for step in make(i):
                if step[0] in do:
                    do[step[0]](*step[1:])
                at.passed(step)
        at.rate, at.i, at.first = {}, None, 0
        at.done = {n: before.get(n, 0) + rate.get(n, 0) * (end - first) for n in {*before, *rate}}


def build(nc, weights, x, x_turned, params, consts, level_masks, positions, final_gain, out):
    with ExitStack() as ctx:
        def sem(name):
            return ctx.enter_context(nc.semaphore(name))

        arena_bytes = 212480
        base = -(-nc.sbuf_base // 32) * 32
        ctx.enter_context(nc.sbuf_tensor("arena", [P, arena_bytes // 4], F32))
        assert nc.sbuf_base >= base + arena_bytes

        def place(name, offset, shape, dtype=F32):
            offset = -(-offset // 32) * 32
            size = int(np.prod(shape)) * 4
            assert offset + size <= arena_bytes, (name, offset + size)
            return nc.alloc_sbuf_tensor_at(name, [P, *shape], dtype, offset=base + offset), offset + size

        o = 0
        raw, o = place("raw", o, [RING, CH])
        w_hi, o = place("w_hi", o, [RING, CH], F32R)
        w_lo, o = place("w_lo", o, [RING, CH], F32R)
        hT_hi, o = place("hT_hi", o, [KT, SEQ], F32R)
        hT_lo, o = place("hT_lo", o, [KT, SEQ], F32R)
        merged, _ = place("merged", o, [4, T, N])
        xT, _ = place("xT", o, [KT, SEQ])
        tokens, o = place("tokens", o, [T, D])
        piece, o = place("piece", o, [2, N])
        par, o = place("par", o, [N_PARAMS])
        ident, o = place("ident", o, [P])
        factor_diag, _ = place("factor_diag", o, [T, P])
        causal, o = place("causal", o, [3 * P])
        factor_row, _ = place("factor_row", o, [SEQ])
        cos2, o = place("cos2", o, [T, ROPE])
        sin2, o = place("sin2", o, [T, ROPE])
        ones, _ = place("ones", o, [P])
        kpeT, o = place("kpeT", o, [SEQ])
        sq_sum, o = place("sq_sum", o, [T, 4])
        stat, o = place("stat", o, [T, 4])
        root, o = place("root", o, [T, 4])
        rstd, o = place("rstd", o, [T, 4])
        bound, o = place("bound", o, [2, HEADS])
        pos_f, o = place("pos_f", o, [T])
        spare, o = place("spare", o, [2 * len(LEVELS)])
        shared = o

        recT_hi, o = place("recT_hi", shared, [KT, SEQ], F32R)
        recT_lo, o = place("recT_lo", o, [KT, SEQ], F32R)
        latents = o
        kk, o = place("kk", o, [4, SEQ])
        qq, o = place("qq", o, [4, SEQ])
        bb, o = place("bb", o, [4, SEQ])
        fac, o = place("fac", o, [2, 4, SEQ])
        rest = o
        forget, o = place("forget", o, [4, SEQ])
        krT, o = place("krT", o, [SEQ])
        kpe_tok, o = place("kpe_tok", o, [T, P])
        kpe_t1, o = place("kpe_t1", o, [T, ROPE])
        kpe_t2, o = place("kpe_t2", o, [T, ROPE])
        scores_T, o = place("scores_T", o, [4, 3, P])
        x_rows, _ = place("x_rows", o, [T, D])
        hv, o = place("hv", o, [T, N])
        hgate, o = place("hgate", o, [T, N])
        rec, o = place("rec", o, [T, N])
        square, o = place("square", o, [T, N])
        scan_mask, o = place("scan_mask", o, [4, SEQ])
        lmask, o = place("lmask", o, [len(LEVELS), P], I32)
        sums01, o = place("sums01", o, [4])
        gate_b_at = o
        gate_b, o = place("gate_b", o, [2, T, N])
        means4, o = place("means4", o, [T, 4])

        cqT_hi, o = place("cqT_hi", latents, [4, SEQ], F32R)
        cqT_lo, o = place("cqT_lo", o, [4, SEQ], F32R)
        ckvT_hi, o = place("ckvT_hi", o, [4, SEQ], F32R)
        ckvT_lo, o = place("ckvT_lo", o, [4, SEQ], F32R)
        assert o <= rest
        latent, _ = place("latent", rest, [T, N])
        gate_a, _ = place("gate_a", latents, [2, T, N])
        angle, o = place("angle", gate_b_at, [4, T, 32])
        freq, o = place("freq", o, [32])
        logit, o = place("logit", o, [4, HEADS])
        pos_i, _ = place("pos_i", o, [T], I32)

        attT_hi, o = place("attT_hi", shared, [KT, SEQ], F32R)
        attT_lo, o = place("attT_lo", o, [KT, SEQ], F32R)
        qp_tok, o = place("qp_tok", latents + 16384, [T, 256])
        rope1, o = place("rope1", o, [T, 256])
        rope2, o = place("rope2", o, [T, 256])
        qT, o = place("qT", o, [2, 4, SEQ])
        kT, o = place("kT", o, [2, 4, SEQ])
        s_sb, o = place("s_sb", o, [2, 3 * P])
        probs, o = place("probs", o, [2, 3 * P])
        probsT, o = place("probsT", o, [2, 3 * P])
        neg_max, o = place("neg_max", o, [2, T])
        row_sum, o = place("row_sum", o, [2, T])
        row_inv, o = place("row_inv", o, [2, T])
        qpT, o = place("qpT", o, [2, 2, SEQ])
        vv, o = place("vv", o, [2, T, N])

        x_again, o = place("x_again", latents + 16384, [T, D])
        merged_hi, o = place("merged_hi", o, [KT, SEQ], F32R)
        merged_lo, o = place("merged_lo", o, [KT, SEQ], F32R)
        x2_squares, _ = place("x2_squares", shared, [T, N])

        actT_hi, o = place("actT_hi", shared, [FF_KT, SEQ], F32R)
        actT_lo, o = place("actT_lo", o, [FF_KT, SEQ], F32R)
        uT, o = place("uT", o, [4, SEQ])
        yconv, o = place("yconv", o, [2, 2, SEQ])
        silu_g, o = place("silu_g", o, [2 * SEQ])
        prod, o = place("prod", o, [2 * SEQ])
        gain_row, o = place("gain_row", 3 * RING * CH * 4, [D])
        result, _ = place("result", o, [T, D])

        acc = ctx.enter_context(nc.psum_tensor("acc", [P, 2, T, N], F32))
        turn = ctx.enter_context(nc.psum_tensor("turn", [P, 2, N], F32))
        misc = ctx.enter_context(nc.psum_tensor("misc", [P, 2, N], F32))

        raw_in = [sem(f"raw_in{s}") for s in range(RING)]
        hi_made, lo_made, chunk_used = sem("hi_made"), sem("lo_made"), sem("chunk_used")
        acc_read = [sem("acc_read0"), sem("acc_read1")]
        turn_full, misc_full = sem("turn_full"), sem("misc_full")
        turn_read = [sem("turn_read0"), sem("turn_read1")]
        misc_read = [sem("misc_read0"), sem("misc_read1")]
        operand_hi, operand_lo = sem("operand_hi"), sem("operand_lo")
        x_in = [sem("x_in0"), sem("x_in1")]
        par_in, const_in, scan_in, lmask_in = sem("par_in"), sem("const_in"), sem("scan_in"), sem("lmask_in")
        causal_in, freq_in, pos_in = sem("causal_in"), sem("freq_in"), sem("pos_in")
        x_again_in, gain_in, stored = sem("x_again_in"), sem("gain_in"), sem("stored")
        squares, means, roots = sem("squares"), sem("means"), sem("roots")
        xT_in = [sem(f"xT_in{c}") for c in range(4)]
        h_first = sem("h_first")
        h_gained, h_scaled, h_his, h_los = sem("h_gained"), sem("h_scaled"), sem("h_his"), sem("h_los")
        inverses = sem("inverses")
        angles, bounds_exp, bounds_done, sines = sem("angles"), sem("bounds_exp"), sem("bounds_done"), sem("sines")
        forget_bounded, logs, cumsummed = sem("forget_bounded"), sem("logs"), sem("cumsummed")
        decay_diff, decay_exp, factors = sem("decay_diff"), sem("decay_exp"), sem("factors")
        gate_scaled, mix_squared, mix_mean, mix_root, rec_made = (
            sem("gate_scaled"), sem("mix_squared"), sem("mix_mean"), sem("mix_root"), sem("rec_made"))
        lat_squared, lat_mean, lat_root, lat_inverse = (
            sem("lat_squared"), sem("lat_mean"), sem("lat_root"), sem("lat_inverse"))
        rope_key, maxima, exps, inverted, probs_made, att_hi = (
            sem("rope_key"), sem("maxima"), sem("exps"), sem("inverted"), sem("probs_made"), sem("att_hi"))
        rope_query = sem("rope_query")
        diag_made = sem("diag_made")
        tap0, taps, silu_made, product, act_hi, act_lo = (
            sem("tap0"), sem("taps"), sem("silu_made"), sem("product"), sem("act_hi"), sem("act_lo"))
        pool_own = sem("pool_own")
        sum_own, table_own, forget_own, cumsum_own, mix_own, mix_own2 = (
            sem("sum_own"), sem("table_own"), sem("forget_own"), sem("cumsum_own"), sem("mix_own"), sem("mix_own2"))
        merged_made, merged_his, merged_los = sem("merged_made"), sem("merged_his"), sem("merged_los")
        gained, warm, x_own = sem("gained"), sem("warm"), sem("x_own")
        y_rows = sem("y_rows")
        result_ready = [sem("result_ready0"), sem("result_ready1")]

        operands = {"h": (hT_hi, hT_lo), "rec": (recT_hi, recT_lo), "cq": (cqT_hi, cqT_lo),
                    "ckv": (ckvT_hi, ckvT_lo), "att": (attT_hi, attT_lo), "merged": (merged_hi, merged_lo),
                    "first h": (hT_hi, hT_lo), "h2": (hT_hi, hT_lo),
                    "act": (actT_hi, actT_lo)}
        rows_of = {"h2": tokens, "rec": rec, "cq": latent, "ckv": latent}
        gains = {"h2": G_FFN, "cq": G_Q, "ckv": G_KV}

        def f32(ap):
            return ap.bitcast(F32)

        def banks(at):
            u = at["trans"]
            return u.mod(2), u

        def halves(ap, h):
            v = ap.rearrange("p a s -> p (a s)").rearrange("p (m two h) -> p m two h", two=2, h=h)
            return v[:, :, 0, :], v[:, :, 1, :]

        block = ctx.enter_context(nc.Block())

        @block.sync
        def _(sp):
            def load(slot, n):
                sp.dma_start(raw[:, slot, :], weights[bass.ds(n, 1), :, :].rearrange("a p c -> p (a c)")
                             ).then_inc(raw_in[slot], 16)

            def load_turned(c):
                sp.dma_start(xT[:, 4 * c:4 * c + 4, :], x_turned[:, 4 * c:4 * c + 4, :]).then_inc(xT_in[c], 16)

            for t in range(T):
                sp.dma_start(x_rows[:, t, :], x[t * P:(t + 1) * P, :]).then_inc(x_in[t], 16)
            sp.dma_start(ident[:], consts[:, C_IDENT:C_IDENT + P]).then_inc(const_in, 16)
            load(0, 0)
            sp.dma_start(par[:], params).then_inc(par_in, 16)
            load_turned(0)
            load(1, 1)
            load_turned(1)
            load(2, 2)
            load_turned(2)
            load(3, 3)
            load_turned(3)
            sp.dma_start(freq[:], consts[:, C_FREQ:C_FREQ + 32]).then_inc(freq_in, 16)
            sp.dma_start(pos_i[:], positions).then_inc(pos_in, 16)

            with sp.Fori(1, N_CHUNKS // RING) as r:
                for s in range(RING):
                    sp.wait_ge(lo_made, r * RING + (s + 1 - RING))
                    load(s, r * RING + s)
            for n in range(N_CHUNKS // RING * RING, N_CHUNKS):
                sp.wait_ge(lo_made, n + 1 - RING)
                load(n % RING, n)
            for part in range(4):
                for t in (1, 0):
                    sp.wait_ge(result_ready[t], part + 1)
                    cols = slice(part * N, (part + 1) * N)
                    sp.dma_start(out[t * P:(t + 1) * P, cols], result[:, t, cols]).then_inc(stored, 16)
            sp.wait_ge(stored, 16 * 4 * T)

        @block.tensor
        def _(pe):
            at = At()
            p_bank = {}

            def chunk(src, k0, nk, columns, lag, form, first, last):
                n, g = at["chunk"], at["group"]
                slot, b = n.mod(RING), g.mod(2)
                hi, lo = operands[src]
                wh = w_hi[:, slot, 0:nk * columns].rearrange("p (k c) -> p k c", c=columns)
                wl = w_lo[:, slot, 0:nk * columns].rearrange("p (k c) -> p k c", c=columns)
                wait(pe, lo_made, n.plus(1))
                if first:
                    wait(pe, acc_read[b], g.over(2))
                    if src == "att":
                        for m in range(2):
                            wait(pe, misc_read[m], at["misc"].plus(1 - m).over(2).plus(1))
                if lag is not None:
                    if src == "act":
                        wait(pe, act_lo, at["ff_gate"])
                    elif src == "first h":
                        wait(pe, h_los, at["h_lo"].plus(-lag))
                    elif src == "h":
                        pass
                    elif src == "merged":
                        wait(pe, merged_los, at["merge"].plus(-lag))
                    else:
                        wait(pe, operand_lo, at["operand"].plus(-lag))
                for k in range(nk if form == "features" else 0):
                    for c in range(0, columns, P):
                        width = min(P, columns - c)
                        half, at_col = c // (2 * P), c % (2 * P) // P * SEQ
                        to = acc[0:width, b, half, at_col:at_col + SEQ]
                        begin = first and k == 0 and at_col == 0
                        end = last and k == nk - 1 and (at_col > 0 or columns <= P)
                        w_h, w_l = wh[:, k, c:c + width], wl[:, k, c:c + width]
                        pe.matmul(to, w_h, hi[:, k0 + k, :], start=begin, stop=False)
                        pe.matmul(to, w_h, lo[:, k0 + k, :], start=False, stop=False)
                        ins = pe.matmul(to, w_l, hi[:, k0 + k, :], start=False, stop=end)
                for k in range(nk if form == "tokens" else 0):
                    for t in range(T):
                        x_h = hi[:, k0 + k, t * P:(t + 1) * P]
                        x_l = lo[:, k0 + k, t * P:(t + 1) * P]
                        to = acc[:, b, t, 0:columns]
                        begin, end = first and k == 0, last and k == nk - 1
                        pe.matmul(to, x_h, wh[:, k, :], start=begin, stop=False)
                        pe.matmul(to, x_h, wl[:, k, :], start=False, stop=False)
                        ins = pe.matmul(to, x_l, wh[:, k, :], start=False, stop=end)
                ins.then_inc(chunk_used, 1)

            def turn_bank():
                b, u = banks(at)
                wait(pe, turn_read[b], u.over(2))
                return b

            def turns(b, pieces):
                for q, (src, rows) in enumerate(pieces):
                    ins = pe.transpose(turn[0:rows, b, q * P:(q + 1) * P], src, ident[:])
                ins.then_inc(turn_full, 1)

            def operand(kind, p, i):
                b = turn_bank()
                if kind == "h2":
                    g = GROUP_OUT + p // 2
                    pe.wait_ge(acc_read[g % 2], g // 2 + 1)
                elif kind == "rec":
                    wait(pe, rec_made, at["mix_norm"])
                elif kind in ("cq", "ckv"):
                    g = GROUP_CQ if kind == "cq" else GROUP_CQ + 1
                    pe.wait_ge(acc_read[g % 2], g // 2 + 1)
                rows = rows_of[kind]
                turns(b, [(rows[:, t, (2 * p + k) * P:(2 * p + k + 1) * P], P) for k in range(2) for t in range(T)])

            def kr_turn():
                b = turn_bank()
                g = at["group"].plus(-1)
                wait(pe, acc_read[g.mod(2)], g.over(2).plus(1))
                for t in range(T):
                    ins = pe.transpose(turn[:, b, t * ROPE:(t + 1) * ROPE], krT[0:ROPE, t * P:(t + 1) * P],
                                       ident[0:ROPE, 0:ROPE])
                ins.then_inc(turn_full, 1)

            def kpe_turn():
                b = turn_bank()
                pe.wait_ge(rope_key, 1)
                turns(b, [(kpe_tok[:, t, :], P) for t in range(T)])

            def level(n, p):
                m = at["misc"]
                b, h, f = m.mod(2), LEVELS[n], fac[:, n % 2]
                wait(pe, misc_read[b], m.over(2).plus(1))
                wait(pe, factors, at["factors"])
                for a in range(2):
                    head = 2 * p + a
                    if h == 2 * CHUNK:
                        ins = pe.matmul(misc[:, b, a * P:(a + 1) * P], f[:, head, 0:P], f[:, head, P:2 * P],
                                        start=True, stop=True)
                        continue
                    for t in range(T):
                        cols, q = slice(t * P, (t + 1) * P), 2 * a + t
                        keys, queries = (f, f) if h > 1 else (kk, qq)
                        if h == CHUNK:
                            ins = pe.matmul(misc[0:h, b, q * P + h:(q + 1) * P], keys[:, head, t * P:t * P + h],
                                            queries[:, head, t * P + h:(t + 1) * P], start=True, stop=True)
                            continue
                        ins = pe.matmul(misc[:, b, q * P:(q + 1) * P], keys[:, head, cols], queries[:, head, cols],
                                        start=True, stop=True)
                ins.then_inc(misc_full, 1)

            def mix(t):
                m = at["misc"]
                b = m.mod(2)
                wait(pe, misc_read[b], m.over(2).plus(1))
                if t == 0:
                    wait(pe, misc_read[1 - b], m.plus(1 - (1 - b)).over(2).plus(1))
                for h in range(4):
                    to = misc[:, b, h * P:(h + 1) * P]
                    cols = slice(h * P, (h + 1) * P)
                    if t == 0:
                        ins = pe.matmul(to, scores_T[:, h, 0, :], hv[:, 0, cols], start=True, stop=True)
                    else:
                        pe.matmul(to, scores_T[:, h, 2, :], hv[:, 0, cols], start=True, stop=False)
                        ins = pe.matmul(to, scores_T[:, h, 1, :], hv[:, 1, cols], start=False, stop=True)
                ins.then_inc(misc_full, 1)

            def q_group(j):
                return Count(GROUP_Q0 + 4 * j)

            def qp_turn(j):
                b = turn_bank()
                pe.wait_ge(rope_query, j + 1)
                turns(b, [(qp_tok[:, t, a * P:(a + 1) * P], P) for a in range(2) for t in range(T)])

            def scores(h):
                m = at["misc"]
                b, j, a = m.mod(2), h // 4, h % 4
                wait(pe, misc_read[b], m.over(2).plus(1))
                if a == 0:
                    for r in range(2):
                        wait(pe, turn_read[r], at["trans"].plus(1 - r).over(2))
                    for g in (q_group(j).plus(2), q_group(j).plus(3)):
                        wait(pe, acc_read[g.mod(2)], g.over(2).plus(1))
                half = slice((a % 2) * ROPE, (a % 2 + 1) * ROPE)
                for t in range(T):
                    to = misc[:, b, 0:P] if t == 0 else misc[:, b, P:3 * P]
                    keys = (t + 1) * P
                    pe.matmul(to, qT[:, j % 2, a, t * P:(t + 1) * P], kT[:, j % 2, a, 0:keys], start=True, stop=False)
                    ins = pe.matmul(to, qpT[half, j % 2, a // 2, t * P:(t + 1) * P], kpeT[half, 0:keys],
                                    start=False, stop=True)
                ins.then_inc(misc_full, 1)

            def p_turn(h):
                b = turn_bank()
                pe.wait_ge(probs_made, h + 1)
                p_bank[h] = at["trans"].k
                turns(b, [(probs[:, h % 2, q * P:(q + 1) * P], P) for q in range(3)])

            def pv(h):
                m = at["misc"]
                b, j, a = m.mod(2), h // 4, h % 4
                wait(pe, misc_read[b], m.over(2).plus(1))
                u = p_bank[h]
                wait(pe, turn_read[u % 2], Count(u // 2 + 1))
                cols = slice(a * P, (a + 1) * P)
                pe.matmul(misc[:, b, 0:P], vv[:, j % 2, 0, cols], probsT[:, h % 2, 0:P], start=True, stop=True)
                pe.matmul(misc[:, b, P:2 * P], vv[:, j % 2, 0, cols], probsT[:, h % 2, P:2 * P], start=True, stop=False)
                pe.matmul(misc[:, b, P:2 * P], vv[:, j % 2, 1, cols], probsT[:, h % 2, 2 * P:3 * P],
                          start=False, stop=True).then_inc(misc_full, 1)

            def row_scale(t):
                b = turn_bank()
                u = at["row_scale"].k
                wait(pe, diag_made, at["row_scale"].over(2).plus(1))
                pe.wait_ge(const_in, 16)
                pe.matmul(turn[:, b, 0:P], ones[:], factor_diag[:, t, :], start=True, stop=True).then_inc(turn_full, 1)
                if u == 1:
                    pe.wait_ge(misc_read[0], 1)
                    for _ in range(WARM_UP):
                        pe.matmul(misc[:, 0, 0:P], ones[:], ones[:], start=True, stop=True)

            walk(pe, at, dict(chunk=chunk, operand=operand, kr_turn=kr_turn, kpe_turn=kpe_turn,
                              level=level, mix=mix, qp_turn=qp_turn, scores=scores, p_turn=p_turn, pv=pv,
                              row_scale=row_scale))

        @block.scalar
        def _(act):
            at = At()

            def from_acc(out_ap, func, extra=(), since=0):
                g = at["group"].plus(-1)
                wait(act, chunk_used, at["chunk"].plus(-since))
                for s, count in extra:
                    wait(act, s, count)
                act.activation(out_ap, acc[:, g.mod(2)], func).then_inc(acc_read[g.mod(2)], 1)

            def heads_rows(ap):
                return ap.rearrange("p (t h) s -> p t (h s)", t=T)

            def from_turn(out_ap, func, columns=N):
                b, u = banks(at)
                wait(act, turn_full, u.plus(1))
                act.activation(out_ap, turn[:, b, 0:columns], func).then_inc(turn_read[b], 1)

            def split():
                n = at["split"]
                slot = n.mod(RING)
                wait(act, raw_in[slot], n.over(RING).plus(1).times(16))
                wait(act, chunk_used, n.plus(1 - RING))
                act.activation(w_hi[:, slot, :], raw[:, slot, :], ACT.Copy).then_inc(hi_made, 1)

            def x_norm():
                for t, width in ((0, D), (1, X_SHARE)):
                    act.wait_ge(x_in[t], 16)
                    act.activation(x_rows[:, t, 0:width], x_rows[:, t, 0:width], ACT.Square,
                                   accum_out=sq_sum[:, t, 0:1]).then_inc(squares, 1)
                norm_root(0)

            def h_gain(p):
                act.wait_ge(xT_in[p // 2], 16)
                act.wait_ge(par_in, 16)
                for k in range(2 * p, 2 * p + 2):
                    ins = act.activation(xT[:, k, :], xT[:, k, :], ACT.Copy, scale=par[:, G_ATTN + k:G_ATTN + k + 1])
                ins.then_inc(h_gained, 1)

            def h_make(p):
                if p < H_FIRST:
                    act.wait_ge(h_first, p + 1)
                else:
                    act.wait_ge(h_scaled, p + 1 - H_FIRST)
                act.activation(hT_hi[:, 2 * p:2 * p + 2, :], xT[:, 2 * p:2 * p + 2, :], ACT.Copy).then_inc(h_his, 1)

            def norm_root(which):
                act.wait_ge(means, which + 1)
                act.activation(root[:, :, 0], stat[:, :, 0], ACT.Sqrt).then_inc(roots, 1)

            def operand(kind, p, i):
                b, u = banks(at)
                s = at["operand"]
                hi = operands[kind][0]
                kt = bass.ds(i * 4 + 2 * p, 2) if kind == "rec" else slice(2 * p, 2 * p + 2)
                wait(act, turn_read[b], u.over(2).plus(1))
                act.activation(hi[:, kt, :].rearrange("p k s -> p (k s)"), piece[:, s.mod(2), :],
                               ACT.Copy).then_inc(operand_hi, 1)

            def tables_step():
                act.wait_ge(turn_full, 2)
                act.dma_start(causal[:], consts[:, C_CAUSAL:C_CAUSAL + 3 * P]).then_inc(causal_in, 16)
                act.wait_ge(angles, 1)
                act.activation(sin2[:, :, 0:32], angle[:, 2], ACT.Sin, scale=-1.0)
                act.activation(sin2[:, :, 32:64], angle[:, 2], ACT.Sin)
                act.activation(cos2[:, :, 0:32], angle[:, 3], ACT.Sin)
                act.activation(cos2[:, :, 32:64], angle[:, 3], ACT.Sin).then_inc(sines, 1)

            def bounds():
                act.dma_start(scan_mask[:], consts[:, C_SCAN:C_SCAN + 4 * SEQ].rearrange("p (h s) -> p h s", h=4)
                              ).then_inc(scan_in, 16)
                act.dma_start(lmask[:], level_masks).then_inc(lmask_in, 16)
                act.wait_ge(bounds_exp, 1)
                act.activation(logit[:, 1, :], logit[:, 0, :], ACT.Exp).then_inc(bounds_done, 1)

            def hf_out():
                from_acc(heads_rows(forget[:]), ACT.Sigmoid)

            def hq_out(since):
                from_acc(heads_rows(qq[:]), ACT.Silu, [(misc_full, at["misc"])], since)

            def log_forget():
                wait(act, forget_bounded, at["forget"])
                act.activation(fac[:, 0], fac[:, 0], ACT.Ln)
                act.activation(fac[:, 1], fac[:, 1], ACT.Ln, scale=SPAN).then_inc(logs, 1)

            def hi_out():
                from_acc(hv[:], ACT.Copy)

            def hg_out():
                from_acc(hgate[:], ACT.Silu, [(rec_made, at["mix_norm"])])

            def decay(n):
                wait(act, decay_diff, at["decay"].plus(1))
                act.activation(fac[:, n % 2], fac[:, n % 2], ACT.Exp).then_inc(decay_exp, 1)

            def mix(t):
                m = at["misc"]
                wait(act, misc_full, m.plus(1))
                act.activation(square[:, t, :], misc[:, m.mod(2), :], ACT.Square).then_inc(mix_squared, 1)

            def mix_norm():
                wait(act, mix_mean, at["mix_norm"].plus(1))
                act.activation(root[:], means4[:], ACT.Sqrt).then_inc(mix_root, 1)

            def gate_out(g, which):
                if which == "a":
                    from_acc(gate_a[:, g], ACT.Sigmoid, [(merged_made, at["branch_a"])])
                else:
                    from_acc(gate_b[:, g], ACT.Sigmoid)

            def latent_step(w):
                g = at["group"].k - 1
                b = g % 2
                wait(act, chunk_used, at["chunk"])
                for t in range(T):
                    act.activation(square[:, t, :], acc[:, b, t, :], ACT.Square,
                                   accum_out=sq_sum[:, t, w:w + 1]).then_inc(lat_squared, 1)
                act.wait_ge(lat_mean, w + 1)
                act.activation(root[:, :, 1], stat[:, :, 1], ACT.Sqrt).then_inc(lat_root, 1)
                act.wait_ge(lat_inverse, w + 1)
                wait(act, turn_full, at["trans"])
                act.activation(latent[:, 0, :], acc[:, b, 0, :], ACT.Copy, scale=rstd[:, 0, 1:2])
                act.activation(latent[:, 1, :], acc[:, b, 1, :], ACT.Copy,
                               scale=rstd[:, 1, 1:2]).then_inc(acc_read[b], 1)

            def key_out():
                g = at["group"].plus(-1)
                wait(act, chunk_used, at["chunk"])
                act.activation(krT[0:ROPE, :], acc[0:ROPE, g.mod(2), 0, 0:SEQ], ACT.Copy).then_inc(acc_read[g.mod(2)], 1)

            def kpe_turn():
                from_turn(kpeT[:], ACT.Copy, SEQ)

            def q_out(j):
                from_acc(heads_rows(qT[:, j % 2]), ACT.Copy, [(misc_full, at["misc"])])

            def k_out(j):
                from_acc(heads_rows(kT[:, j % 2]), ACT.Copy, [(misc_full, at["misc"])])

            def v_out(j):
                from_acc(vv[:, j % 2], ACT.Copy, [(misc_full, at["misc"])])

            def qp_turn(j):
                from_turn(qpT[:, j % 2].rearrange("p h s -> p (h s)"), ACT.Copy)

            def scores(h):
                r = h % 2
                act.wait_ge(maxima, h + 1)
                act.activation(probs[:, r, 0:P], s_sb[:, r, 0:P], ACT.Exp, bias=neg_max[:, r, 0:1],
                               accum_out=row_sum[:, r, 0:1])
                act.activation(probs[:, r, P:3 * P], s_sb[:, r, P:3 * P], ACT.Exp, bias=neg_max[:, r, 1:2],
                               accum_out=row_sum[:, r, 1:2]).then_inc(exps, 1)

            def p_turn(h):
                from_turn(probsT[:, h % 2, :], ACT.Copy, 3 * P)

            def pv(h):
                m = at["misc"]
                wait(act, misc_full, m.plus(1))
                act.activation(attT_hi[:, h, :], misc[:, m.mod(2), 0:SEQ], ACT.Copy).then_inc(att_hi, 1)

            def reload_x():
                wait(act, chunk_used, at["chunk"])
                wait(act, merged_made, at["branch_a"])
                act.dma_start(x_again[:], x.rearrange("(t p) d -> p t d", p=P)).then_inc(x_again_in, 16)

            def merge(j):
                wait(act, chunk_used, at["chunk"].plus(-2))
                wait(act, merged_made, Count(j + 1))
                act.activation(merged_hi[:, 4 * j:4 * j + 4, :], merged[:, j].rearrange("p t (h s) -> p (t h) s", s=SEQ),
                               ACT.Copy).then_inc(merged_his, 1)

            def squares_of(junk_rows, j, y_last=False):
                g = at["group"].k - 1
                last = y_last and j == 3
                if not last:
                    act.wait_ge(acc_read[g % 2], g // 2 + 1)
                for t in range(T):
                    if last:
                        act.wait_ge(y_rows, t + 1)
                    act.activation(junk_rows[:, t, :], tokens[:, t, j * N:(j + 1) * N], ACT.Square,
                                   accum_out=sq_sum[:, t, j:j + 1]).then_inc(squares, 1)

            def x2_squares_of(j):
                squares_of(x2_squares, j)

            def y_squares_of(j):
                squares_of(uT[:].rearrange("p (t h) s -> p t (h s)", t=T), j, y_last=True)
                if j == 2:
                    act.activation(root[:, 0, 0:1], root[:, 0, 1:2], ACT.Sqrt)

            def h2_norm():
                norm_root(1)

            def conv(i, g):
                n = at["group"].plus(-1)
                wait(act, acc_read[n.mod(2)], n.over(2).plus(1))
                wait(act, product, at["ff_gate"])
                for p in range(2):
                    for f in range(2):
                        taps_at = conv_taps(i, g, p, f)
                        ins = act.activation(yconv[:, p, f, :], uT[:, 2 * p + f, :], ACT.Identity,
                                             scale=par[:, bass.ds(taps_at + 2, 1)],
                                             bias=par[:, bass.ds(taps_at + 3, 1)])
                ins.then_inc(tap0, 1)

            def ff_gate(i, g):
                wait(act, taps, at["ff_gate"].plus(1).times(2))
                act.activation(silu_g[:], yconv[:, 0].rearrange("p f s -> p (f s)"), ACT.Silu).then_inc(silu_made, 1)
                wait(act, product, at["ff_gate"].plus(1))
                act.activation(actT_hi[:, bass.ds(i * 4 + 2 * g, 2), :].rearrange("p k s -> p (k s)"), prod[:],
                               ACT.Copy).then_inc(act_hi, 1)

            def load_final_gain():
                wait(act, chunk_used, at["chunk"])
                act.dma_start(gain_row[:], final_gain).then_inc(gain_in, 16)

            def final():
                norm_root(2)
                act.wait_ge(inverses, 3)
                act.wait_ge(gained, 5)
                for part in range(4):
                    cols = slice(part * N, (part + 1) * N)
                    act.activation(result[:, 0, cols], result[:, 0, cols], ACT.Copy,
                                   scale=rstd[:, 0, 0:1]).then_inc(result_ready[0], 1)

            act.wait_ge(warm, 1)
            act.activation(root[:, 0, 0:1], root[:, 0, 1:2], ACT.Sqrt)
            walk(act, at, dict(split=split, x_norm=x_norm, h_gain=h_gain, h_make=h_make, operand=operand,
                               tables=tables_step, bounds=bounds, hf_out=hf_out, hq_out=hq_out,
                               log_forget=log_forget, hi_out=hi_out, hg_out=hg_out, decay=decay, mix=mix,
                               mix_norm=mix_norm, gate_out=gate_out, latent=latent_step, key_out=key_out, kpe_turn=kpe_turn,
                               q_out=q_out, k_out=k_out, v_out=v_out, qp_turn=qp_turn, merge=merge,
                               scores=scores, p_turn=p_turn, pv=pv, reload_x=reload_x, x2_out=x2_squares_of,
                               h2_norm=h2_norm, conv=conv, ff_gate=ff_gate, y_out=y_squares_of,
                               load_final_gain=load_final_gain, final=final))

        @block.vector
        def _(dve):
            at = At()
            factors_read = [None] * T

            def acc_here():
                g = at["group"].plus(-1)
                wait(dve, chunk_used, at["chunk"])
                return g.mod(2), g

            def split():
                n = at["split"]
                slot = n.mod(RING)
                wait(dve, hi_made, n.plus(1))
                dve.tensor_tensor(w_lo[:, slot, :], raw[:, slot, :], f32(w_hi[:, slot, :]),
                                  ALU.subtract).then_inc(lo_made, 1)

            def mean(columns, width, count_sem, to=0):
                dve.tensor_scalar(stat[:, :, to], columns, 1.0 / width, EPS, ALU.mult, ALU.add).then_inc(count_sem, 1)

            def norm_inverse(which):
                dve.wait_ge(roots, which + 1)
                dve.reciprocal(rstd[:, :, 0], root[:, :, 0]).then_inc(inverses, 1)
                dve.wait_ge(inverses, which + 1)

            def x_norm():
                dve.wait_ge(x_in[1], 16)
                right = x_rows[:, 1, X_SHARE:D]
                dve.tensor_tensor(right, right, right, ALU.mult).then_inc(x_own, 1)
                dve.wait_ge(x_own, 1)
                dve.tensor_reduce(sq_sum[:, 1, 1:2], right, AX.X, ALU.add).then_inc(x_own, 1)
                dve.wait_ge(squares, 2)
                dve.wait_ge(x_own, 2)
                dve.tensor_tensor(sq_sum[:, 1, 0:1], sq_sum[:, 1, 0:1], sq_sum[:, 1, 1:2], ALU.add).then_inc(x_own, 1)
                dve.wait_ge(x_own, 3)
                mean(sq_sum[:, :, 0], D, means)
                norm_inverse(0)
                dve.wait_ge(const_in, 16)
                factors_on_diagonal()

            def factors_on_diagonal():
                for t in range(T):
                    ins = dve.tensor_scalar(factor_diag[:, t, :], ident[:], rstd[:, t, 0:1], None, ALU.mult)
                ins.then_inc(diag_made, 1)

            def h_make(p):
                if p < H_FIRST:
                    for s, count in factors_read:
                        wait(dve, s, count)
                    dve.wait_ge(par_in, 16)
                    dve.wait_ge(xT_in[p // 2], 16)
                    for k in range(2 * p, 2 * p + 2):
                        ins = dve.scalar_tensor_tensor(out=xT[:, k, :], in0=xT[:, k, :],
                                                       scalar=par[:, G_ATTN + k:G_ATTN + k + 1], in1=factor_row[:],
                                                       op0=ALU.mult, op1=ALU.mult)
                    ins.then_inc(h_first, 1)

            def h_lo(p):
                dve.wait_ge(h_his, p + 1)
                dve.tensor_tensor(hT_lo[:, 2 * p:2 * p + 2, :], xT[:, 2 * p:2 * p + 2, :],
                                  f32(hT_hi[:, 2 * p:2 * p + 2, :]), ALU.subtract).then_inc(h_los, 1)

            def summed_norm(which):
                dve.wait_ge(squares, 2 + 2 * 4 * which)
                dve.tensor_reduce(stat[:, :, 2], sq_sum[:], AX.X, ALU.add).then_inc(sum_own, 1)
                dve.wait_ge(sum_own, which)
                mean(stat[:, :, 2], D, means)
                norm_inverse(which)

            def h2_norm():
                dve.memset(ones[:], 1.0)
                summed_norm(1)
                factors_on_diagonal()

            def row_scale(t):
                b, u = banks(at)
                wait(dve, turn_full, u.plus(1))
                dve.tensor_copy(factor_row[:, t * P:(t + 1) * P], turn[:, b, 0:P]).then_inc(turn_read[b], 1)
                factors_read[t] = (turn_read[b], u.over(2).plus(1))

            def up_out():
                b, _ = acc_here()
                for s, count in factors_read:
                    wait(dve, s, count)
                dve.tensor_tensor(uT[:], acc[:, b].rearrange("p t (h s) -> p (t h) s", s=SEQ),
                                  factor_row[:].unsqueeze(1).to_broadcast([P, 4, SEQ]), ALU.mult
                                  ).then_inc(acc_read[b], 1)

            def merge(j):
                wait(dve, merged_his, Count(j + 1))
                dve.tensor_tensor(merged_lo[:, 4 * j:4 * j + 4, :],
                                  merged[:, j].rearrange("p t (h s) -> p (t h) s", s=SEQ),
                                  f32(merged_hi[:, 4 * j:4 * j + 4, :]), ALU.subtract).then_inc(merged_los, 1)

            def operand(kind, p, i):
                b, u = banks(at)
                s = at["operand"]
                lo = operands[kind][1]
                hi = operands[kind][0]
                kt = bass.ds(i * 4 + 2 * p, 2) if kind == "rec" else slice(2 * p, 2 * p + 2)
                wait(dve, turn_full, u.plus(1))
                if kind in gains:
                    g0 = gains[kind] + 2 * p
                    dve.wait_ge(par_in, 16)
                    dve.tensor_tensor(piece[:, s.mod(2), :].rearrange("p (k s) -> p k s", k=2),
                                      turn[:, b, :].rearrange("p (k s) -> p k s", k=2),
                                      par[:, g0:g0 + 2].unsqueeze(2).to_broadcast([P, 2, SEQ]),
                                      ALU.mult).then_inc(turn_read[b], 1)
                else:
                    dve.tensor_copy(piece[:, s.mod(2), :], turn[:, b, :]).then_inc(turn_read[b], 1)
                wait(dve, operand_hi, s.plus(1))
                dve.tensor_tensor(lo[:, kt, :].rearrange("p k s -> p (k s)"), piece[:, s.mod(2), :],
                                  f32(hi[:, kt, :].rearrange("p k s -> p (k s)")), ALU.subtract).then_inc(operand_lo, 1)

            def tables_step():
                count = [0]

                def own(ins):
                    count[0] += 1
                    ins.then_inc(table_own, 1)
                    dve.wait_ge(table_own, count[0])

                two_pi = 2.0 * np.pi
                c1 = 6.28125
                c2 = float(np.float32(np.round((two_pi - c1) * 2.0 ** 20) / 2.0 ** 20))
                c3 = float(two_pi - c1 - c2)
                rounder = 1.5 * 2.0 ** 23
                top = 3.1415925
                dve.wait_ge(pos_in, 16)
                dve.wait_ge(freq_in, 16)
                own(dve.tensor_copy(pos_f[:], pos_i[:]))
                for t in range(T):
                    ins = dve.tensor_scalar(angle[:, 0, t, :], freq[:], pos_f[:, t:t + 1], None, ALU.mult)
                own(ins)
                own(dve.tensor_scalar(angle[:, 1], angle[:, 0], 1.0 / two_pi, rounder, ALU.mult, ALU.add))
                own(dve.tensor_scalar(angle[:, 1], angle[:, 1], -rounder, None, ALU.add))
                for c in (c1, c2, c3):
                    own(dve.scalar_tensor_tensor(out=angle[:, 0], in0=angle[:, 1], scalar=-c, in1=angle[:, 0],
                                                 op0=ALU.mult, op1=ALU.add))
                own(dve.tensor_scalar(angle[:, 2], angle[:, 0], top, -top, ALU.min, ALU.max))
                own(dve.scalar_tensor_tensor(out=angle[:, 1], in0=angle[:, 2], scalar=-1.0, in1=angle[:, 2],
                                             op0=ALU.mult, op1=ALU.max))
                dve.tensor_scalar(angle[:, 3], angle[:, 1], -1.0, float(np.pi / 2), ALU.mult,
                                  ALU.add).then_inc(angles, 1)

            def bounds():
                dve.wait_ge(par_in, 16)
                logits = par[:, LOGITS:LOGITS + HEADS]
                dve.tensor_tensor(logit[:, 0, :], logits, logits, ALU.subtract).then_inc(bounds_exp, 1)
                dve.wait_ge(bounds_done, 1)
                dve.reciprocal(logit[:, 2, :], logit[:, 1, :]).then_inc(bounds_done, 1)
                dve.wait_ge(bounds_done, 2)
                dve.tensor_tensor(logit[:, 3, :], logit[:, 1, :], logit[:, 2, :], ALU.mult).then_inc(bounds_done, 1)
                dve.wait_ge(bounds_done, 3)
                dve.tensor_tensor(bound[:, 0, :], logit[:, 3, :], logit[:, 3, :], ALU.subtract).then_inc(bounds_done, 1)
                dve.wait_ge(bounds_done, 4)
                dve.tensor_scalar(bound[:, 1, :], bound[:, 0, :], -1.0, 1.0, ALU.mult, ALU.add).then_inc(bounds_done, 1)

            def forget_step(i):
                g = at["group"].plus(-2)
                wait(dve, acc_read[g.mod(2)], g.over(2).plus(1))
                wait(dve, misc_full, at["misc"])
                dve.wait_ge(bounds_done, 5)
                for h in range(4):
                    head = bass.ds(i * 4 + h, 1)
                    ins = dve.tensor_scalar(forget[:, h, :], forget[:, h, :], bound[:, 1, head], bound[:, 0, head],
                                            ALU.mult, ALU.add)
                ins.then_inc(forget_own, 1)
                wait(dve, forget_own, at["forget"].plus(1))
                dve.tensor_scalar(fac[:, 0], forget[:], 1.0 / SPAN, None, ALU.max)
                dve.tensor_scalar(fac[:, 1], forget[:], MIN_FORGET, 1.0 / SPAN, ALU.max, ALU.min)
                dve.tensor_scalar(kk[:], forget[:], -1.0, 1.0, ALU.mult, ALU.add).then_inc(forget_bounded, 1)

            def cumsum():
                wait(dve, logs, at["log_forget"])
                dve.wait_ge(scan_in, 16)
                dve.tensor_tensor(fac[:, 0], fac[:, 0], fac[:, 1], ALU.add).then_inc(cumsum_own, 1)
                wait(dve, cumsum_own, at["cumsum"].plus(1))
                dve.tensor_tensor_scan(bb[:].rearrange("p h s -> p (h s)"), scan_mask[:].rearrange("p h s -> p (h s)"),
                                       fac[:, 0].rearrange("p h s -> p (h s)"), 0.0, ALU.mult,
                                       ALU.add).then_inc(cumsummed, 1)

            def factors_step(n):
                wait(dve, decay_exp, at["factors"].plus(1))
                f_lo, f_up = halves(fac[:, n % 2], LEVELS[n])
                k_lo, k_up = halves(kk[:], LEVELS[n])
                _, q_up = halves(qq[:], LEVELS[n])
                if LEVELS[n] == 1:
                    dve.tensor_tensor(k_up, k_up, f_lo, ALU.mult)
                    dve.tensor_tensor(q_up, q_up, f_up, ALU.mult).then_inc(factors, 1)
                    return
                dve.tensor_tensor(f_lo, f_lo, k_lo, ALU.mult)
                dve.tensor_tensor(f_up, f_up, q_up, ALU.mult).then_inc(factors, 1)

            def level(n, p):
                m = at["misc"]
                b = m.mod(2)
                wait(dve, misc_full, m.plus(1))
                heads = slice(2 * p, 2 * p + 2)
                if LEVELS[n] == CHUNK:
                    ins = dve.tensor_copy(scores_T[0:CHUNK, heads, 0:2, CHUNK:P],
                                          misc[0:CHUNK, b, :].rearrange("p (h t s) -> p h t s", h=2, t=2)[:, :, :, CHUNK:P])
                elif n == 0:
                    ins = dve.tensor_copy(scores_T[:, heads, 2, :], misc[:, b, 0:2 * P].rearrange("p (h s) -> p h s", h=2))
                else:
                    dve.memset(spare[:, 2 * n + p:2 * n + p + 1], 0.0)
                    dve.wait_ge(lmask_in, 16)
                    ins = dve.copy_predicated(
                        scores_T[:, heads, 0:2, :],
                        lmask[:, n, :].unsqueeze(1).unsqueeze(1).to_broadcast([P, 2, 2, P]),
                        misc[:, b, :].rearrange("p (h t s) -> p h t s", h=2, t=2))
                ins.then_inc(misc_read[b], 1)

            def mix(t):
                wait(dve, mix_squared, at["mix"].plus(1))
                dve.tensor_reduce(stat[:, t, :], square[:, t, :].rearrange("p (h v) -> p h v", h=4), AX.X,
                                  ALU.add).then_inc(mix_own, 1)

            def mix_norm():
                wait(dve, mix_own, at["mix"])
                dve.tensor_scalar(means4[:], stat[:], 1.0 / P, EPS, ALU.mult, ALU.add).then_inc(mix_mean, 1)
                wait(dve, mix_root, at["mix_norm"].plus(1))
                dve.reciprocal(rstd[:], root[:]).then_inc(mix_own2, 1)
                wait(dve, mix_own2, at["mix_norm"].plus(1))
                m0 = at["misc"].plus(-2)
                for t in range(T):
                    b = m0.plus(t).mod(2)
                    dve.tensor_tensor(rec[:, t, :].rearrange("p (h v) -> p h v", h=4),
                                      misc[:, b, :].rearrange("p (h v) -> p h v", h=4),
                                      rstd[:, t, :].unsqueeze(2).to_broadcast([P, 4, P]),
                                      ALU.mult).then_inc(misc_read[b], 1)
                for t in range(T):
                    c = m0.plus(t)
                    wait(dve, misc_read[c.mod(2)], c.over(2).plus(2))
                wait(dve, gate_scaled, at["gate_scale"])
                dve.tensor_tensor(rec[:], rec[:], hgate[:], ALU.mult).then_inc(rec_made, 1)

            def latent_step(w):
                dve.wait_ge(lat_squared, 2 * (w + 1))
                mean(sq_sum[:, :, w], LORA, lat_mean, to=1)
                dve.wait_ge(lat_root, w + 1)
                dve.reciprocal(rstd[:, :, 1], root[:, :, 1]).then_inc(lat_inverse, 1)

            def rotate(out1, out2, src, t, heads):
                v = src.rearrange("p (h r) -> p h r", r=ROPE)
                o1 = out1.rearrange("p (h r) -> p h r", r=ROPE)
                o2 = out2.rearrange("p (h r) -> p h r", r=ROPE)
                half = ROPE // 2
                dve.tensor_tensor(o1, v, cos2[:, t, :].unsqueeze(1).to_broadcast([P, heads, ROPE]), ALU.mult)
                dve.tensor_tensor(o2[:, :, 0:half], v[:, :, half:ROPE],
                                  sin2[:, t, 0:half].unsqueeze(1).to_broadcast([P, heads, half]), ALU.mult)
                return dve.tensor_tensor(o2[:, :, half:ROPE], v[:, :, 0:half],
                                         sin2[:, t, half:ROPE].unsqueeze(1).to_broadcast([P, heads, half]), ALU.mult)

            def kr_turn():
                b, u = banks(at)
                wait(dve, turn_full, u.plus(1))
                dve.wait_ge(sines, 1)
                for t in range(T):
                    ins = rotate(kpe_t1[:, t, :], kpe_t2[:, t, :], turn[:, b, t * ROPE:(t + 1) * ROPE], t, 1)
                ins.then_inc(turn_read[b], 1)
                wait(dve, turn_read[b], u.over(2).plus(1))
                for c in range(2):
                    ins = dve.tensor_tensor(kpe_tok[:, :, c * ROPE:(c + 1) * ROPE], kpe_t1[:], kpe_t2[:], ALU.add)
                ins.then_inc(rope_key, 1)

            def q_rope(j):
                b, g = acc_here()
                for t in range(T):
                    ins = rotate(rope1[:, t, :], rope2[:, t, :], acc[:, b, t, 0:256], t, 4)
                ins.then_inc(acc_read[b], 1)
                wait(dve, acc_read[b], g.over(2).plus(1))
                dve.tensor_tensor(qp_tok[:], rope1[:], rope2[:], ALU.add).then_inc(rope_query, 1)

            def gate_ready(g):
                dve.wait_ge(acc_read[g % 2], g // 2 + 1)

            def branch_b(g, j, gate_group):
                b, _ = acc_here()
                gate_ready(gate_group)
                dve.tensor_tensor(merged[:, j], acc[:, b], gate_b[:, g], ALU.mult
                                  ).then_inc(acc_read[b], 1)

            def branch_a(g, j, gate_group):
                b, n = acc_here()
                gate_ready(gate_group)
                dve.tensor_tensor(gate_a[:, g], acc[:, b], gate_a[:, g], ALU.mult).then_inc(acc_read[b], 1)
                wait(dve, acc_read[b], n.over(2).plus(1))
                dve.tensor_tensor(merged[:, j], merged[:, j], gate_a[:, g], ALU.add).then_inc(merged_made, 1)

            def scores(h):
                m = at["misc"]
                b, r = m.mod(2), h % 2
                wait(dve, misc_full, m.plus(1))
                dve.wait_ge(causal_in, 16)
                dve.scalar_tensor_tensor(out=s_sb[:, r, :], in0=misc[:, b, 0:3 * P], scalar=SCALE, in1=causal[:],
                                         op0=ALU.mult, op1=ALU.add).then_inc(misc_read[b], 1)
                wait(dve, misc_read[b], m.over(2).plus(2))
                dve.tensor_reduce(neg_max[:, r, 0:1], s_sb[:, r, 0:P], AX.X, ALU.max, negate=True)
                dve.tensor_reduce(neg_max[:, r, 1:2], s_sb[:, r, P:3 * P], AX.X, ALU.max,
                                  negate=True).then_inc(maxima, 1)

            def probs_step(h):
                dve.wait_ge(exps, h + 1)
                dve.reciprocal(row_inv[:, h % 2, :], row_sum[:, h % 2, :]).then_inc(inverted, 1)

            def pv(h):
                m = at["misc"]
                b = m.mod(2)
                dve.wait_ge(att_hi, h + 1)
                dve.tensor_tensor(attT_lo[:, h, :], misc[:, b, 0:SEQ], f32(attT_hi[:, h, :]), ALU.subtract
                                  ).then_inc(misc_read[b], 1)

            def x2_out(j):
                b, _ = acc_here()
                dve.wait_ge(x_again_in, 16)
                cols = slice(j * N, (j + 1) * N)
                dve.tensor_tensor(tokens[:, :, cols], acc[:, b], x_again[:, :, cols], ALU.add).then_inc(acc_read[b], 1)

            def y_out(j):
                b, _ = acc_here()
                cols = slice(j * N, (j + 1) * N)
                if j < 3:
                    dve.tensor_tensor(tokens[:, :, cols], acc[:, b], tokens[:, :, cols], ALU.add).then_inc(acc_read[b], 1)
                else:
                    for t in range(T):
                        dve.tensor_tensor(tokens[:, t, cols], acc[:, b, t], tokens[:, t, cols], ALU.add
                                          ).then_inc(y_rows, 1)
                    dve.wait_ge(y_rows, 2)
                    dve.wait_ge(gain_in, 16)
                    dve.tensor_tensor(result[:, 1, cols], tokens[:, 1, cols], gain_row[:, cols], ALU.mult
                                      ).then_inc(gained, 1)

            def conv(i, g):
                wait(dve, tap0, at["conv"].plus(1))
                for back in (1, 2):
                    for p in range(2):
                        for f in range(2):
                            w = par[:, bass.ds(conv_taps(i, g, p, f) + 2 - back, 1)]
                            y = yconv[:, p, f, back:SEQ]
                            ins = dve.scalar_tensor_tensor(out=y, in0=uT[:, 2 * p + f, 0:SEQ - back], scalar=w,
                                                           in1=y, op0=ALU.mult, op1=ALU.add)
                    ins.then_inc(taps, 1)
                    if back == 1:
                        wait(dve, taps, at["conv"].times(2).plus(1))

            def ff_gate(i, g):
                wait(dve, silu_made, at["ff_gate"].plus(1))
                dve.tensor_tensor(prod[:], silu_g[:], yconv[:, 1].rearrange("p f s -> p (f s)"),
                                  ALU.mult).then_inc(product, 1)
                wait(dve, act_hi, at["ff_gate"].plus(1))
                kt = bass.ds(i * 4 + 2 * g, 2)
                dve.tensor_tensor(actT_lo[:, kt, :].rearrange("p k s -> p (k s)"), prod[:],
                                  f32(actT_hi[:, kt, :].rearrange("p k s -> p (k s)")),
                                  ALU.subtract).then_inc(act_lo, 1)

            def final():
                summed_norm(2)
                dve.wait_ge(gained, 5)
                for part in range(4):
                    cols = slice(part * N, (part + 1) * N)
                    dve.tensor_scalar(result[:, 1, cols], result[:, 1, cols], rstd[:, 1, 0:1], None,
                                      ALU.mult).then_inc(result_ready[1], 1)

            dve.memset(root[:], 1.0).then_inc(warm, 1)
            dve.memset(ones[:], 1.0)
            dve.memset(scores_T[:, 0:2], 0.0).then_inc(misc_read[0], 1)
            dve.memset(scores_T[:, 2:4], 0.0).then_inc(misc_read[1], 1)
            walk(dve, at, dict(split=split, x_norm=x_norm, h_make=h_make, h_lo=h_lo, operand=operand, tables=tables_step, bounds=bounds,
                               forget=forget_step, cumsum=cumsum, factors=factors_step, level=level, mix=mix,
                               mix_norm=mix_norm, latent=latent_step, kr_turn=kr_turn, q_rope=q_rope,
                               branch_b=branch_b, branch_a=branch_a, scores=scores, probs=probs_step, pv=pv,
                               merge=merge, x2_out=x2_out, h2_norm=h2_norm, row_scale=row_scale, up_out=up_out, conv=conv, ff_gate=ff_gate, y_out=y_out,
                               final=final))

        @block.gpsimd
        def _(pool):
            at = At()

            def h_make(p):
                if p < H_FIRST:
                    return
                for b in range(2):
                    pool.wait_ge(turn_read[b], 1)
                pool.wait_ge(h_gained, p + 1 - H_FIRST)
                pool.tensor_tensor(xT[:, 2 * p:2 * p + 2, :], xT[:, 2 * p:2 * p + 2, :],
                                   factor_row[:].unsqueeze(1).to_broadcast([P, 2, SEQ]), ALU.mult).then_inc(h_scaled, 1)

            def gate_scale():
                g = at["group"].plus(-1)
                wait(pool, acc_read[g.mod(2)], g.over(2).plus(1))
                pool.wait_ge(par_in, 16)
                v = hgate[:].rearrange("p t (h v) -> p (t h) v", h=4)
                pool.tensor_tensor(v, v, par[:, G_HGRN:G_HGRN + P].unsqueeze(1).to_broadcast([P, 4 * T, P]),
                                   ALU.mult).then_inc(gate_scaled, 1)

            def diff(n):
                h, f = LEVELS[n], fac[:, n % 2]
                wait(pool, cumsummed, at["cumsum"])
                if n >= 2:
                    wait(pool, misc_full, at["misc"])
                if h == 2 * CHUNK:
                    b4 = bb[:].rearrange("p h (c s) -> p h c s", s=CHUNK)
                    f4 = f.rearrange("p h (c s) -> p h c s", s=CHUNK)
                    end = b4[:, :, :, CHUNK - 1:CHUNK]
                    pool.tensor_tensor(sums01[:].unsqueeze(2), end[:, :, 0, :], end[:, :, 1, :],
                                       ALU.add).then_inc(pool_own, 1)
                    pool.tensor_tensor(f4[:, :, 1, :], end[:, :, 1, :].to_broadcast([P, 4, CHUNK]), b4[:, :, 1, :],
                                       ALU.subtract)
                    pool.tensor_copy(f4[:, :, 2, :], b4[:, :, 2, :])
                    pool.tensor_tensor(f4[:, :, 3, :], b4[:, :, 3, :], end[:, :, 2, :].to_broadcast([P, 4, CHUNK]),
                                       ALU.add)
                    wait(pool, pool_own, at["cumsum"])
                    pool.tensor_tensor(f4[:, :, 0, :], sums01[:].unsqueeze(2).to_broadcast([P, 4, CHUNK]),
                                       b4[:, :, 0, :], ALU.subtract).then_inc(decay_diff, 1)
                    return
                f_lo, f_up = halves(f, h)
                b_lo, b_up = halves(bb[:], h)
                blocks = 4 * SEQ // (2 * h)
                end = b_lo[:, :, h - 1:h].to_broadcast([P, blocks, h])
                if h == 1:
                    pool.tensor_tensor(f_lo, b_lo, b_up, ALU.subtract)
                    pool.tensor_tensor(f_up, b_up, b_lo, ALU.subtract).then_inc(decay_diff, 1)
                    return
                pool.tensor_tensor(f_lo, end, b_lo, ALU.subtract)
                (pool.tensor_copy(f_up, b_up) if h == CHUNK else
                 pool.tensor_tensor(f_up, b_up, end, ALU.subtract)).then_inc(decay_diff, 1)

            def probs_step(h):
                r = h % 2
                pool.wait_ge(inverted, h + 1)
                pool.tensor_scalar(probs[:, r, 0:P], probs[:, r, 0:P], row_inv[:, r, 0:1], None, ALU.mult)
                pool.tensor_scalar(probs[:, r, P:3 * P], probs[:, r, P:3 * P], row_inv[:, r, 1:2], None,
                                   ALU.mult).then_inc(probs_made, 1)

            def y_out(j):
                if j < 3:
                    g = at["group"].k - 1
                    cols = slice(j * N, (j + 1) * N)
                    pool.wait_ge(acc_read[g % 2], g // 2 + 1)
                    pool.wait_ge(gain_in, 16)
                    pool.tensor_tensor(result[:, :, cols], tokens[:, :, cols],
                                       gain_row[:, cols].unsqueeze(1).to_broadcast([P, T, N]), ALU.mult
                                       ).then_inc(gained, 1)
                else:
                    cols = slice(j * N, (j + 1) * N)
                    pool.wait_ge(y_rows, 1)
                    pool.tensor_tensor(result[:, 0, cols], tokens[:, 0, cols], gain_row[:, cols], ALU.mult
                                       ).then_inc(gained, 1)

            walk(pool, at, dict(h_make=h_make, gate_scale=gate_scale, diff=diff, probs=probs_step, y_out=y_out))


def conv_taps(i, g, p, f):
    return i * (2 * 16) + (CONV + 16 * g + 8 * p + 4 * f)


def shape_constants():
    c = np.zeros((P, N_CONST), np.float32)
    c[:, C_IDENT:C_IDENT + P] = np.eye(P)
    triangle = np.where(np.arange(P)[None, :] <= np.arange(P)[:, None], 0.0, MASKED)
    c[:, C_CAUSAL:C_CAUSAL + P] = triangle
    c[:, C_CAUSAL + 2 * P:C_CAUSAL + 3 * P] = triangle
    c[:, C_SCAN:C_SCAN + 4 * SEQ] = (np.arange(4 * SEQ) % CHUNK != 0)
    c[:, C_FREQ:] = np.float32(10000.0) ** (-np.arange(0, ROPE, 2, dtype=np.float32) / np.float32(ROPE))
    masks = np.zeros((P, len(LEVELS), P), np.int32)
    s, t = np.arange(P)[:, None], np.arange(P)[None, :]
    for n, h in enumerate(LEVELS):
        if h < P:
            masks[:, n] = (s // (2 * h) == t // (2 * h)) & (s // h % 2 == 0) & (t // h % 2 == 1)
            if h == 1:
                masks[:, n] |= s == t
    return c, masks


def kernel(**inputs):
    import concourse.bacc as bacc
    from concourse.bass_utils import run_bass_kernel_spmd

    a = {k: np.asarray(v) for k, v in inputs.items()}
    w_in, w_uq, w_ukv = a["w_in"][0], a["w_uq"][0], a["w_ukv"][0]
    w_a, w_b, w_out, w_up, w_down = (a[k][0] for k in ("w_branch_a", "w_branch_b", "w_out", "w_up", "w_down"))
    stream = np.empty((N_CHUNKS, P, CH), np.float32)
    n = 0

    def pack(w, k_tiles=2):
        nonlocal n
        count = w.shape[0] // (k_tiles * P)
        stream[n:n + count] = w.reshape(count, k_tiles, P, w.shape[1]).transpose(0, 2, 1, 3).reshape(count, P, CH)
        n += count

    o = np.concatenate([[0], np.cumsum([LORA, LORA, ROPE, D, D, D, D, D, D])])
    c_q, c_kv, k_rope, hq, hf, hi, hg, gate_a, gate_b = (w_in[:, o[k]:o[k + 1]] for k in range(9))

    def block(w, j):
        return w[:, j * N:(j + 1) * N]

    for j in range(QUADS):
        for w in (hf, hq, hi, hg):
            pack(block(w, j))
    pack(block(gate_b, 0))
    pack(block(gate_b, 1))
    pack(c_q)
    pack(c_kv)
    pack(k_rope, KT)
    pack(block(w_b, 0))
    pack(block(w_b, 1))
    for w in (gate_b, w_b):
        pack(block(w, 2))
        pack(block(w, 3))
    uq = w_uq.reshape(LORA, HEADS, NOPE + ROPE)
    ukv = w_ukv.reshape(LORA, HEADS, 2, 128)
    for j in range(QUADS):
        heads = slice(4 * j, 4 * j + 4)
        pack(uq[:, heads, :NOPE].reshape(LORA, N))
        pack(uq[:, heads, NOPE:].reshape(LORA, 256), 4)
        pack(ukv[:, heads, 0].reshape(LORA, N))
        pack(ukv[:, heads, 1].reshape(LORA, N))
    for first in (0, 2):
        for w in (gate_a, w_a):
            pack(block(w, first))
            pack(block(w, first + 1))
    for j in range(4):
        pack(block(w_out, j))
    up = w_up.reshape(D, 2, FF_GROUPS, 256)
    for g in range(FF_GROUPS):
        pack(up[:, :, g].reshape(D, N))
    for j in range(4):
        pack(block(w_down, j))
    assert n == N_CHUNKS

    def along_partitions(v):
        return v.reshape(-1, P).T

    taps = np.concatenate([a["conv_w"][0], a["conv_b"]], 0)
    taps = taps.reshape(4, 2, FF_GROUPS, 2, P).transpose(4, 2, 1, 3, 0).reshape(P, -1)
    params = np.concatenate([along_partitions(a[k][0]) for k in ("attn_norm_g", "q_norm_g", "kv_norm_g", "ffn_norm_g",
                                                                   "hgrn_lb_logits")]
                            + [np.broadcast_to(a["hgrn_out_norm_g"][0], (P, P)), taps], 1)
    constants, masks = shape_constants()
    arrays = {
        "weights": stream,
        "x": a["x"][0],
        "x_turned": a["x"][0].reshape(SEQ, KT, P).transpose(2, 1, 0),
        "params": params,
        "consts": constants,
        "level_masks": masks,
        "positions": a["positions"][0].reshape(T, P).T,
        "final_gain": np.broadcast_to(a["final_norm_g"], (P, D)),
    }
    arrays = {k: np.ascontiguousarray(v) for k, v in arrays.items()}
    nc = bacc.Bacc("TRN2", target_bir_lowering=False, num_devices=1)
    aps = {k: nc.dram_tensor(k, v.shape, mybir.dt.from_np(v.dtype), kind="ExternalInput").ap()
           for k, v in arrays.items()}
    out = nc.dram_tensor("out", (SEQ, D), F32, kind="ExternalOutput").ap()
    build(nc, out=out, **aps)
    result = run_bass_kernel_spmd(nc, [arrays], core_ids=[0])
    return result.results[0]["out"].reshape(1, SEQ, D)
```
